# Optimizing a Trainium2 kernel written in Bass

```python
import jax, jax.numpy as jnp
from jax import lax
import numpy as np

D_MODEL = 1024
BATCH = 1
SEQ = 1024
DEPTH = 2

PLE_DIM = 256
HEAD_DIM = 64
SGU_HEADS = 4
SGU_WIDTH = SGU_HEADS * HEAD_DIM
CHUNK = 128
CONV_GROUPS = 4
CONV_WIDTH = CONV_GROUPS * HEAD_DIM
CONV_KERNEL = 31
MLA_HEADS = 8
MLA_NOPE = 64
MLA_ROPE = 32
MLA_QK = MLA_NOPE + MLA_ROPE
MLA_V = 64
MLA_WIDTH = MLA_HEADS * MLA_V
Q_RANK = 256
KV_RANK = 128
ROPE_THETA = 10000.0
Q_BLOCK = 128
MIX_WIDTH = SGU_WIDTH + CONV_WIDTH + MLA_WIDTH
IN_WIDTH = 2 * SGU_WIDTH + 2 * CONV_WIDTH + Q_RANK + KV_RANK + MLA_ROPE
IN_SPLITS = [2 * SGU_WIDTH, 2 * SGU_WIDTH + 2 * CONV_WIDTH,
             2 * SGU_WIDTH + 2 * CONV_WIDTH + Q_RANK,
             2 * SGU_WIDTH + 2 * CONV_WIDTH + Q_RANK + KV_RANK]
N_GROUPS = 4
EXPERTS_PER_GROUP = 8
N_EXPERTS = N_GROUPS * EXPERTS_PER_GROUP
D_EXPERT = 256
TOP_K = 2
EXPERT_BLOCK = 128
MAX_START = 4096
EPS = 1e-6

kernel_name = "hymba_sgu_conformer_mla_hmoe"

def rmsnorm(x, g):
    xf = x.astype(jnp.float32)
    y = xf * lax.rsqrt(jnp.mean(xf * xf, axis=-1, keepdims=True) + EPS)
    return (y * g.astype(jnp.float32)).astype(x.dtype)

def layernorm(x, g, b):
    xf = x.astype(jnp.float32)
    mu = jnp.mean(xf, axis=-1, keepdims=True)
    var = jnp.mean(jnp.square(xf - mu), axis=-1, keepdims=True)
    y = (xf - mu) * lax.rsqrt(var + EPS)
    return (y * g.astype(jnp.float32) + b.astype(jnp.float32)).astype(x.dtype)

def rope(x, cos, sin):
    xf = x.astype(jnp.float32)
    x1, x2 = jnp.split(xf, 2, axis=-1)
    return jnp.concatenate([x1 * cos - x2 * sin, x2 * cos + x1 * sin], axis=-1).astype(x.dtype)

def sgu_mixer(z, ln_g, ln_b, w_s, b_s):
    B, S, _ = z.shape
    z = jax.nn.gelu(z)
    u, v = jnp.split(z, 2, axis=-1)
    v = layernorm(v.reshape(B, S, SGU_HEADS, HEAD_DIM),
                  ln_g.reshape(SGU_HEADS, HEAD_DIM), ln_b.reshape(SGU_HEADS, HEAD_DIM))
    v = v.reshape(B, S // CHUNK, CHUNK, SGU_HEADS, HEAD_DIM)
    causal = jnp.tril(jnp.ones((CHUNK, CHUNK), w_s.dtype))
    s = jnp.einsum('hij,bnjhd->bnihd', w_s * causal, v)
    s = s + jnp.transpose(b_s)[None, None, :, :, None]
    return u * s.reshape(B, S, SGU_WIDTH)

def conv_mixer(z, conv_w, conv_b, ln_g, ln_b, pw_w, pw_b):
    B, S, _ = z.shape
    a, g = jnp.split(z, 2, axis=-1)
    y = a * jax.nn.sigmoid(g)
    y = lax.conv_general_dilated(
        y, conv_w[:, None, :].astype(y.dtype), window_strides=(1,),
        padding=[(CONV_KERNEL - 1, 0)], dimension_numbers=('NWC', 'WIO', 'NWC'),
        feature_group_count=CONV_WIDTH) + conv_b
    y = layernorm(y.reshape(B, S, CONV_GROUPS, HEAD_DIM),
                  ln_g.reshape(CONV_GROUPS, HEAD_DIM), ln_b.reshape(CONV_GROUPS, HEAD_DIM))
    y = jax.nn.silu(y.reshape(B, S, CONV_WIDTH))
    return y @ pw_w + pw_b

def causal_block_attention(q, k, v):
    B, S, H, _ = q.shape
    nb = S // Q_BLOCK
    qb = jnp.transpose(q.reshape(B, nb, Q_BLOCK, H, MLA_QK), (1, 0, 2, 3, 4))
    kpos = jnp.arange(S)
    scale = MLA_QK ** -0.5

    def block(args):
        qi, bi = args
        s = jnp.einsum('bqhd,bkhd->bhqk', qi, k, preferred_element_type=jnp.float32) * scale
        qpos = bi * Q_BLOCK + jnp.arange(Q_BLOCK)
        s = jnp.where(kpos[None, :] <= qpos[:, None], s, -1e30)
        pr = jax.nn.softmax(s, axis=-1).astype(v.dtype)
        return jnp.einsum('bhqk,bkhd->bqhd', pr, v)

    o = lax.map(block, (qb, jnp.arange(nb)))
    return jnp.transpose(o, (1, 0, 2, 3, 4)).reshape(B, S, H * MLA_V)

def mla_mixer(c_q, c_kv, k_pe, cos, sin, qa_g, w_uq, kva_g, w_ukv, qn_g, kn_g):
    B, S, _ = c_q.shape
    q = (rmsnorm(c_q, qa_g) @ w_uq).reshape(B, S, MLA_HEADS, MLA_QK)
    kv = (rmsnorm(c_kv, kva_g) @ w_ukv).reshape(B, S, MLA_HEADS, MLA_NOPE + MLA_V)
    q_nope = rmsnorm(q[..., :MLA_NOPE], qn_g[:MLA_NOPE])
    q_pe = rope(rmsnorm(q[..., MLA_NOPE:], qn_g[MLA_NOPE:]), cos, sin)
    k_nope = rmsnorm(kv[..., :MLA_NOPE], kn_g[:MLA_NOPE])
    v = kv[..., MLA_NOPE:]
    k_pe = rope(rmsnorm(k_pe, kn_g[MLA_NOPE:])[:, :, None, :], cos, sin)
    q = jnp.concatenate([q_nope, q_pe], axis=-1)
    k = jnp.concatenate([k_nope, jnp.broadcast_to(k_pe, (B, S, MLA_HEADS, MLA_ROPE))], axis=-1)
    return causal_block_attention(q, k, v)

def hier_moe(m, wg, bg, we, be, w_gate, w_up, w_down):
    B, S, D = m.shape
    t = m.reshape(-1, D)
    N = t.shape[0]
    glog = (t @ wg + bg).astype(jnp.float32)
    gprob = jax.nn.softmax(glog, axis=-1)
    g_idx = jnp.argmax(glog, axis=-1)
    g_w = jnp.take_along_axis(gprob, g_idx[:, None], axis=1)[:, 0]
    elog = (t @ we + be).astype(jnp.float32).reshape(N, N_GROUPS, EXPERTS_PER_GROUP)
    elog = jnp.take_along_axis(elog, g_idx[:, None, None], axis=1)[:, 0, :]
    eprob = jax.nn.softmax(elog, axis=-1)
    topv, topi = lax.top_k(eprob, TOP_K)
    topv = topv / jnp.sum(topv, axis=-1, keepdims=True)

    nk = N * TOP_K
    flat_e = (g_idx[:, None] * EXPERTS_PER_GROUP + topi).reshape(-1)
    flat_tok = jnp.repeat(jnp.arange(N, dtype=jnp.int32), TOP_K)
    flat_w = (g_w[:, None] * topv).reshape(-1)
    order = jnp.argsort(flat_e)
    e_s, tok_s, w_s = flat_e[order], flat_tok[order], flat_w[order]
    counts = jnp.bincount(flat_e, length=N_EXPERTS)
    start = jnp.cumsum(counts) - counts
    padded = (counts + EXPERT_BLOCK - 1) // EXPERT_BLOCK * EXPERT_BLOCK
    pend = jnp.cumsum(padded)
    pstart = pend - padded
    dest = pstart[e_s] + (jnp.arange(nk) - start[e_s])
    P = nk + N_EXPERTS * EXPERT_BLOCK
    nb = P // EXPERT_BLOCK
    buf_tok = jnp.zeros((P,), jnp.int32).at[dest].set(tok_s)
    buf_w = jnp.zeros((P,), t.dtype).at[dest].set(w_s.astype(t.dtype))
    blk_e = jnp.minimum(jnp.searchsorted(pend, jnp.arange(nb) * EXPERT_BLOCK, side='right'),
                        N_EXPERTS - 1)

    def expert_block(args):
        tok_b, w_b, e = args
        xb = t[tok_b]
        hb = jax.nn.silu(xb @ w_gate[e]) * (xb @ w_up[e])
        return (hb @ w_down[e]) * w_b[:, None]

    y = lax.map(expert_block, (buf_tok.reshape(nb, EXPERT_BLOCK),
                               buf_w.reshape(nb, EXPERT_BLOCK), blk_e))
    out = jnp.zeros((N, D), t.dtype).at[buf_tok].add(y.reshape(P, D))
    return out.reshape(B, S, D)

def setup_inputs(seed: int = 0) -> dict:
    key = jax.random.key(seed)
    ks = iter(jax.random.split(key, 48))
    L = DEPTH

    def nrm(shape, scale):
        return jax.random.normal(next(ks), shape, jnp.float32) * scale

    def gain(shape):
        return 1.0 + nrm(shape, 0.01)

    x = nrm((BATCH, SEQ, D_MODEL), 1.0)
    p = nrm((DEPTH, BATCH, SEQ, PLE_DIM), 1.0)
    positions = (jax.random.randint(next(ks), (BATCH, 1), 0, MAX_START, dtype=jnp.int32)
                 + jnp.arange(SEQ, dtype=jnp.int32)[None, :])
    return {
        "x": x,
        "p": p,
        "positions": positions,
        "mix_norm_g": gain((L, D_MODEL)),
        "w_in": nrm((L, D_MODEL, IN_WIDTH), D_MODEL ** -0.5),
        "sgu_ln_g": gain((L, SGU_WIDTH)),
        "sgu_ln_b": nrm((L, SGU_WIDTH), 0.01),
        "sgu_w": nrm((L, SGU_HEADS, CHUNK, CHUNK), CHUNK ** -0.5),
        "sgu_b": gain((L, SGU_HEADS, CHUNK)),
        "conv_w": nrm((L, CONV_KERNEL, CONV_WIDTH), CONV_KERNEL ** -0.5),
        "conv_b": nrm((L, CONV_WIDTH), 0.01),
        "conv_ln_g": gain((L, CONV_WIDTH)),
        "conv_ln_b": nrm((L, CONV_WIDTH), 0.01),
        "conv_pw_w": nrm((L, CONV_WIDTH, CONV_WIDTH), CONV_WIDTH ** -0.5),
        "conv_pw_b": nrm((L, CONV_WIDTH), 0.01),
        "q_a_norm_g": gain((L, Q_RANK)),
        "w_uq": nrm((L, Q_RANK, MLA_HEADS * MLA_QK), Q_RANK ** -0.5),
        "kv_a_norm_g": gain((L, KV_RANK)),
        "w_ukv": nrm((L, KV_RANK, MLA_HEADS * (MLA_NOPE + MLA_V)), KV_RANK ** -0.5),
        "q_norm_g": gain((L, MLA_QK)),
        "k_norm_g": gain((L, MLA_QK)),
        "branch_norm_g": gain((L, MIX_WIDTH)),
        "w_o": nrm((L, MIX_WIDTH, D_MODEL), MIX_WIDTH ** -0.5),
        "ffn_norm_g": gain((L, D_MODEL)),
        "router_group_w": nrm((L, D_MODEL, N_GROUPS), D_MODEL ** -0.5),
        "router_group_b": nrm((L, N_GROUPS), 0.01),
        "router_expert_w": nrm((L, D_MODEL, N_EXPERTS), D_MODEL ** -0.5),
        "router_expert_b": nrm((L, N_EXPERTS), 0.01),
        "moe_w_gate": nrm((L, N_EXPERTS, D_MODEL, D_EXPERT), D_MODEL ** -0.5),
        "moe_w_up": nrm((L, N_EXPERTS, D_MODEL, D_EXPERT), D_MODEL ** -0.5),
        "moe_w_down": nrm((L, N_EXPERTS, D_EXPERT, D_MODEL), D_EXPERT ** -0.5),
        "ple_norm_g": gain((L, D_MODEL)),
        "ple_gate_w": nrm((L, D_MODEL, D_MODEL), D_MODEL ** -0.5),
        "ple_proj_w": nrm((L, PLE_DIM, D_MODEL), PLE_DIM ** -0.5),
        "ple_post_norm_g": gain((L, D_MODEL)),
    }

def reference(x, p, positions, mix_norm_g, w_in, sgu_ln_g, sgu_ln_b, sgu_w, sgu_b,
              conv_w, conv_b, conv_ln_g, conv_ln_b, conv_pw_w, conv_pw_b,
              q_a_norm_g, w_uq, kv_a_norm_g, w_ukv, q_norm_g, k_norm_g,
              branch_norm_g, w_o, ffn_norm_g, router_group_w, router_group_b,
              router_expert_w, router_expert_b, moe_w_gate, moe_w_up, moe_w_down,
              ple_norm_g, ple_gate_w, ple_proj_w, ple_post_norm_g):
    inv_freq = ROPE_THETA ** (-jnp.arange(0, MLA_ROPE, 2, dtype=jnp.float32) / MLA_ROPE)
    ang = positions.astype(jnp.float32)[..., None] * inv_freq
    cos = jnp.cos(ang)[:, :, None, :]
    sin = jnp.sin(ang)[:, :, None, :]

    h = x
    for i in range(DEPTH):
        a = rmsnorm(h, mix_norm_g[i])
        z = a @ w_in[i]
        z_sgu, z_conv, c_q, c_kv, k_pe = jnp.split(z, IN_SPLITS, axis=-1)
        y_a = sgu_mixer(z_sgu, sgu_ln_g[i], sgu_ln_b[i], sgu_w[i], sgu_b[i])
        y_b = conv_mixer(z_conv, conv_w[i], conv_b[i], conv_ln_g[i], conv_ln_b[i],
                         conv_pw_w[i], conv_pw_b[i])
        y_c = mla_mixer(c_q, c_kv, k_pe, cos, sin, q_a_norm_g[i], w_uq[i],
                        kv_a_norm_g[i], w_ukv[i], q_norm_g[i], k_norm_g[i])
        bg = branch_norm_g[i]
        y = jnp.concatenate([
            rmsnorm(y_a, bg[:SGU_WIDTH]),
            rmsnorm(y_b, bg[SGU_WIDTH:SGU_WIDTH + CONV_WIDTH]),
            rmsnorm(y_c, bg[SGU_WIDTH + CONV_WIDTH:]),
        ], axis=-1)
        h = h + y @ w_o[i]

        m = rmsnorm(h, ffn_norm_g[i])
        h = h + hier_moe(m, router_group_w[i], router_group_b[i], router_expert_w[i],
                         router_expert_b[i], moe_w_gate[i], moe_w_up[i], moe_w_down[i])

        gate = jax.nn.sigmoid(rmsnorm(h, ple_norm_g[i]) @ ple_gate_w[i])
        e = rmsnorm(p[i] @ ple_proj_w[i], ple_post_norm_g[i])
        h = h + gate * e
    return h


_drawn_inputs = setup_inputs


def setup_inputs(seed=0):
    import zlib

    import numpy as np

    out = dict(_drawn_inputs(seed))
    spreads = {}
    factors = {'mix_norm_g': 2.91,
     'sgu_ln_g': 5.844,
     'sgu_ln_b': 4.846,
     'sgu_b': 4.202,
     'conv_b': 2.772,
     'conv_ln_g': 4.235,
     'conv_ln_b': 4.013,
     'conv_pw_b': 3.581,
     'q_a_norm_g': 3.52,
     'kv_a_norm_g': 3.153,
     'q_norm_g': 3.686,
     'k_norm_g': 3.509,
     'branch_norm_g': 2.761,
     'ffn_norm_g': 2.924,
     'router_group_b': 3.671,
     'router_expert_b': 3.552,
     'ple_norm_g': 8.0,
     'ple_post_norm_g': 8.0}
    for name, (base, spread) in spreads.items():
        noise = np.random.default_rng([zlib.crc32(name.encode()), seed]).standard_normal(out[name].shape)
        drawn = base * np.exp(spread * noise) if base else spread * noise
        out[name] = __import__('jax').numpy.asarray(drawn.astype(out[name].dtype))
    for name, factor in factors.items():
        out[name] = (out[name] * factor).astype(out[name].dtype)
    return out
```

```python
from contextlib import ExitStack

import numpy as np

import concourse.bass as bass
from concourse import mybir

F32 = mybir.dt.float32
BF16 = mybir.dt.bfloat16
F16 = mybir.dt.float16
I32 = mybir.dt.int32
ALU = mybir.AluOpType
ACT = mybir.ActivationFunctionType
AX = mybir.AxisListType

P = 128
HEAD = 64
EPS = 1e-6
ROPE_THETA = 10000.0
BIG = 1e30
GELU_C = 0.7978845608028654
GELU_A = 0.044715
ROUND = 12582912.0
TWO_PI_HI = 6.28125
TWO_PI_MID = round((2 * np.pi - TWO_PI_HI) * 2 ** 20) / 2 ** 20
TWO_PI_LO = float(np.float32(2 * np.pi - TWO_PI_HI - TWO_PI_MID))


class Steps:

    def __init__(self, sem, names, credit=0):
        self.sem, self.names, self.per, self.credit, self.at = sem, list(names), len(names), credit, 0

    def next(self, name):
        assert self.names[self.at] == name, (name, self.names[self.at])
        self.at = (self.at + 1) % self.per
        return self.sem, 1

    def after(self, index, name=None):
        n = self.per if name is None else self.names.index(name) + 1
        return self.sem, index * self.per + (n + self.credit * self.per)

    def before(self, index):
        return self.sem, index * self.per + self.credit * self.per


def build(nc, I, out):
    DEPTH, _, SEQ, PLE = I["p"].shape
    D = I["x"].shape[2]
    TILES, KD = SEQ // P, D // P
    SGU = I["sgu_ln_g"].shape[1]
    GROUPS = SGU // HEAD
    TAPS = I["conv_w"].shape[1]
    QR, KVR = I["q_a_norm_g"].shape[1], I["kv_a_norm_g"].shape[1]
    QK = I["q_norm_g"].shape[1]
    HEADS = I["w_uq"].shape[2] // QK
    ROPE = QK - HEAD
    HR = ROPE // 2
    IN = I["w_in"].shape[2]
    MLA_IN = IN - 4 * SGU
    NG, NE = I["router_group_w"].shape[2], I["router_expert_w"].shape[2]
    EPG = NE // NG
    F = I["moe_w_gate"].shape[3]
    TOPK = 2
    MAXB = (SEQ * TOPK - NE) // P + NE
    MAXB1 = MAXB + 1
    SCALE = float(QK) ** -0.5
    HC = HEADS // 2
    PAIRS = TILES // 2
    assert (TILES, KD, D, F, MAXB1 % 3, HC * P) == (8, 8, 1024, 256, 0, 512)

    with ExitStack() as ctx:
        def sb(name, shape, dt=F32):
            return ctx.enter_context(nc.sbuf_tensor(name, shape, dt))

        def sem(name):
            return ctx.enter_context(nc.semaphore(name))

        def steps(name, names, credit=0):
            return Steps(sem(name), names, credit)

        m_dram = nc.dram_tensor("moe_inputs", (SEQ, D), F32).ap()
        y_rows = nc.dram_tensor("choice_outputs", (2 * SEQ + P, D), F32).ap()
        qk_dram = nc.dram_tensor("qk_heads", (2, QK, HEADS, SEQ), F32).ap()

        ps = ctx.enter_context(nc.psum_tensor("ps", [P, 8, 512], F32))

        def bank(n, a=0, b=512):
            return ps[:, n, a:b]

        def banks(n):
            return ps[:, n:n + 2, :].rearrange("p a b -> p (a b)")

        h = sb("h", [P, TILES, D])
        A = sb("region_a", [P, KD * IN])
        B = sb("region_b", [P, 2 * TILES * 640])
        C = sb("region_c", [P, 13312])
        junk = sb("junk", [P, D])
        gains = sb("gains", [P, 3, D])
        MIX, BRANCH, FFN = 0, 1, 2

        def at(region, off, *shape):
            n = int(np.prod(shape))
            v = region[:, off:off + n]
            if len(shape) == 1:
                return v
            names = " ".join("abcd"[:len(shape)])
            return v.rearrange(f"p ({names}) -> p {names}", **dict(zip("abcd", shape)))

        w_in = at(A, 0, KD, IN)
        stage = [at(A, 2048 * u, 2, HEADS, P) for u in range(2)]
        q_ring = [at(A, 4096 + 1024 * u, SEQ) for u in range(2)]
        k_ring = [at(A, 6144 + 1024 * u, SEQ) for u in range(2)]
        prob = [at(A, 8192 + 1024 * u, SEQ) for u in range(2)]
        prob_t = [at(A, 10240 + 512 * u, 4, P) for u in range(2)]
        qk_sq = at(A, 8192, HEADS, QK)
        k_sq = at(A, 8192 + 768, HEADS, HEAD)
        xc = at(A, 9472, HEADS + 1, 2, HR)
        xs = at(A, 9472 + 288, HEADS + 1, 2, HR)
        x_blk = [at(A, 6144 + 1024 * u, D) for u in range(3)]
        xT = at(A, 9216, KD, P)
        hid = at(A, 10240, F)
        hid_t = at(A, 10496, 2, P)
        hid_g = at(A, 10752, F)
        w_uq = at(B, 0, 2, HEADS * QK)
        w_ukv = at(B, 1536, HEADS * 2 * HEAD)
        zc = at(B, 2560, TILES, MLA_IN)
        T0 = 2560 + TILES * MLA_IN
        sg_t, sg_uv = at(B, T0, 512), at(B, T0 + 512, 512)
        gl_t, gl = at(B, T0 + 1024, SGU), at(B, T0 + 1280, SGU)
        v_c, v_sq, v_n = (at(B, T0 + 1536 + 256 * i, GROUPS, HEAD) for i in range(3))
        acc = at(B, T0 + 2304, 2, P)
        c_c, c_sq, c_n = (at(B, T0 + 2560 + 256 * i, GROUPS, HEAD) for i in range(3))
        c_th, c_y = at(B, T0 + 3328, SGU), at(B, T0 + 3584, SGU)
        c_yT = at(B, T0 + 3840, 2, P)
        cn = at(B, T0, QR + KVR)
        cnT = at(B, T0 + 384, 3, P)
        pe_x = at(B, T0 + 768, HEADS + 1, ROPE)
        qs = [at(B, T0 + 1056 + 1536 * u, HEADS, QK) for u in range(2)]
        ks = [at(B, T0 + 1824 + 1536 * u, HEADS, QK) for u in range(2)]
        w_o = at(B, 0, KD, D)
        ple_g = at(B, 0, KD, D)
        ple_p = at(B, KD * D, 2, D)
        a_buf = [at(C, 1024 * u, D) for u in range(2)]
        aT = [at(C, 2048 + 1024 * u, KD, P) for u in range(2)]
        vals = at(C, 0, TILES, HEADS, HEAD)
        y = at(C, 4096, TILES, D)
        cin = [at(C, 12288 + 316 * u, 2, P + TAPS - 1) for u in range(2)]
        y_blk = at(C, 12288, D)
        y_got = [[at(C, 4096 + 2048 * u + 1024 * k, D) for k in range(2)] for u in range(2)]
        gate_t, e_buf = at(C, 8192, D), at(C, 9216, D)
        p_tile = [at(C, 10240 + 256 * u, PLE) for u in range(2)]
        pT = at(C, 10752, 2, P)
        slot = [C[:, 0:6144], C[:, 6144:12288], A[:, 0:6144]]
        w_gu = [s[:, 0:KD * 2 * F].rearrange("p (k f) -> p k f", k=KD) for s in slot]
        w_dn = [s[:, KD * 2 * F:6144].rearrange("p (k f) -> p k f", k=2) for s in slot]
        RS = 6144

        def rs(i, *shape):
            return at(A, RS + 256 * i, *shape)

        vec = sb("vecs", [P, 7 * 256])
        names = ["sgu_g", "sgu_b", "cln_g", "cln_b", "pw_b", "qa_g"]
        V = {n: vec[:, 256 * i:256 * i + 256] for i, n in enumerate(names)}
        V["kva_g"] = vec[:, 1536:1536 + KVR]
        qg = sb("q_gain", [P, QK])
        kg = sb("k_gain", [P, QK])
        gq = sb("score_gain", [P, QK])
        ws_raw = at(C, 11264, GROUPS, P)
        wsT = sb("sgu_w_t", [P, GROUPS, P])
        cw_raw = at(C, 11776, SGU)[0:32]
        cw = sb("conv_w_cols", [P, 2, 32])
        sb_raw = at(C, 12032, P)[0:GROUPS]
        s_bias = sb("sgu_b_cols", [P, GROUPS])
        pw = sb("conv_pw", [P, 2, SGU])
        w_r = sb("router_w", [P, KD, NG + NE])
        b_r = sb("router_b", [P, NG + NE])
        lg = sb("logits", [P, TILES, NG + NE])
        wts = sb("moe_weights", [P, 2, TILES])
        idx = sb("block_tokens", [P, MAXB1 + 3], I32)
        out_idx = sb("block_rows", [P, MAXB1 + 3], I32)
        idx_ring = sb("idx_ring", [P, 3], I32)
        out_ring = sb("out_ring", [P, 1], I32)
        cells = sb("cells", [1, 64], I32)
        run = sb("running", [1, 4])
        ms = sb("mean_sq", [P, 2, 3])
        rstd = sb("rstd", [P, 2, 3])
        pool_t = sb("pool_t", [P, 3])
        m_c, r_c, t_c = sb("m_c", [P, 3]), sb("r_c", [P, 3]), sb("t_c", [P, 3])
        m_qk, r_qk, t_qk = sb("m_qk", [P, 24]), sb("r_qk", [P, 24]), sb("t_qk", [P, 24])
        st_v = sb("st_v", [P, 5, GROUPS])
        st_c = sb("st_c", [P, 5, GROUPS])
        m_e = sb("m_e", [P, 3])
        neg_max = sb("neg_max", [P, 2])
        denom = sb("denom", [P, 4])
        rden = sb("rden", [P, 2])
        ident = sb("ident", [P, P])
        ident_b = sb("ident_b", [P, P], BF16)
        mask_b = sb("mask_b", [P, P], BF16)
        tri_b = sb("tri_b", [P, P], BF16)
        ones_b = sb("ones_b", [P, P], BF16)
        iota = sb("iota", [P, P])
        token = sb("token", [P, TILES, 2])
        padding = sb("padding", [P, 1])
        neg_half = sb("neg_half", [P, 24])
        eps_y = sb("eps_y", [P, 3])
        cos, sin = sb("cos", [P, TILES, HR]), sb("sin", [P, TILES, HR])
        pos_raw = sb("positions", [TILES, P], I32)
        hot_s = A[:, RS + 3072:RS + 3072 + 1024].bitcast(F16).rearrange("p (n s) -> p n s", n=2 * TILES)
        hot_b = A[:, RS + 4096:RS + 4096 + 384].bitcast(F16).rearrange("p (n b) -> p n b", n=2 * TILES)
        picked_b = A[:, RS + 4480:RS + 4480 + 128].bitcast(BF16).rearrange("p (t e) -> p t e", t=TILES)
        nb_col = A[:, RS + 4608:RS + 4608 + 64].bitcast(BF16)

        pos_loaded = sem("pos_loaded")
        h_loaded, w_in_loaded, small_loaded = sem("h_loaded"), sem("w_in_loaded"), sem("small_loaded")
        wo_loaded, ple_loaded = sem("wo_loaded"), sem("ple_loaded")
        qk_stored = [sem(f"qk_stored{u}") for u in range(2)]
        qk_loaded = [sem(f"qk_loaded{u}") for u in range(2)]
        m_stored = [sem(f"m_stored{u}") for u in range(2)]
        gu_loaded = [sem(f"gu_loaded{u}") for u in range(3)]
        dn_loaded = [sem(f"dn_loaded{u}") for u in range(3)]
        x_gathered = [sem(f"x_gathered{u}") for u in range(3)]
        y_stored = sem("y_stored")
        y_fetched = [sem(f"y_fetched{u}") for u in range(2)]
        p_loaded = [sem(f"p_loaded{u}") for u in range(2)]
        out_stored = sem("out_stored")
        h_final = sem("h_final")
        blocks_done = sem("blocks_done")

        S_pool0 = steps("const_pool", ["memsets", "selects"])
        S_vec0 = steps("const_vec", ["casts", "pos", "cols", "ang", "turns", "whole", "r_hi", "r_mid", "r_lo",
                                     "clamped", "neg", "abs", "cosarg"])
        S_pe0, S_act0 = steps("const_pe", ["pos_t"]), steps("const_act", ["sin", "cos"])
        F_act, F_pool = steps("f_act", ["squared", "aT_lo"]), steps("f_pool", ["eps", "rstd"])
        F_vec, F_pe = steps("f_vec", ["a", "aT_hi"]), steps("f_pe", ["T_lo", "T_hi"])
        L_pool, L_pe = steps("l_pool", ["sgu_masked"]), steps("l_pe", ["prep_T"])
        L_act = steps("l_act", ["prep_evac"])
        L_vec = steps("l_vec", ["cin_zero", "gq_pe", "gq_nope"])
        Z_pe = steps("z_pe", ["z_sgu", "z_glu", "z_mla", "s", "gluT"])
        Z_act = steps("z_act", ["sgu_square", "sgu_tanh", "glu_tanh", "mla_copied", "cin_body", "cin_head"], credit=1)
        Z_vec = steps("z_vec", ["sgu_poly", "sgu_cubic", "sgu_gated", "glu", "v_sum", "v_mean", "v_centred",
                                "v_squared", "v_sumsq", "v_scaled", "v_gained", "v_ready", "s_biased", "y_sgu"])
        Z_pool = steps("z_pool", ["v_eps", "v_rstd"])
        C_pe = steps("c_pe", ["coT", "ybT", "pw"], credit=1)
        C_act = steps("c_act", ["c_tanh", "ybT_evac"], credit=1)
        C_pool = steps("c_pool", ["c_eps", "c_rstd"], credit=1)
        taps = [f"tap{k}_{c}" for k in range(TAPS) for c in range(2)]
        C_vec = steps("c_vec", taps + ["c_sum", "c_mean", "c_centred", "c_squared", "c_sumsq", "c_scaled",
                                       "c_gained", "c_normed", "c_silu", "y_conv"], credit=1)
        Q_act = steps("q_act", ["c_squared", "cnT", "qk_squared", "v_stored"])
        Q_pool = steps("q_pool", ["c_eps", "c_rstd", "qk_eps", "qk_rstd"])
        Q_vec = steps("q_vec", ["cn", "kpe", "sumsq", "q_nope", "q_pe", "k_nope", "q_gained", "pe_gained",
                                "xc", "xs", "heads"], credit=1)
        Q_pe = steps("q_pe", ["cT", "q_mm", "kv_mm"])
        R_pe = steps("r_pe", ["q_lo", "q_hi", "k_lo", "k_hi"], credit=1)
        R_act, R_vec = steps("r_act", ["q_lo", "k_lo"], credit=1), steps("r_vec", ["q_hi", "k_hi"], credit=1)
        S_pe = steps("s_pe", [f"s{j}" for j in range(TILES)])
        T_pe = steps("t_pe", [n for j in range(TILES) for n in ([f"lo{j}"] + [f"hi{j}"] * (j >= 4))])
        O_pe = steps("o_pe", [f"o{j}" for j in range(TILES)])
        S_act = steps("s_act", [n for j in range(TILES) for n in
                                ([f"exp{j}"] + [f"hi{j - 1}"] * (j > 4))] + ["hi7"])
        vnames = ["max0"]
        for j in range(TILES):
            vnames += [f"max{j + 1}"] * (j + 1 < TILES) + [f"lo{j}"] + ([f"inv{j - 1}", f"fin{j - 1}"] if j else [])
        S_vec = steps("s_vec", vnames + ["inv7", "fin7"])
        W_pe, W_vec = steps("w_pe", ["lo", "hi"]), steps("w_vec", ["lo", "hi"], credit=1)
        G_pe, G_vec = steps("g_pe", ["logits"]), steps("g_vec", ["logits"], credit=1)
        K_act, K_pe = steps("k_act", ["g_exp", "e_exp"]), steps("k_pe", ["ranks", "starts", "lists"])
        K_vec = steps("k_vec", [
            "g_max", "g_diff", "g_sum", "g_w", "g_miss", "g_cand", "g_first", "g_hot", "g_far", "e_in",
            "m1", "d1", "miss1", "cand1", "i1", "hot1", "rest", "m2", "d2", "miss2", "cand2", "i2", "hot2",
            "picked", "e_diff", "cnt_i", "cnt_up", "cnt_nb", "nb_f", "nb_col", "start_f", "row", "r1", "dest1",
            "r2", "dest2", "dest_i", "blk_i", "blk_f", "slot_f", "hots", "le", "owner", "active", "by_slot",
            "e_den", "e_rden", "w1", "w2", "before", "run_n", "run_slots", "empty", "rows_i",
            "list_i", "owner_i", "cells"])
        M_gu, M_xT, M_dn = steps("m_gu", ["gu"]), steps("m_xT", ["lo", "hi"]), steps("m_dn", ["lo", "hi"])
        M_hT = steps("m_hT", ["hT"])
        M_tanh, M_xlo = steps("m_tanh", ["tanh"]), steps("m_xlo", ["x"])
        M_ylo, M_h = steps("m_ylo", ["y"]), steps("m_h", ["h"])
        M_silu, M_prod = steps("m_silu", ["silu"]), steps("m_prod", ["prod"])
        M_xhi, M_yhi = steps("m_xhi", ["x"]), steps("m_yhi", ["y"])
        M_idx, M_oidx = steps("m_idx", ["idx"]), steps("m_oidx", ["idx"])
        E_comb = steps("e_comb", ["first", "second"], credit=1)
        E_pe = steps("e_pe", ["pT", "g_lo", "g_hi", "e"])
        E_act = steps("e_act", ["pT", "t_lo", "t_hi", "e_sq"], credit=1)
        E_pool = steps("e_pool", ["eps", "rstd"])
        E_vec = steps("e_vec", ["e_scaled", "gated"], credit=1)

        def guarded(eng, cond, fn):
            if cond is True:
                fn()
            else:
                with eng.If(cond):
                    fn()

        def tile_loop(eng, front, main):
            front(0, 0, 0)
            with eng.Fori(0, PAIRS) as i:
                front(2 * i + 1, 1, i)
                main(2 * i, 0, i)
                guarded(eng, i < PAIRS - 1, lambda: front((2 * i + 2).with_bounds(min_val=2, max_val=TILES - 2), 0, i + 1))
                main(2 * i + 1, 1, i)

        def pair_loop(eng, main, lagged):
            with eng.Fori(0, PAIRS) as i:
                main(2 * i, 0, i)
                guarded(eng, i > 0, lambda: lagged((2 * i - 1).with_bounds(min_val=1, max_val=TILES - 1), 1, i - 1))
                main(2 * i + 1, 1, i)
                lagged(2 * i, 0, i)
            lagged(TILES - 1, 1, PAIRS - 1)

        def mixer_loop(eng, front, parts):
            front(0, 0, 0)
            with eng.Fori(0, PAIRS) as i:
                front(2 * i + 1, 1, i)
                for kind, fn in parts:
                    if kind == "main":
                        fn(2 * i, 0)
                    else:
                        guarded(eng, i > 0, lambda: fn((2 * i - 1).with_bounds(min_val=1, max_val=TILES - 1), 1))
                guarded(eng, i < PAIRS - 1, lambda: front((2 * i + 2).with_bounds(min_val=2, max_val=TILES - 2), 0, i + 1))
                for kind, fn in parts:
                    if kind == "main":
                        fn(2 * i + 1, 1)
                    else:
                        fn(2 * i, 0)
            for kind, fn in parts:
                if kind == "tail":
                    fn(TILES - 1, 1)

        def block_loop(eng, step):
            with eng.Fori(0, MAXB1 // 3) as i:
                for u in range(3):
                    b = 3 * i + (1 + u)
                    step(b, ((1 + u) % 3, i + (u == 2)), ((2 + u) % 3, i + (u >= 1)), (u, i))

        def settle(eng, passed):
            eng.sem_inc(passed, 1)

        def counters(eng, l, passed):
            eng.wait_ge(*K_vec.after(l, "cells"))
            settle(eng, passed)
            top = 2 * MAXB1
            prev = eng.value_load(cells[0:1, 48:49], min_val=0, max_val=top)
            n = eng.value_load(cells[0:1, 52:53], min_val=0, max_val=MAXB)
            used = [eng.value_load(cells[0:1, 49 + k:50 + k], min_val=0, max_val=top) for k in range(3)]
            return prev, n, used

        block = ctx.enter_context(nc.Block())

        @block.sync
        def _(sp):
            passed = sem("sp_passed")
            for u in range(2):
                sp.sem_inc(qk_stored[u], 32)
            sp.dma_start(pos_raw[:, :], I["positions"][0].rearrange("(t p) -> t p", p=P)).then_inc(pos_loaded, 16)
            sp.dma_start(h[:, :, :], I["x"][0].rearrange("(t p) d -> p t d", p=P)).then_inc(h_loaded, 16)
            with sp.Fori(0, DEPTH) as l:
                sp.wait_ge(blocks_done, l)
                sp.dma_start(w_in, I["w_in"][l].rearrange("(k p) n -> p k n", p=P)).then_inc(w_in_loaded, 16)
                sp.wait_ge(h_final, TILES * l + TILES)
                small = [
                    (gains[:, MIX], I["mix_norm_g"]), (gains[:, BRANCH], I["branch_norm_g"]),
                    (gains[:, FFN], I["ffn_norm_g"]), (V["sgu_g"], I["sgu_ln_g"]), (V["sgu_b"], I["sgu_ln_b"]),
                    (V["cln_g"], I["conv_ln_g"]), (V["cln_b"], I["conv_ln_b"]), (V["pw_b"], I["conv_pw_b"]),
                    (V["qa_g"], I["q_a_norm_g"]), (V["kva_g"], I["kv_a_norm_g"]), (qg[:, :], I["q_norm_g"]),
                    (kg[:, :], I["k_norm_g"]), (b_r[:, 0:NG], I["router_group_b"]),
                    (b_r[:, NG:NG + NE], I["router_expert_b"]),
                ]
                for dst, src in small:
                    sp.dma_start(dst, src[l].partition_broadcast(P)).then_inc(small_loaded, 16)
                sp.dma_start(ws_raw[:, :, :], I["sgu_w"][l].rearrange("h i j -> i h j")).then_inc(small_loaded, 16)
                sp.dma_start(cw_raw[0:TAPS, :], I["conv_w"][l]).then_inc(small_loaded, 16)
                sp.dma_start(cw_raw[TAPS:TAPS + 1, :], I["conv_b"][l].partition_broadcast(1)).then_inc(small_loaded, 16)
                sp.dma_start(sb_raw[:, :], I["sgu_b"][l]).then_inc(small_loaded, 16)
                sp.dma_start(pw[:, :, :], I["conv_pw_w"][l].rearrange("(k p) n -> p k n", p=P)).then_inc(small_loaded, 16)
                with nc.allow_non_contiguous_dma(reason="short rows of the router"):
                    sp.dma_start(w_r[:, :, 0:NG], I["router_group_w"][l].rearrange("(k p) n -> p k n", p=P)).then_inc(small_loaded, 16)
                    sp.dma_start(w_r[:, :, NG:NG + NE], I["router_expert_w"][l].rearrange("(k p) n -> p k n", p=P)).then_inc(small_loaded, 16)
                sp.dma_start(w_uq, I["w_uq"][l].rearrange("(k p) n -> p k n", p=P)).then_inc(small_loaded, 16)
                sp.dma_start(w_ukv, I["w_ukv"][l]).then_inc(small_loaded, 16)

                with sp.Fori(0, PAIRS) as i:
                    for u in range(2):
                        g = TILES * l + 2 * i + u
                        sp.wait_ge(*R_act.after(g))
                        sp.wait_ge(*R_vec.after(g))
                        for s in range(2):
                            sp.dma_start(qk_dram[s][:, :, bass.ds((2 * i + u) * P, P)], stage[u][0:QK, s]).then_inc(qk_stored[u], 16)
                for u in range(2):
                    sp.wait_ge(qk_stored[u], 32 * PAIRS * l + (32 * PAIRS + 32))
                    settle(sp, passed)

                def load_head(head, u):
                    sp.dma_start(q_ring[u][0:QK], qk_dram[0][:, head, :]).then_inc(qk_loaded[u], 16)
                    sp.dma_start(k_ring[u][0:QK], qk_dram[1][:, head, :]).then_inc(qk_loaded[u], 16)

                load_head(0, 0)
                load_head(1, 1)
                sp.dma_start(w_o, I["w_o"][l].rearrange("(k p) n -> p k n", p=P)).then_inc(wo_loaded, 16)
                with sp.Fori(0, HEADS // 2 - 1) as i:
                    for u in range(2):
                        sp.wait_ge(*S_pe.after(HEADS * l + 2 * i + u))
                        load_head(2 * i + (2 + u), u)
                sp.wait_ge(*W_pe.before(TILES * l + TILES))
                sp.dma_start(ple_g, I["ple_gate_w"][l].rearrange("(k p) n -> p k n", p=P)).then_inc(ple_loaded, 16)
                sp.dma_start(ple_p, I["ple_proj_w"][l].rearrange("(k p) n -> p k n", p=P)).then_inc(ple_loaded, 16)
                sp.dma_start(gains[:, BRANCH], I["ple_post_norm_g"][l].partition_broadcast(P)).then_inc(ple_loaded, 16)
                sp.dma_start(gains[:, MIX], I["ple_norm_g"][l].partition_broadcast(P)).then_inc(ple_loaded, 16)
                with sp.Fori(0, PAIRS) as i:
                    for u in range(2):
                        sp.wait_ge(*F_vec.after(32 * l + 2 * i + (16 + u), "a"))
                        sp.dma_start(m_dram[bass.ds((2 * i + u) * P, P), :], a_buf[u]).then_inc(m_stored[u], 16)

                prev, n, used = counters(sp, l, passed)

                def load_gu(b, s):
                    e = sp.value_load(cells[0:1, bass.ds(b, 1)] if not isinstance(b, int) else cells[0:1, b:b + 1], min_val=0, max_val=NE - 1)
                    sp.dma_start(w_gu[s][:, :, 0:F], I["moe_w_gate"][l, e].rearrange("(k p) f -> p k f", p=P)).then_inc(gu_loaded[s], 16)
                    sp.dma_start(w_gu[s][:, :, F:2 * F], I["moe_w_up"][l, e].rearrange("(k p) f -> p k f", p=P)).then_inc(gu_loaded[s], 16)
                    return e

                def load_dn(e, s):
                    sp.dma_start(w_dn[s], I["moe_w_down"][l, e].rearrange("(k p) f -> p k f", p=P)).then_inc(dn_loaded[s], 16)

                for b in range(3):
                    load_dn(load_gu(b, b), b)

                def weights(b, here, nxt, last):
                    def go():
                        sp.wait_ge(*M_gu.after(prev + b - 1))
                        e = load_gu(b + 2, last[0])
                        sp.wait_ge(*M_dn.after(prev + b - 1))
                        load_dn(e, last[0])
                    guarded(sp, b + 2 < n, go)

                block_loop(sp, weights)

            with sp.Fori(0, TILES) as t:
                sp.wait_ge(h_final, TILES * DEPTH + t + 1)
                sp.dma_start(out[0, bass.ds(t * P, P), :], h[:, t, :]).then_inc(out_stored, 16)
            sp.wait_ge(out_stored, 16 * TILES)

        N_SMALL = 16 * 23

        @block.gpsimd
        def _(gp):
            passed = sem("gp_passed")
            gp.sem_inc(C_pool.sem, C_pool.per)
            for ap, val in ((ident, 0.0), (tri_b, 0.0), (mask_b, 0.0), (ones_b, 1.0), (neg_half, -0.5)):
                nc.gpsimd.memset(ap[:, :], val)
            nc.gpsimd.memset(eps_y[:, 0:1], 4 * EPS)
            nc.gpsimd.memset(eps_y[:, 1:3], EPS)
            nc.gpsimd.iota(iota[:, :], pattern=[[1, P]], base=0, channel_multiplier=0, allow_small_or_imprecise_dtypes=True)
            nc.gpsimd.iota(padding[:, :], pattern=[[1, 1]], base=2 * SEQ + 1, channel_multiplier=1,
                           allow_small_or_imprecise_dtypes=True)
            nc.gpsimd.iota(token[:, :, :], pattern=[[P, TILES], [SEQ, 2]], base=1, channel_multiplier=1,
                           allow_small_or_imprecise_dtypes=True).then_inc(*S_pool0.next("memsets"))
            gp.wait_ge(*S_pool0.after(0, "memsets"))
            nc.gpsimd.affine_select(out=ident[:, :], in_=ident[:, :], pattern=[[-1, P]], compare_op=ALU.not_equal,
                                    fill=1.0, base=0, channel_multiplier=1)
            nc.gpsimd.affine_select(out=tri_b[:, :], in_=tri_b[:, :], pattern=[[-1, P]], compare_op=ALU.is_ge,
                                    fill=1.0, base=0, channel_multiplier=1)
            nc.gpsimd.affine_select(out=mask_b[:, :], in_=mask_b[:, :], pattern=[[-1, P]], compare_op=ALU.is_ge,
                                    fill=-BIG, base=0, channel_multiplier=1).then_inc(*S_pool0.next("selects"))

            def rsqrt(dst, tmp, src, n, eps, own, index, first, second, mul=1.0):
                gp.wait_ge(*own.before(index))
                settle(gp, passed)
                if isinstance(eps, float):
                    i = nc.gpsimd.tensor_scalar(tmp, src, mul, eps, ALU.mult, ALU.add)
                else:
                    i = nc.gpsimd.tensor_tensor(tmp, src, eps, ALU.add)
                i.then_inc(*own.next(first))
                gp.wait_ge(*own.after(index, first))
                nc.gpsimd.tensor_tensor(dst, tmp, neg_half[:, 0:n], ALU.pow).then_inc(*own.next(second))

            with gp.Fori(0, DEPTH) as l:
                gp.wait_ge(small_loaded, N_SMALL * l + N_SMALL)
                settle(gp, passed)
                nc.gpsimd.affine_select(out=ws_raw[:, :, :], in_=ws_raw[:, :, :], pattern=[[0, GROUPS], [-1, P]],
                                        compare_op=ALU.is_ge, fill=0.0, base=0,
                                        channel_multiplier=1).then_inc(*L_pool.next("sgu_masked"))

                def front(ph):
                    def go(t, u, i):
                        r = 32 * l + t + 8 * ph
                        n = 3 if ph == 1 else 1
                        gp.wait_ge(*F_act.after(r, "squared"))
                        rsqrt(rstd[:, u, 0:n], pool_t[:, 0:n], ms[:, u, 0:n], n, eps_y[:, 0:3] if ph == 1 else EPS,
                              F_pool, r, "eps", "rstd")
                    return go

                def sgu_rstd(t, u):
                    g = TILES * l + t
                    gp.wait_ge(*Z_vec.after(g, "v_sumsq"))
                    rsqrt(st_v[:, 4, :], st_v[:, 3, :], st_v[:, 2, :], GROUPS, 4 * EPS, Z_pool, g, "v_eps", "v_rstd", 1.0 / HEAD)

                def conv_rstd(t, u):
                    g = TILES * l + t
                    gp.wait_ge(*C_vec.after(g, "c_sumsq"))
                    rsqrt(st_c[:, 4, :], st_c[:, 3, :], st_c[:, 2, :], GROUPS, EPS, C_pool, g, "c_eps", "c_rstd", 1.0 / HEAD)

                mixer_loop(gp, front(0), [("tail", conv_rstd), ("main", sgu_rstd)])

                with gp.Fori(0, PAIRS) as i:
                    for u in range(2):
                        g = TILES * l + 2 * i + u
                        gp.wait_ge(*Q_act.after(g, "c_squared"))
                        gp.wait_ge(*Q_pool.before(g))
                        settle(gp, passed)
                        nc.gpsimd.tensor_scalar(t_c[:, :], m_c[:, :], 1.0, EPS, ALU.mult, ALU.add).then_inc(*Q_pool.next("c_eps"))
                        gp.wait_ge(*Q_pool.after(g, "c_eps"))
                        nc.gpsimd.tensor_tensor(r_c[:, :], t_c[:, :], neg_half[:, 0:3], ALU.pow).then_inc(*Q_pool.next("c_rstd"))
                        gp.wait_ge(*Q_vec.after(g, "sumsq"))
                        settle(gp, passed)
                        nc.gpsimd.tensor_scalar(t_qk[:, :], m_qk[:, :], 1.0, EPS, ALU.mult, ALU.add).then_inc(*Q_pool.next("qk_eps"))
                        gp.wait_ge(*Q_pool.after(g, "qk_eps"))
                        nc.gpsimd.tensor_tensor(r_qk[:, :], t_qk[:, :], neg_half[:, :], ALU.pow).then_inc(*Q_pool.next("qk_rstd"))

                nothing = lambda *a: None
                tile_loop(gp, front(1), nothing)
                tile_loop(gp, front(2), nothing)

                prev, n, used = counters(gp, l, passed)
                for u in range(2):
                    gp.wait_ge(m_stored[u], 16 * PAIRS * l + 16 * PAIRS)
                    settle(gp, passed)

                def gather(b, s, m):
                    col = idx[:, b:b + 1] if isinstance(b, int) else idx[:, bass.ds(b, 1)]
                    nc.gpsimd.tensor_copy(idx_ring[:, s:s + 1], col).then_inc(*M_idx.next("idx"))
                    gp.wait_ge(*M_idx.after(m))
                    settle(gp, passed)
                    nc.gpsimd.indirect_dma_start(
                        out=x_blk[s], out_offset=None, in_=m_dram,
                        in_offset=bass.IndirectOffsetOnAxis(ap=idx_ring[:, s:s + 1], axis=0)).then_inc(x_gathered[s], 16)

                gather(0, 0, prev)
                gather(1, 1, prev + 1)
                gather(2, 2, prev + 2)

                def rows(b, here, nxt, last):
                    def ahead():
                        gp.wait_ge(*M_xT.after(prev + b - 1))
                        settle(gp, passed)
                        gather(b + 2, last[0], prev + b + 2)

                    def store():
                        gp.wait_ge(*M_ylo.after(prev + b - 1))
                        gp.wait_ge(*M_yhi.after(prev + b - 1))
                        settle(gp, passed)
                        nc.gpsimd.tensor_copy(out_ring[:, :], out_idx[:, bass.ds(b - 1, 1)]).then_inc(*M_oidx.next("idx"))
                        gp.wait_ge(*M_oidx.after(prev + b - 1))
                        settle(gp, passed)
                        nc.gpsimd.indirect_dma_start(
                            out=y_rows, out_offset=bass.IndirectOffsetOnAxis(ap=out_ring[:, 0:1], axis=0),
                            in_=y_blk, in_offset=None).then_inc(y_stored, 16)
                    guarded(gp, b + 2 < n, ahead)
                    guarded(gp, b <= n, store)

                block_loop(gp, rows)
                gp.wait_ge(y_stored, (prev + n) * 16)
                settle(gp, passed)

                def ple_front(t, u, i):
                    g = TILES * l + t
                    gp.wait_ge(*E_comb.after(g - 2))
                    settle(gp, passed)
                    for k in range(2):
                        gp.dma_start(y_got[u][k], y_rows[bass.ds(t * P + k * SEQ, P), :] if not isinstance(t, int)
                                     else y_rows[t * P + k * SEQ:(t + 1) * P + k * SEQ, :]).then_inc(y_fetched[u], 16)
                    gp.dma_start(p_tile[u], I["p"][l, 0, bass.ds(t * P, P), :] if not isinstance(t, int) else I["p"][l, 0, t * P:(t + 1) * P, :]).then_inc(p_loaded[u], 16)
                    front(3)(t, u, i)

                def ple_main(t, u, i):
                    g = TILES * l + t
                    gp.wait_ge(*E_act.after(g, "e_sq"))
                    rsqrt(m_e[:, 2:3], m_e[:, 1:2], m_e[:, 0:1], 1, 4 * EPS, E_pool, g, "eps", "rstd")

                tile_loop(gp, ple_front, ple_main)

        @block.scalar
        def _(act):
            passed = sem("act_passed")
            for s in (E_act, Z_act, C_act, R_act):
                act.sem_inc(s.sem, s.per)
            act.wait_ge(*S_vec0.after(0, "cosarg"))
            nc.scalar.activation(sin[:, :, :], sin[:, :, :], ACT.Sin).then_inc(*S_act0.next("sin"))
            nc.scalar.activation(cos[:, :, :], cos[:, :, :], ACT.Sin).then_inc(*S_act0.next("cos"))

            with act.Fori(0, DEPTH) as l:
                act.wait_ge(*L_pe.after(l))
                nc.scalar.copy(wsT[:, :, :], bank(7).rearrange("p (h i) -> p h i", h=GROUPS))
                nc.scalar.activation(cw[:, :, 0:TAPS], bank(6, 0, 64).rearrange("p (c k) -> p c k", c=2)[:, :, 0:TAPS],
                                     ACT.Copy, scale=0.5)
                nc.scalar.copy(cw[:, :, TAPS:32], bank(6, 0, 64).rearrange("p (c k) -> p c k", c=2)[:, :, TAPS:32])
                nc.scalar.copy(s_bias[:, :], bank(6, 64, 64 + GROUPS)).then_inc(*L_act.next("prep_evac"))

                def front(ph):
                    def go(t, u, i):
                        r = 32 * l + t + 8 * ph
                        g = TILES * l + t
                        if ph == 0:
                            act.wait_ge(h_final, g + 1)
                        elif ph == 1:
                            act.wait_ge(*F_act.before(r))
                        elif ph == 2:
                            act.wait_ge(*W_vec.after(g))
                        else:
                            act.wait_ge(*E_comb.after(g))
                        if ph == 1:
                            for k, (a, b) in enumerate(((0, 256), (256, 512), (512, 1024))):
                                i = nc.scalar.activation(junk[:, a:b], y[:, t, a:b], ACT.Square, scale=float(b - a) ** -0.5,
                                                         accum_out=ms[:, u, k:k + 1])
                        else:
                            i = nc.scalar.activation(junk[:, :], h[:, t, :], ACT.Square, scale=float(D) ** -0.5,
                                                     accum_out=ms[:, u, 0:1])
                        i.then_inc(*F_act.next("squared"))
                        act.wait_ge(*F_pe.after(r, "T_lo"))
                        nc.scalar.copy(aT[u][:, 0:4, :].rearrange("p a b -> p (a b)"), bank(0)).then_inc(*F_act.next("aT_lo"))
                    return go

                def z_main(t, u):
                    g = TILES * l + t
                    act.wait_ge(*Z_pe.after(g, "z_sgu"))
                    nc.scalar.activation(sg_t, bank(2), ACT.Square).then_inc(*Z_act.next("sgu_square"))
                    act.wait_ge(*Z_vec.after(g, "sgu_cubic"))
                    nc.scalar.activation(sg_t, sg_t, ACT.Tanh, scale=GELU_C).then_inc(*Z_act.next("sgu_tanh"))
                    act.wait_ge(*Z_pe.after(g, "z_glu"))
                    nc.scalar.activation(gl_t, bank(3, SGU, 2 * SGU), ACT.Tanh, scale=0.5).then_inc(*Z_act.next("glu_tanh"))
                    act.wait_ge(*Z_pe.after(g, "z_mla"))
                    nc.scalar.copy(zc[:, t, :], bank(4, 0, MLA_IN)).then_inc(*Z_act.next("mla_copied"))

                def c_tanh(t, u):
                    act.wait_ge(*C_vec.after(TILES * l + t, "c_normed"))
                    nc.scalar.activation(c_th, c_n.rearrange("p a b -> p (a b)"), ACT.Tanh, scale=0.5).then_inc(*C_act.next("c_tanh"))

                def z_cin(t, u):
                    g = TILES * l + t
                    gt = bank(6, 0, 2 * P).rearrange("p (c s) -> p c s", c=2)
                    act.wait_ge(*Z_pe.after(g, "gluT"))
                    nc.scalar.copy(cin[u][:, :, TAPS - 1:], gt).then_inc(*Z_act.next("cin_body"))
                    nc.scalar.copy(cin[1 - u][:, :, 0:TAPS - 1], gt[:, :, P - TAPS + 1:]).then_inc(*Z_act.next("cin_head"))

                def c_yT_evac(t, u):
                    act.wait_ge(*C_pe.after(TILES * l + t, "ybT"))
                    nc.scalar.copy(c_yT.rearrange("p a b -> p (a b)"), bank(7, 2 * P, 4 * P)).then_inc(*C_act.next("ybT_evac"))

                mixer_loop(act, front(0), [("main", z_main), ("tail", c_tanh), ("main", z_cin), ("tail", c_yT_evac)])

                def heads_view(b, lo, hi, width):
                    return ps[:, b:b + 2, 0:HC * width].rearrange("p a (h d) -> p a h d", h=HC)[:, :, :, lo:hi]

                def fold(ap):
                    return ap.rearrange("p (a h) d -> p a h d", a=2)

                def q_main(t, u, i):
                    g = TILES * l + t
                    act.wait_ge(*Z_act.before(TILES * l + TILES))
                    act.wait_ge(*Q_act.before(g))
                    c0 = 0
                    for k, n in enumerate((QR, KVR, ROPE)):
                        ins = nc.scalar.activation(junk[:, c0:c0 + n], zc[:, t, c0:c0 + n], ACT.Square, scale=float(n) ** -0.5,
                                                   accum_out=m_c[:, k:k + 1])
                        c0 += n
                    ins.then_inc(*Q_act.next("c_squared"))
                    act.wait_ge(*Q_pe.after(g, "cT"))
                    nc.scalar.copy(cnT.rearrange("p a b -> p (a b)"), bank(6, 0, 3 * P)).then_inc(*Q_act.next("cnT"))
                    act.wait_ge(*Q_pe.after(g, "kv_mm"))
                    nc.scalar.activation(fold(qk_sq)[:, :, :, 0:HEAD], heads_view(2, 0, HEAD, QK), ACT.Square, scale=float(HEAD) ** -0.5)
                    nc.scalar.activation(fold(qk_sq)[:, :, :, HEAD:QK], heads_view(2, HEAD, QK, QK), ACT.Square, scale=float(ROPE) ** -0.5)
                    nc.scalar.activation(fold(k_sq), heads_view(4, 0, HEAD, P), ACT.Square,
                                         scale=float(HEAD) ** -0.5).then_inc(*Q_act.next("qk_squared"))
                    nc.scalar.copy(vals[:, t].rearrange("p (a h) d -> p a h d", a=2),
                                   heads_view(4, HEAD, P, P)).then_inc(*Q_act.next("v_stored"))

                def q_lag(t, u, i):
                    g = TILES * l + t
                    act.wait_ge(qk_stored[u], 32 * (PAIRS * l + i) + 32)
                    act.wait_ge(*R_pe.after(g, "q_lo"))
                    nc.scalar.copy(stage[u][0:QK, 0, 0:HC].rearrange("p a b -> p (a b)"), ps[0:QK, 0, :]).then_inc(*R_act.next("q_lo"))
                    act.wait_ge(*R_pe.after(g, "k_lo"))
                    nc.scalar.copy(stage[u][0:QK, 1, 0:HC].rearrange("p a b -> p (a b)"), ps[0:QK, 7, :]).then_inc(*R_act.next("k_lo"))

                pair_loop(act, q_main, q_lag)

                def attend(hh, first_of_layer):
                    for j in range(TILES):
                        n = (j + 1) * P
                        act.wait_ge(*S_vec.after(hh, f"max{j}"))
                        nc.scalar.activation(prob[j % 2][:, 0:n], banks(2 * (j % 2))[:, 0:n], ACT.Exp, bias=neg_max[:, j % 2:j % 2 + 1],
                                             accum_out=denom[:, j % 4:j % 4 + 1]).then_inc(*S_act.next(f"exp{j}"))
                        if j > 4:
                            evac_hi(hh, j - 1)
                    evac_hi(hh, TILES - 1)

                def evac_hi(hh, j):
                    w = (j - 3) * P
                    act.wait_ge(*T_pe.after(hh, f"hi{j}"))
                    nc.scalar.copy(prob_t[1].rearrange("p a b -> p (a b)")[:, 0:w], bank(5, 0, w)).then_inc(*S_act.next(f"hi{j}"))

                with act.Fori(0, HEADS // 2) as i:
                    for u in range(2):
                        attend(HEADS * l + 2 * i + u, u == 0)

                nothing = lambda *a: None
                act.wait_ge(*S_vec.before(HEADS * l + HEADS))
                tile_loop(act, front(1), nothing)
                tile_loop(act, front(2), nothing)
                act.wait_ge(*K_vec.after(l, "g_diff"))
                nc.scalar.activation(rs(1, TILES, NG), rs(0, TILES, NG), ACT.Exp).then_inc(*K_act.next("g_exp"))
                act.wait_ge(*K_vec.after(l, "e_diff"))
                nc.scalar.activation(rs(9, 2, TILES)[:, 1], rs(9, 2, TILES)[:, 0], ACT.Exp).then_inc(*K_act.next("e_exp"))

                prev, n, used = counters(act, l, passed)

                def x_lo(m):
                    act.wait_ge(*M_xT.after(m, "lo"))
                    nc.scalar.copy(xT[:, 0:4].rearrange("p a b -> p (a b)"), bank(0)).then_inc(*M_xlo.next("x"))

                def tanh(m):
                    act.wait_ge(*M_gu.after(m))
                    nc.scalar.activation(hid_g, bank(2, 0, F), ACT.Tanh, scale=0.5).then_inc(*M_tanh.next("tanh"))

                def h_evac(m):
                    act.wait_ge(*M_hT.after(m))
                    nc.scalar.copy(hid_t.rearrange("p a b -> p (a b)"), bank(3, 0, 2 * P)).then_inc(*M_h.next("h"))

                def y_lo(m):
                    act.wait_ge(y_stored, m * 16)
                    act.wait_ge(*M_dn.after(m, "lo"))
                    nc.scalar.copy(y_blk[:, 0:512], bank(4)).then_inc(*M_ylo.next("y"))

                x_lo(prev)
                tanh(prev)
                x_lo(prev + 1)
                h_evac(prev)

                def expert(b, here, nxt, last):
                    m = prev + b
                    guarded(act, b < n, lambda: tanh(m))
                    guarded(act, b + 1 < n, lambda: x_lo(m + 1))
                    guarded(act, b <= n, lambda: y_lo(m - 1))
                    guarded(act, b < n, lambda: h_evac(m))

                block_loop(act, expert)

                def ple_main(t, u, i):
                    g = TILES * l + t
                    act.wait_ge(*E_pe.after(g, "pT"))
                    nc.scalar.copy(pT.rearrange("p a b -> p (a b)"), bank(6, 0, 2 * P)).then_inc(*E_act.next("pT"))
                    act.wait_ge(*E_vec.before(g))
                    act.wait_ge(*E_pe.after(g, "g_lo"))
                    nc.scalar.activation(gate_t[:, 0:512], bank(2), ACT.Tanh, scale=0.5).then_inc(*E_act.next("t_lo"))
                    act.wait_ge(*E_pe.after(g, "g_hi"))
                    nc.scalar.activation(gate_t[:, 512:1024], bank(3), ACT.Tanh, scale=0.5).then_inc(*E_act.next("t_hi"))
                    act.wait_ge(*E_pe.after(g, "e"))
                    nc.scalar.activation(junk[:, :], banks(4), ACT.Square, scale=2 * float(D) ** -0.5,
                                         accum_out=m_e[:, 0:1]).then_inc(*E_act.next("e_sq"))

                tile_loop(act, front(3), ple_main)

        @block.vector
        def _(v):
            passed = sem("v_passed")
            for s in (W_vec, G_vec, E_comb, E_vec, C_vec, Q_vec, R_vec):
                v.sem_inc(s.sem, s.per)

            def wide(ap, axis, *shape):
                return ap.unsqueeze(axis).to_broadcast([P, *shape])

            def link0(ins, name):
                ins.then_inc(*S_vec0.next(name))
                v.wait_ge(*S_vec0.after(0, name))

            ang, turns = at(B, T0, TILES, HR), at(B, T0 + 128, TILES, HR)
            freq, pos_cols, pos_f = at(B, T0 + 256, HR), at(B, T0 + 272, TILES), at(B, T0 + 280, P)[0:TILES]
            inv_freq = (ROPE_THETA ** (-np.arange(0, ROPE, 2, dtype=np.float64) / ROPE)).astype(np.float32)
            v.memset(run[:, :], 0.0)
            for k in range(HR):
                v.memset(freq[:, k:k + 1], float(inv_freq[k]))
            v.wait_ge(*S_pool0.after(0, "selects"))
            link0(v.tensor_copy(ident_b[:, :], ident[:, :]), "casts")
            v.wait_ge(pos_loaded, 16)
            v.tensor_copy(pos_f, pos_raw[:, :]).then_inc(*S_vec0.next("pos"))
            v.wait_ge(*S_pe0.after(0))
            link0(v.tensor_copy(pos_cols, bank(0, 0, TILES)), "cols")
            link0(v.tensor_tensor(ang, wide(pos_cols, 2, TILES, HR), wide(freq, 1, TILES, HR), ALU.mult), "ang")
            link0(v.tensor_scalar(turns, ang, 1 / (2 * np.pi), ROUND, ALU.mult, ALU.add), "turns")
            link0(v.tensor_scalar(turns, turns, ROUND, None, ALU.subtract), "whole")
            link0(v.scalar_tensor_tensor(ang, turns, -TWO_PI_HI, ang, ALU.mult, ALU.add), "r_hi")
            link0(v.scalar_tensor_tensor(ang, turns, -TWO_PI_MID, ang, ALU.mult, ALU.add), "r_mid")
            link0(v.scalar_tensor_tensor(ang, turns, -TWO_PI_LO, ang, ALU.mult, ALU.add), "r_lo")
            link0(v.tensor_scalar(sin[:, :, :], ang, 3.1415925, -3.1415925, ALU.min, ALU.max), "clamped")
            link0(v.tensor_scalar(cos[:, :, :], sin[:, :, :], -1.0, None, ALU.mult), "neg")
            link0(v.tensor_tensor(cos[:, :, :], cos[:, :, :], sin[:, :, :], ALU.max), "abs")
            v.tensor_scalar(cos[:, :, :], cos[:, :, :], -1.0, np.pi / 2, ALU.mult, ALU.add).then_inc(*S_vec0.next("cosarg"))
            v.wait_ge(h_loaded, 16)
            v.sem_inc(h_final, TILES)

            with v.Fori(0, DEPTH) as l:
                v.wait_ge(small_loaded, N_SMALL * l + N_SMALL)
                v.memset(cin[0][:, :, 0:TAPS - 1], 0.0).then_inc(*L_vec.next("cin_zero"))
                v.tensor_scalar(gq[:, HEAD:QK], qg[:, HEAD:QK], SCALE, None, ALU.mult).then_inc(*L_vec.next("gq_pe"))
                v.scalar_tensor_tensor(gq[:, 0:HEAD], qg[:, 0:HEAD], SCALE, kg[:, 0:HEAD], ALU.mult,
                                       ALU.mult).then_inc(*L_vec.next("gq_nope"))
                v.wait_ge(*L_vec.after(l))
                v.wait_ge(*L_act.after(l))

                def front(ph):
                    def go(t, u, i):
                        r = 32 * l + t + 8 * ph
                        gain = (MIX, BRANCH, FFN, MIX)[ph]
                        v.wait_ge(*F_pool.after(r, "rstd"))
                        if ph == 2:
                            v.wait_ge(m_stored[u], 16 * (PAIRS * l + i))
                        cuts = (0, 256, 512, 1024) if ph == 1 else (0, D)
                        src = y if ph == 1 else h
                        for k, (a, b) in enumerate(zip(cuts, cuts[1:])):
                            ins = v.scalar_tensor_tensor(a_buf[u][:, a:b], src[:, t, a:b], rstd[:, u, k:k + 1],
                                                         gains[:, gain, a:b], ALU.mult, ALU.mult)
                        ins.then_inc(*F_vec.next("a"))
                        v.wait_ge(*F_pe.after(r, "T_hi"))
                        v.tensor_copy(aT[u][:, 4:8, :].rearrange("p a b -> p (a b)"), bank(1)).then_inc(*F_vec.next("aT_hi"))
                    return go

                def conv(t, u):
                    q = TILES * l + t
                    v.wait_ge(*Z_act.after(q, "cin_body"))
                    for k in range(TAPS):
                        for c in range(2):
                            src = cin[u][:, c, k:k + P]
                            if k:
                                v.wait_ge(*C_vec.after(q, f"tap{k - 1}_{c}"))
                                ins = v.scalar_tensor_tensor(acc[:, c, :], src, cw[:, c, k:k + 1], acc[:, c, :], ALU.mult, ALU.add)
                            else:
                                ins = v.tensor_scalar(acc[:, c, :], src, cw[:, c, 0:1], cw[:, c, TAPS:TAPS + 1], ALU.mult, ALU.add)
                            ins.then_inc(*C_vec.next(f"tap{k}_{c}"))

                def gelu_glu(t, u):
                    g = TILES * l + t

                    def link(ins, name):
                        ins.then_inc(*Z_vec.next(name))
                        v.wait_ge(*Z_vec.after(g, name))

                    v.wait_ge(*Z_act.after(g, "sgu_square"))
                    link(v.tensor_scalar(sg_t, sg_t, GELU_A, 1.0, ALU.mult, ALU.add), "sgu_poly")
                    v.tensor_tensor(sg_t, sg_t, bank(2), ALU.mult).then_inc(*Z_vec.next("sgu_cubic"))
                    v.wait_ge(*Z_act.after(g, "sgu_tanh"))
                    v.scalar_tensor_tensor(sg_uv, sg_t, 1.0, bank(2), ALU.add, ALU.mult).then_inc(*Z_vec.next("sgu_gated"))
                    v.wait_ge(*Z_act.after(g, "glu_tanh"))
                    v.scalar_tensor_tensor(gl, gl_t, 1.0, bank(3, 0, SGU), ALU.add, ALU.mult).then_inc(*Z_vec.next("glu"))

                def centre(src, st, centred, squared, link, p):
                    link(v.tensor_reduce(st[:, 0, :], src, AX.X, ALU.add), p + "_sum")
                    link(v.tensor_scalar(st[:, 1, :], st[:, 0, :], 1.0 / HEAD, None, ALU.mult), p + "_mean")
                    link(v.tensor_tensor(centred, src, wide(st[:, 1, :], 2, GROUPS, HEAD), ALU.subtract), p + "_centred")
                    link(v.tensor_tensor(squared, centred, centred, ALU.mult), p + "_squared")
                    v.tensor_reduce(st[:, 2, :], squared, AX.X, ALU.add).then_inc(*{"v": Z_vec, "c": C_vec}[p].next(p + "_sumsq"))

                def scaled(st, centred, dst, gain, bias, link, p, last):
                    link(v.tensor_tensor(dst, centred, wide(st[:, 4, :], 2, GROUPS, HEAD), ALU.mult), p + "_scaled")
                    flat = dst.rearrange("p a b -> p (a b)")
                    link(v.tensor_tensor(flat, flat, V[gain], ALU.mult), p + "_gained")
                    v.tensor_tensor(flat, flat, V[bias], ALU.add).then_inc(*{"v": Z_vec, "c": C_vec}[p].next(last))

                def conv_norm(t, u):
                    q = TILES * l + t

                    def link(ins, name):
                        ins.then_inc(*C_vec.next(name))
                        v.wait_ge(*C_vec.after(q, name))

                    v.wait_ge(*C_pe.after(q, "coT"))
                    centre(bank(7, 0, 256).rearrange("p (a b) -> p a b", a=GROUPS), st_c, c_c, c_sq, link, "c")
                    v.wait_ge(*C_pool.after(q, "c_rstd"))
                    scaled(st_c, c_c, c_n, "cln_g", "cln_b", link, "c", "c_normed")

                def gate_norm(t, u):
                    g = TILES * l + t

                    def link(ins, name):
                        ins.then_inc(*Z_vec.next(name))
                        v.wait_ge(*Z_vec.after(g, name))

                    v.wait_ge(*Z_vec.after(g, "glu"))
                    centre(sg_uv[:, 256:512].rearrange("p (a b) -> p a b", a=GROUPS), st_v, v_c, v_sq, link, "v")
                    v.wait_ge(*Z_pool.after(g, "v_rstd"))
                    scaled(st_v, v_c, v_n, "sgu_g", "sgu_b", link, "v", "v_ready")
                    v.wait_ge(*Z_pe.after(g, "s"))
                    link(v.tensor_tensor(v_sq, bank(5, 0, 256).rearrange("p (a b) -> p a b", a=GROUPS),
                                         wide(s_bias[:, :], 2, GROUPS, HEAD), ALU.add), "s_biased")
                    v.tensor_tensor(y[:, t, 0:SGU], v_sq.rearrange("p a b -> p (a b)"), sg_uv[:, 0:SGU],
                                    ALU.mult).then_inc(*Z_vec.next("y_sgu"))

                def conv_out(t, u):
                    q = TILES * l + t
                    v.wait_ge(*C_act.after(q, "c_tanh"))
                    v.scalar_tensor_tensor(c_y, c_th, 1.0, c_n.rearrange("p a b -> p (a b)"), ALU.add,
                                           ALU.mult).then_inc(*C_vec.next("c_silu"))
                    v.wait_ge(*C_pe.after(q, "pw"))
                    v.scalar_tensor_tensor(y[:, t, SGU:2 * SGU], bank(5, 256, 512), 0.5, V["pw_b"], ALU.mult,
                                           ALU.add).then_inc(*C_vec.next("y_conv"))

                mixer_loop(v, front(0), [("tail", conv), ("main", gelu_glu), ("tail", conv_norm), ("main", gate_norm),
                                         ("tail", conv_out)])

                def heads_view(b, lo, hi, width):
                    return ps[:, b:b + 2, 0:HC * width].rearrange("p a (h d) -> p a h d", h=HC)[:, :, :, lo:hi]

                def fold(ap):
                    return ap.rearrange("p (a h) d -> p a h d", a=2)

                def per_head(ap, d):
                    return ap.rearrange("p (a h) -> p a h", a=2).unsqueeze(3).to_broadcast([P, 2, HC, d])

                def q_main(t, u, i):
                    g = TILES * l + t

                    def link(ins, name):
                        ins.then_inc(*Q_vec.next(name))
                        v.wait_ge(*Q_vec.after(g, name))

                    v.wait_ge(*Q_pool.after(g, "c_rstd"))
                    v.scalar_tensor_tensor(cn[:, 0:QR], zc[:, t, 0:QR], r_c[:, 0:1], V["qa_g"], ALU.mult, ALU.mult)
                    v.scalar_tensor_tensor(cn[:, QR:QR + KVR], zc[:, t, QR:QR + KVR], r_c[:, 1:2], V["kva_g"], ALU.mult,
                                           ALU.mult).then_inc(*Q_vec.next("cn"))
                    v.scalar_tensor_tensor(pe_x[:, HEADS, :], zc[:, t, QR + KVR:MLA_IN], r_c[:, 2:3], kg[:, HEAD:QK], ALU.mult,
                                           ALU.mult).then_inc(*Q_vec.next("kpe"))
                    v.wait_ge(*Q_act.after(g, "qk_squared"))
                    v.tensor_reduce(m_qk[:, 0:8], qk_sq[:, :, 0:HEAD], AX.X, ALU.add)
                    v.tensor_reduce(m_qk[:, 8:16], qk_sq[:, :, HEAD:QK], AX.X, ALU.add)
                    v.tensor_reduce(m_qk[:, 16:24], k_sq, AX.X, ALU.add).then_inc(*Q_vec.next("sumsq"))
                    v.wait_ge(*Q_pool.after(g, "qk_rstd"))
                    v.wait_ge(*Q_act.after(g, "v_stored"))
                    v.tensor_tensor(fold(qs[u])[:, :, :, 0:HEAD], heads_view(2, 0, HEAD, QK), per_head(r_qk[:, 0:8], HEAD),
                                    ALU.mult).then_inc(*Q_vec.next("q_nope"))
                    v.tensor_tensor(fold(pe_x[:, 0:HEADS, :]), heads_view(2, HEAD, QK, QK), per_head(r_qk[:, 8:16], ROPE),
                                    ALU.mult).then_inc(*Q_vec.next("q_pe"))
                    v.tensor_tensor(fold(ks[u])[:, :, :, 0:HEAD], heads_view(4, 0, HEAD, P), per_head(r_qk[:, 16:24], HEAD),
                                    ALU.mult).then_inc(*Q_vec.next("k_nope"))
                    v.wait_ge(*Q_vec.after(g, "k_nope"))
                    v.tensor_tensor(qs[u][:, :, 0:HEAD], qs[u][:, :, 0:HEAD], wide(gq[:, 0:HEAD], 1, HEADS, HEAD),
                                    ALU.mult).then_inc(*Q_vec.next("q_gained"))
                    link(v.tensor_tensor(pe_x[:, 0:HEADS, :], pe_x[:, 0:HEADS, :], wide(gq[:, HEAD:QK], 1, HEADS, ROPE), ALU.mult),
                         "pe_gained")
                    halves = pe_x.rearrange("p h (a r) -> p h a r", a=2)
                    for tab, dst, name in ((cos, xc, "xc"), (sin, xs, "xs")):
                        v.tensor_tensor(dst, halves, tab[:, t, :].unsqueeze(1).unsqueeze(1).to_broadcast([P, HEADS + 1, 2, HR]),
                                        ALU.mult).then_inc(*Q_vec.next(name))
                    v.wait_ge(*Q_vec.after(g, "xs"))
                    for dst, src in ((qs[u], slice(0, HEADS)), (ks[u], None)):
                        def pick(x, half):
                            if src is None:
                                return x[:, HEADS:HEADS + 1, half, :].to_broadcast([P, HEADS, HR])
                            return x[:, 0:HEADS, half, :]
                        v.tensor_tensor(dst[:, :, HEAD:HEAD + HR], pick(xc, 0), pick(xs, 1), ALU.subtract)
                        ins = v.tensor_tensor(dst[:, :, HEAD + HR:QK], pick(xc, 1), pick(xs, 0), ALU.add)
                    ins.then_inc(*Q_vec.next("heads"))

                def q_lag(t, u, i):
                    g = TILES * l + t
                    v.wait_ge(qk_stored[u], 32 * (PAIRS * l + i) + 32)
                    v.wait_ge(*R_pe.after(g, "q_hi"))
                    v.tensor_copy(stage[u][0:QK, 0, HC:].rearrange("p a b -> p (a b)"), ps[0:QK, 1, :]).then_inc(*R_vec.next("q_hi"))
                    v.wait_ge(*R_pe.after(g, "k_hi"))
                    v.tensor_copy(stage[u][0:QK, 1, HC:].rearrange("p a b -> p (a b)"), ps[0:QK, 0, :]).then_inc(*R_vec.next("k_hi"))

                pair_loop(v, q_main, q_lag)

                def attend(hh, head):
                    def row_max(j):
                        v.wait_ge(*S_pe.after(hh, f"s{j}"))
                        v.tensor_reduce(neg_max[:, j % 2:j % 2 + 1], banks(2 * (j % 2))[:, 0:(j + 1) * P], AX.X, ALU.max,
                                        negate=True).then_inc(*S_vec.next(f"max{j}"))

                    def evac_lo(j):
                        w = min(j + 1, 4) * P
                        v.wait_ge(*T_pe.after(hh, f"lo{j}"))
                        v.tensor_copy(prob_t[0].rearrange("p a b -> p (a b)")[:, 0:w], bank(4, 0, w)).then_inc(*S_vec.next(f"lo{j}"))

                    def finish(j):
                        v.wait_ge(*O_pe.after(hh, f"o{j}"))
                        v.reciprocal(rden[:, j % 2:j % 2 + 1], denom[:, j % 4:j % 4 + 1]).then_inc(*S_vec.next(f"inv{j}"))
                        v.wait_ge(*S_vec.after(hh, f"inv{j}"))
                        v.tensor_scalar(y[:, j, bass.ds(head * HEAD + 2 * SGU, HEAD)], bank(6 + j % 2, 0, HEAD), rden[:, j % 2:j % 2 + 1],
                                        None, ALU.mult).then_inc(*S_vec.next(f"fin{j}"))

                    row_max(0)
                    for j in range(TILES):
                        if j + 1 < TILES:
                            row_max(j + 1)
                        evac_lo(j)
                        if j:
                            finish(j - 1)
                    finish(TILES - 1)

                with v.Fori(0, HEADS // 2) as i:
                    for u in range(2):
                        attend(HEADS * l + 2 * i + u, 2 * i + u)

                def w_main(t, u, i):
                    g = TILES * l + t
                    for k, half in enumerate(("lo", "hi")):
                        v.wait_ge(*W_pe.after(g, half))
                        hv = h[:, t, 512 * k:512 * k + 512]
                        v.tensor_tensor(hv, hv, bank(2 + 2 * u + k), ALU.add).then_inc(*W_vec.next(half))

                tile_loop(v, front(1), w_main)

                def g_main(t, u, i):
                    g = TILES * l + t
                    v.wait_ge(*G_pe.after(g))
                    v.tensor_tensor(lg[:, t, :], bank(2 + u, 0, NG + NE), b_r[:, :], ALU.add).then_inc(*G_vec.next("logits"))

                v.wait_ge(*W_vec.before(TILES * l + TILES))
                tile_loop(v, front(2), g_main)
                v.wait_ge(*G_vec.before(TILES * l + TILES))

                def link(ins, name):
                    ins.then_inc(*K_vec.next(name))
                    v.wait_ge(*K_vec.after(l, name))

                def sm(i):
                    return at(A, RS + 2560 + 8 * i, TILES)

                def bc(ap, n):
                    return ap.unsqueeze(2).to_broadcast([P, TILES, n])

                def row(n):
                    return iota[:, 0:n].unsqueeze(1).to_broadcast([P, TILES, n])

                gl_ = lg[:, :, 0:NG]
                el = lg[:, :, NG:NG + NE]
                link(v.tensor_reduce(sm(0), gl_, AX.X, ALU.max), "g_max")
                link(v.tensor_tensor(rs(0, TILES, NG), gl_, bc(sm(0), NG), ALU.subtract), "g_diff")
                v.wait_ge(*K_act.after(l, "g_exp"))
                link(v.tensor_reduce(sm(1), rs(1, TILES, NG), AX.X, ALU.add), "g_sum")
                link(v.reciprocal(sm(2), sm(1)), "g_w")
                link(v.tensor_scalar(rs(2, TILES, NG), rs(0, TILES, NG), 0.0, 64.0, ALU.is_lt, ALU.mult), "g_miss")
                link(v.tensor_tensor(rs(3, TILES, NG), rs(2, TILES, NG), row(NG), ALU.add), "g_cand")
                link(v.tensor_reduce(sm(3), rs(3, TILES, NG), AX.X, ALU.min), "g_first")
                link(v.tensor_tensor(rs(4, TILES, NG), row(NG), bc(sm(3), NG), ALU.is_equal), "g_hot")
                link(v.tensor_scalar(rs(5, TILES, NG), rs(4, TILES, NG), 1.0, BIG, ALU.subtract, ALU.mult), "g_far")
                link(v.tensor_tensor(rs(6, TILES, NG, EPG), el.rearrange("p t (g e) -> p t g e", g=NG),
                                     rs(5, TILES, NG).unsqueeze(3).to_broadcast([P, TILES, NG, EPG]), ALU.add), "e_in")

                def largest(src, top, where, hot, n):
                    link(v.tensor_reduce(top, src, AX.X, ALU.max), f"m{n}")
                    link(v.tensor_tensor(rs(7, TILES, NE), src, bc(top, NE), ALU.subtract), f"d{n}")
                    link(v.tensor_scalar(rs(8, TILES, NE), rs(7, TILES, NE), 0.0, 64.0, ALU.is_lt, ALU.mult), f"miss{n}")
                    link(v.tensor_tensor(rs(7, TILES, NE), rs(8, TILES, NE), row(NE), ALU.add), f"cand{n}")
                    link(v.tensor_reduce(where, rs(7, TILES, NE), AX.X, ALU.min), f"i{n}")
                    link(v.tensor_tensor(hot, row(NE), bc(where, NE), ALU.is_equal), f"hot{n}")

                hot1, hot2, rest = rs(2, TILES, NE), rs(4, TILES, NE), rs(3, TILES, NE)
                largest(rs(6, TILES, NE), sm(4), sm(5), hot1, 1)
                link(v.scalar_tensor_tensor(rest, hot1, -2 * BIG, rs(6, TILES, NE), ALU.mult, ALU.add), "rest")
                largest(rest, sm(6), sm(7), hot2, 2)
                link(v.tensor_tensor(picked_b, hot1, hot2, ALU.add), "picked")
                e2 = rs(9, 2, TILES)
                link(v.tensor_tensor(e2[:, 0], sm(6), sm(4), ALU.subtract), "e_diff")
                cnt = at(A, RS + 2816, 4).bitcast(I32)[0:NE]
                v.wait_ge(*K_pe.after(l, "ranks"))
                link(v.tensor_copy(cnt[:, 0:1], ps[0:NE, 6, 0:1]), "cnt_i")
                link(v.tensor_scalar(cnt[:, 1:2], cnt[:, 0:1], P - 1, None, ALU.add), "cnt_up")
                link(v.tensor_scalar(cnt[:, 2:3], cnt[:, 1:2], 7, None, ALU.logical_shift_right), "cnt_nb")
                nb_f = at(A, RS + 2824, 1)[0:NE]
                link(v.tensor_copy(nb_f, cnt[:, 2:3]), "nb_f")
                link(v.tensor_scalar(nb_col[0:NE, :], ones_b[0:NE, :], nb_f, None, ALU.mult), "nb_col")
                v.wait_ge(*K_pe.after(l, "starts"))
                ends = rs(5, 2, NE)
                link(v.tensor_copy(ends, bank(6, 64, 64 + 2 * NE).rearrange("p (a e) -> p a e", a=2)), "start_f")
                link(v.scalar_tensor_tensor(rs(6, TILES, NE), ends[:, 0].unsqueeze(1).to_broadcast([P, TILES, NE]), float(P),
                                            bank(7, 0, TILES * NE).rearrange("p (t e) -> p t e", t=TILES), ALU.mult, ALU.add), "row")
                dest_f, dest = at(A, RS + 2832, TILES, 2), at(A, RS + 2896, TILES, 2).bitcast(I32)
                for k, hot in enumerate((hot1, hot2)):
                    link(v.tensor_tensor(rs(7 + k, TILES, NE), hot, rs(6, TILES, NE), ALU.mult), f"r{k + 1}")
                    link(v.tensor_reduce(dest_f[:, :, k], rs(7 + k, TILES, NE), AX.X, ALU.add), f"dest{k + 1}")
                link(v.tensor_copy(dest, dest_f), "dest_i")
                blk_i = at(A, RS + 2848, TILES, 2).bitcast(I32)
                blk_f, slot_f = at(A, RS + 2864, TILES, 2), at(A, RS + 2880, TILES, 2)
                link(v.tensor_scalar(blk_i, dest, 7, None, ALU.logical_shift_right), "blk_i")
                link(v.tensor_copy(blk_f, blk_i), "blk_f")
                link(v.scalar_tensor_tensor(slot_f, blk_f, -float(P), dest_f, ALU.mult, ALU.add), "slot_f")
                for c in range(2 * TILES):
                    t, k = divmod(c, 2)
                    v.tensor_scalar(hot_s[:, c, :], iota[:, :], slot_f[:, t, k:k + 1], None, ALU.is_equal)
                    ins = v.tensor_scalar(hot_b[:, c, :], iota[:, 0:MAXB1], blk_f[:, t, k:k + 1], token[:, t, k:k + 1],
                                          ALU.is_equal, ALU.mult)
                ins.then_inc(*K_vec.next("hots"))
                le = at(C, 4096, MAXB1, NE)[0:1]
                owner = at(C, 4096 + 2048, MAXB1)[0:1]
                active = at(C, 4096 + 2112, MAXB1)[0:1]
                by_slot = at(C, 4096 + 2176, 3)[0:1]
                total = ends[0:1, 1, NE - 1:NE]
                link(v.tensor_tensor(le, ends[0:1, 1].unsqueeze(1).to_broadcast([1, MAXB1, NE]),
                                     iota[0:1, 0:MAXB1].unsqueeze(2).to_broadcast([1, MAXB1, NE]), ALU.is_le), "le")
                link(v.tensor_reduce(owner, le, AX.X, ALU.add), "owner")
                link(v.tensor_scalar(active, iota[0:1, 0:MAXB1], total, None, ALU.is_lt), "active")
                link(v.tensor_reduce(by_slot, active.rearrange("p (i u) -> p u i", u=3), AX.X, ALU.add), "by_slot")
                v.wait_ge(*K_act.after(l, "e_exp"))
                link(v.tensor_scalar(sm(8), e2[:, 1], 1.0, None, ALU.add), "e_den")
                link(v.reciprocal(sm(9), sm(8)), "e_rden")
                link(v.scalar_tensor_tensor(wts[:, 0], sm(2), 0.5, sm(9), ALU.mult, ALU.mult), "w1")
                link(v.tensor_tensor(wts[:, 1], wts[:, 0], e2[:, 1], ALU.mult), "w2")
                link(v.tensor_copy(cells[0:1, 48:52], run[:, :]), "before")
                link(v.tensor_tensor(run[:, 0:1], run[:, 0:1], total, ALU.add), "run_n")
                link(v.tensor_tensor(run[:, 1:4], run[:, 1:4], by_slot, ALU.add), "run_slots")
                v.wait_ge(*K_pe.after(l, "lists"))
                spare = rs(0, MAXB1)
                link(v.tensor_scalar(spare, bank(6, 128, 128 + MAXB1), 0.0, padding[:, :], ALU.is_equal, ALU.mult), "empty")
                link(v.scalar_tensor_tensor(out_idx[:, 0:MAXB1], bank(6, 128, 128 + MAXB1), -1.0, spare, ALU.add, ALU.add), "rows_i")
                v.tensor_scalar(idx[:, 0:MAXB1], out_idx[:, 0:MAXB1], SEQ - 1, None, ALU.bitwise_and).then_inc(*K_vec.next("list_i"))
                v.tensor_copy(cells[0:1, 0:MAXB1], owner).then_inc(*K_vec.next("owner_i"))
                v.tensor_copy(cells[0:1, 52:53], total).then_inc(*K_vec.next("cells"))

                prev, n, used = counters(v, l, passed)

                def x_hi(m):
                    v.wait_ge(*M_xT.after(m, "hi"))
                    v.tensor_copy(xT[:, 4:8].rearrange("p a b -> p (a b)"), bank(1)).then_inc(*M_xhi.next("x"))

                def hidden(m):
                    v.wait_ge(*M_tanh.after(m))
                    v.scalar_tensor_tensor(hid, hid_g, 1.0, bank(2, 0, F), ALU.add, ALU.mult).then_inc(*M_silu.next("silu"))
                    v.wait_ge(*M_silu.after(m))
                    v.tensor_tensor(hid, hid, bank(2, F, 2 * F), ALU.mult).then_inc(*M_prod.next("prod"))

                def y_hi(m):
                    v.wait_ge(y_stored, m * 16)
                    v.wait_ge(*M_dn.after(m, "hi"))
                    v.tensor_copy(y_blk[:, 512:1024], bank(5)).then_inc(*M_yhi.next("y"))

                x_hi(prev)
                hidden(prev)
                x_hi(prev + 1)

                def expert(b, here, nxt, last):
                    m = prev + b
                    guarded(v, b < n, lambda: hidden(m))
                    guarded(v, b + 1 < n, lambda: x_hi(m + 1))
                    guarded(v, b <= n, lambda: y_hi(m - 1))

                block_loop(v, expert)
                v.drain().then_inc(blocks_done, 1)

                v.wait_ge(ple_loaded, 64 * l + 64)
                settle(v, passed)

                def ple_front(t, u, i):
                    g = TILES * l + t
                    v.wait_ge(y_fetched[u], 32 * (PAIRS * l + i) + 32)
                    v.scalar_tensor_tensor(h[:, t, :], y_got[u][0], wts[:, 0, t:t + 1] if isinstance(t, int) else wts[:, 0, bass.ds(t, 1)],
                                           h[:, t, :], ALU.mult, ALU.add).then_inc(*E_comb.next("first"))
                    v.wait_ge(*E_comb.after(g, "first"))
                    v.scalar_tensor_tensor(h[:, t, :], y_got[u][1], wts[:, 1, t:t + 1] if isinstance(t, int) else wts[:, 1, bass.ds(t, 1)],
                                           h[:, t, :], ALU.mult, ALU.add).then_inc(*E_comb.next("second"))
                    front(3)(t, u, i)

                def ple_main(t, u, i):
                    g = TILES * l + t
                    v.wait_ge(*E_pool.after(g, "rstd"))
                    v.wait_ge(h_final, g + TILES)
                    v.scalar_tensor_tensor(e_buf, banks(4), m_e[:, 2:3], gains[:, BRANCH], ALU.mult, ALU.mult).then_inc(*E_vec.next("e_scaled"))
                    v.wait_ge(*E_vec.after(g, "e_scaled"))
                    v.wait_ge(*E_act.after(g, "t_hi"))
                    v.scalar_tensor_tensor(e_buf, gate_t, 1.0, e_buf, ALU.add, ALU.mult).then_inc(*E_vec.next("gated"))
                    v.wait_ge(*E_vec.after(g, "gated"))
                    v.tensor_tensor(h[:, t, :], h[:, t, :], e_buf, ALU.add).then_inc(h_final, 1)

                tile_loop(v, ple_front, ple_main)

        @block.tensor
        def _(pe):
            passed = sem("pe_passed")
            for s in (C_pe, R_pe):
                pe.sem_inc(s.sem, s.per)
            T = nc.tensor.transpose
            mm = nc.tensor.matmul
            pe.wait_ge(*S_pool0.after(0, "selects"))
            pe.wait_ge(*S_vec0.after(0, "pos"))
            T(bank(0, 0, TILES), at(B, T0 + 280, P)[0:TILES], ident[0:TILES, 0:TILES]).then_inc(*S_pe0.next("pos_t"))
            pe.wait_ge(*S_vec0.after(0, "cols"))

            with pe.Fori(0, DEPTH) as l:
                pe.wait_ge(*L_pool.after(l))
                pe.wait_ge(*E_act.before(TILES * l))
                pe.wait_ge(*E_vec.before(TILES * l))
                for k in range(GROUPS):
                    T(bank(7, P * k, P * k + P), ws_raw[:, k, :], ident[:, :])
                for c in range(2):
                    T(bank(6, 32 * c, 32 * c + 32), cw_raw[:, P * c:P * c + P], ident[0:32, 0:32])
                T(bank(6, 64, 64 + GROUPS), sb_raw[:, :], ident[0:GROUPS, 0:GROUPS]).then_inc(*L_pe.next("prep_T"))
                pe.wait_ge(*L_act.after(l))

                def front(ph):
                    def go(t, u, i):
                        r = 32 * l + t + 8 * ph
                        pe.wait_ge(*F_act.before(r))
                        pe.wait_ge(*F_vec.before(r))
                        pe.wait_ge(*F_vec.after(r, "a"))
                        for k in range(KD):
                            ins = T(bank(k // 4, P * (k % 4), P * (k % 4) + P), a_buf[u][:, P * k:P * k + P], ident[:, :])
                            if k % 4 == 3:
                                ins.then_inc(*F_pe.next(("T_lo", "T_hi")[k // 4]))
                    return go

                def front_ready(ph, t):
                    r = 32 * l + t + 8 * ph
                    pe.wait_ge(*F_act.after(r, "aT_lo"))
                    pe.wait_ge(*F_vec.after(r, "aT_hi"))

                def product(dst, u, w, a, b):
                    for k in range(KD):
                        ins = mm(dst, aT[u][:, k, :], w[:, k, a:b], start=(k == 0), stop=(k == KD - 1))
                    return ins

                pe.wait_ge(w_in_loaded, 16 * l + 16)
                settle(pe, passed)

                def z_first(t, u):
                    g = TILES * l + t
                    front_ready(0, t)
                    pe.wait_ge(*Z_vec.before(g))
                    product(bank(2), u, w_in, 0, 512).then_inc(*Z_pe.next("z_sgu"))
                    product(bank(3), u, w_in, 512, 1024).then_inc(*Z_pe.next("z_glu"))

                def conv_back(t, u):
                    q = TILES * l + t
                    pe.wait_ge(*C_vec.after(q, f"tap{TAPS - 1}_1"))
                    for c in range(2):
                        ins = T(bank(7, P * c, P * c + P), acc[:, c, :], ident[:, :])
                    ins.then_inc(*C_pe.next("coT"))

                def z_second(t, u):
                    g = TILES * l + t
                    pe.wait_ge(*Z_act.before(g))
                    product(bank(4, 0, MLA_IN), u, w_in, 1024, IN).then_inc(*Z_pe.next("z_mla"))
                    pe.wait_ge(*Z_vec.after(g, "v_ready"))
                    for k in range(GROUPS):
                        ins = mm(bank(5, HEAD * k, HEAD * k + HEAD), wsT[:, k, :], v_n[:, k, :], start=True, stop=True)
                    ins.then_inc(*Z_pe.next("s"))
                    for c in range(2):
                        ins = T(bank(6, P * c, P * c + P), gl[:, P * c:P * c + P], ident[:, :])
                    ins.then_inc(*Z_pe.next("gluT"))

                def pointwise(t, u):
                    q = TILES * l + t
                    pe.wait_ge(*C_vec.after(q, "c_silu"))
                    for c in range(2):
                        ins = T(bank(7, 256 + P * c, 256 + P * c + P), c_y[:, P * c:P * c + P], ident[:, :])
                    ins.then_inc(*C_pe.next("ybT"))
                    pe.wait_ge(*C_act.after(q, "ybT_evac"))
                    for c in range(2):
                        ins = mm(bank(5, 256, 512), c_yT[:, c, :], pw[:, c, :], start=(c == 0), stop=(c == 1))
                    ins.then_inc(*C_pe.next("pw"))

                mixer_loop(pe, front(0), [("main", z_first), ("tail", conv_back), ("main", z_second), ("tail", pointwise)])

                end = TILES * l + TILES
                for s in (Z_vec, C_vec, Z_act):
                    pe.wait_ge(*s.before(end))
                settle(pe, passed)

                def q_main(t, u, i):
                    g = TILES * l + t
                    pe.wait_ge(*Q_vec.after(g, "cn"))
                    for k in range(3):
                        ins = T(bank(6, P * k, P * k + P), cn[:, P * k:P * k + P], ident[:, :])
                    ins.then_inc(*Q_pe.next("cT"))
                    pe.wait_ge(*Q_act.after(g, "cnT"))
                    pe.wait_ge(*Q_vec.before(g))
                    for half in range(2):
                        w = HC * QK
                        for k in range(2):
                            ins = mm(bank(2 + half, 0, w), cnT[:, k, :], w_uq[:, k, w * half:w * half + w], start=(k == 0), stop=(k == 1))
                    ins.then_inc(*Q_pe.next("q_mm"))
                    for half in range(2):
                        ins = mm(bank(4 + half), cnT[:, 2, :], w_ukv[:, 512 * half:512 * half + 512], start=True, stop=True)
                    ins.then_inc(*Q_pe.next("kv_mm"))

                def q_lag(t, u, i):
                    g = TILES * l + t
                    pe.wait_ge(*R_act.before(g))
                    pe.wait_ge(*R_vec.before(g))
                    pe.wait_ge(*Q_vec.after(g, "heads"))
                    for name, b, src in (("q_lo", 0, qs[u][:, 0:HC]), ("q_hi", 1, qs[u][:, HC:]), ("k_lo", 7, ks[u][:, 0:HC]),
                                         ("k_hi", 0, ks[u][:, HC:])):
                        if name == "k_hi":
                            pe.wait_ge(*R_act.after(g, "q_lo"))
                        for k in range(HC):
                            ins = T(ps[0:QK, b, P * k:P * k + P], src[:, k, :], ident[:, :])
                        ins.then_inc(*R_pe.next(name))

                pair_loop(pe, q_main, q_lag)

                for s in (Q_vec, Q_act, R_act, R_vec):
                    pe.wait_ge(*s.before(end))
                settle(pe, passed)

                def attend(hh, i, u, head):
                    pe.wait_ge(qk_loaded[u], 32 * (HEADS // 2 * l + i) + 32)
                    settle(pe, passed)

                    def scores(j):
                        q = q_ring[u][0:QK, P * j:P * j + P]
                        b = 2 * (j % 2)
                        cols = (j + 1) * P
                        for c in range(0, cols, 512):
                            w = min(512, cols - c)
                            last = c + 512 >= cols
                            mm(bank(b + c // 512, 0, w), q, k_ring[u][0:QK, c:c + w], start=True, stop=not last, skip_group_check=True)
                        d = (j * P) % 512
                        mm(bank(b + j // 4, d, d + P), ident_b[:, :], mask_b[:, :], start=False, stop=True,
                           skip_group_check=True).then_inc(*S_pe.next(f"s{j}"))

                    def outputs(j):
                        pe.wait_ge(*S_act.after(hh, f"exp{j}"))
                        for k in range(j + 1):
                            ins = T(bank(4 + k // 4, P * (k % 4), P * (k % 4) + P), prob[j % 2][:, P * k:P * k + P], ident[:, :])
                            if k == min(j, 3):
                                ins.then_inc(*T_pe.next(f"lo{j}"))
                        if j >= 4:
                            ins.then_inc(*T_pe.next(f"hi{j}"))
                        pe.wait_ge(*S_vec.after(hh, f"lo{j}"))
                        if j < 2:
                            pe.wait_ge(*S_vec.before(hh))
                        else:
                            pe.wait_ge(*S_vec.after(hh, f"fin{j - 2}"))
                        for k in range(j + 1):
                            if k == 4:
                                pe.wait_ge(*S_act.after(hh, f"hi{j}"))
                            ins = mm(bank(6 + j % 2, 0, HEAD), prob_t[k // 4][:, k % 4, :], vals[:, k, head, :], start=(k == 0),
                                     stop=(k == j))
                        ins.then_inc(*O_pe.next(f"o{j}"))

                    scores(0)
                    for j in range(TILES):
                        if j + 1 < TILES:
                            scores(j + 1)
                        outputs(j)

                with pe.Fori(0, HEADS // 2) as i:
                    for u in range(2):
                        attend(HEADS * l + 2 * i + u, i, u, 2 * i + u)

                pe.wait_ge(*S_vec.before(HEADS * l + HEADS))
                pe.wait_ge(wo_loaded, 16 * l + 16)
                settle(pe, passed)

                def w_main(t, u, i):
                    g = TILES * l + t
                    front_ready(1, t)
                    pe.wait_ge(*W_vec.after(g - 2))
                    for k, half in enumerate(("lo", "hi")):
                        product(bank(2 + 2 * u + k), u, w_o, 512 * k, 512 * k + 512).then_inc(*W_pe.next(half))

                tile_loop(pe, front(1), w_main)

                pe.wait_ge(*W_vec.before(end))
                settle(pe, passed)

                def g_main(t, u, i):
                    g = TILES * l + t
                    front_ready(2, t)
                    pe.wait_ge(*G_vec.after(g - 2))
                    product(bank(2 + u, 0, NG + NE), u, w_r, 0, NG + NE).then_inc(*G_pe.next("logits"))

                tile_loop(pe, front(2), g_main)

                pe.wait_ge(*K_vec.after(l, "picked"))
                settle(pe, passed)
                for t in range(TILES):
                    mm(ps[0:NE, 6, 0:1], picked_b[:, t, :], ones_b[:, 0:1], start=(t == 0), stop=(t == TILES - 1))
                for t in range(TILES):
                    for s in range(t + 1):
                        lhs = tri_b if s == t else ones_b
                        ins = mm(bank(7, NE * t, NE * t + NE), lhs[:, :], picked_b[:, s, :], start=(s == 0), stop=(s == t))
                ins.then_inc(*K_pe.next("ranks"))
                pe.wait_ge(*K_vec.after(l, "nb_col"))
                settle(pe, passed)
                mm(bank(6, 64, 64 + NE), nb_col[0:NE, :], tri_b[0:NE, 0:NE], start=True, stop=True)
                mm(bank(6, 64 + NE, 64 + 2 * NE), nb_col[0:NE, :], tri_b[0:NE, 0:NE], start=True, stop=False)
                mm(bank(6, 64 + NE, 64 + 2 * NE), nb_col[0:NE, :], ident_b[0:NE, 0:NE], start=False,
                   stop=True).then_inc(*K_pe.next("starts"))
                pe.wait_ge(*K_vec.after(l, "hots"))
                settle(pe, passed)
                for c in range(2 * TILES):
                    ins = mm(bank(6, 128, 128 + MAXB1), hot_s[:, c, :], hot_b[:, c, :], start=(c == 0), stop=(c == 2 * TILES - 1))
                ins.then_inc(*K_pe.next("lists"))

                prev, n, used = counters(pe, l, passed)

                def turn_x(m, s, use):
                    pe.wait_ge(x_gathered[s], (used[s] + use) * 16 + 16)
                    pe.wait_ge(*M_xlo.before(m))
                    pe.wait_ge(*M_xhi.before(m))
                    for k in range(KD):
                        ins = T(bank(k // 4, P * (k % 4), P * (k % 4) + P), x_blk[s][:, P * k:P * k + P], ident[:, :])
                        if k % 4 == 3:
                            ins.then_inc(*M_xT.next(("lo", "hi")[k // 4]))

                def gate_up(m, s, use):
                    pe.wait_ge(gu_loaded[s], (used[s] + use) * 32 + 32)
                    pe.wait_ge(*M_xlo.after(m))
                    pe.wait_ge(*M_xhi.after(m))
                    for k in range(KD):
                        ins = mm(bank(2), xT[:, k, :], w_gu[s][:, k, :], start=(k == 0), stop=(k == KD - 1))
                    ins.then_inc(*M_gu.next("gu"))

                def down(m, s, use):
                    pe.wait_ge(dn_loaded[s], (used[s] + use) * 16 + 16)
                    pe.wait_ge(*M_h.after(m))
                    pe.wait_ge(*M_ylo.before(m))
                    pe.wait_ge(*M_yhi.before(m))
                    for half in range(2):
                        for k in range(2):
                            ins = mm(bank(4 + half), hid_t[:, k, :], w_dn[s][:, k, 512 * half:512 * half + 512], start=(k == 0),
                                     stop=(k == 1))
                        ins.then_inc(*M_dn.next(("lo", "hi")[half]))

                def turn_h(m):
                    pe.wait_ge(*M_prod.after(m))
                    for k in range(2):
                        ins = T(bank(3, P * k, P * k + P), hid[:, P * k:P * k + P], ident[:, :])
                    ins.then_inc(*M_hT.next("hT"))

                turn_x(prev, 0, 0)
                gate_up(prev, 0, 0)
                turn_x(prev + 1, 1, 0)
                turn_h(prev)

                def expert(b, here, nxt, last):
                    m = prev + b
                    guarded(pe, b < n, lambda: gate_up(m, *here))
                    guarded(pe, b + 1 < n, lambda: turn_x(m + 1, *nxt))
                    guarded(pe, b <= n, lambda: down(m - 1, *last))
                    guarded(pe, b < n, lambda: turn_h(m))

                block_loop(pe, expert)

                pe.wait_ge(ple_loaded, 64 * l + 64)
                settle(pe, passed)

                def ple_main(t, u, i):
                    g = TILES * l + t
                    pe.wait_ge(p_loaded[u], 16 * (PAIRS * l + i) + 16)
                    pe.wait_ge(*E_act.after(g - 1, "pT"))
                    for k in range(2):
                        ins = T(bank(6, P * k, P * k + P), p_tile[u][:, P * k:P * k + P], ident[:, :])
                    ins.then_inc(*E_pe.next("pT"))
                    front_ready(3, t)
                    for k, half in enumerate(("g_lo", "g_hi")):
                        pe.wait_ge(*E_act.after(g - 1, ("t_lo", "t_hi")[k]))
                        product(bank(2 + k), u, ple_g, 512 * k, 512 * k + 512).then_inc(*E_pe.next(half))
                    pe.wait_ge(*E_act.after(g, "pT"))
                    pe.wait_ge(*E_vec.after(g - 1, "e_scaled"))
                    for half in range(2):
                        for k in range(2):
                            ins = mm(bank(4 + half), pT[:, k, :], ple_p[:, k, 512 * half:512 * half + 512], start=(k == 0), stop=(k == 1))
                    ins.then_inc(*E_pe.next("e"))

                tile_loop(pe, front(3), ple_main)


_INS = ["x", "p", "positions", "mix_norm_g", "w_in", "sgu_ln_g", "sgu_ln_b", "sgu_w", "sgu_b", "conv_w", "conv_b",
        "conv_ln_g", "conv_ln_b", "conv_pw_w", "conv_pw_b", "q_a_norm_g", "w_uq", "kv_a_norm_g", "w_ukv", "q_norm_g",
        "k_norm_g", "branch_norm_g", "w_o", "ffn_norm_g", "router_group_w", "router_group_b", "router_expert_w",
        "router_expert_b", "moe_w_gate", "moe_w_up", "moe_w_down", "ple_norm_g", "ple_gate_w", "ple_proj_w",
        "ple_post_norm_g"]


def kernel(**inputs):
    import numpy as _np
    import concourse.bacc as _bacc
    from concourse import mybir as _mybir
    from concourse.bass_utils import run_bass_kernel_spmd as _run

    nc = _bacc.Bacc("TRN2", target_bir_lowering=False, num_devices=1)
    arrays, args = {}, {}
    for name in _INS:
        a = _np.ascontiguousarray(inputs[name])
        arrays[f"in_{name}_dram"] = a
        args[name] = nc.dram_tensor(f"in_{name}_dram", a.shape, _mybir.dt.from_np(a.dtype), kind="ExternalInput").ap()
    out = nc.dram_tensor("out_0_dram", inputs["x"].shape, _mybir.dt.from_np(_np.dtype("float32")), kind="ExternalOutput").ap()
    build(nc, args, out)
    r = _run(nc, [arrays], core_ids=[0])
    return r.results[0]["out_0_dram"]
```

```python
from contextlib import ExitStack

import numpy as np

import concourse.bass as bass
from concourse import mybir

F32 = mybir.dt.float32
BF16 = mybir.dt.bfloat16
F16 = mybir.dt.float16
I32 = mybir.dt.int32
ALU = mybir.AluOpType
ACT = mybir.ActivationFunctionType
AX = mybir.AxisListType

P = 128
HEAD = 64
EPS = 1e-6
ROPE_THETA = 10000.0
BIG = 1e30
GELU_C = 0.7978845608028654
GELU_A = 0.044715
ROUND = 12582912.0
TWO_PI_HI = 6.28125
TWO_PI_MID = round((2 * np.pi - TWO_PI_HI) * 2 ** 20) / 2 ** 20
TWO_PI_LO = float(np.float32(2 * np.pi - TWO_PI_HI - TWO_PI_MID))


class Steps:

    def __init__(self, sem, names, credit=0):
        self.sem, self.names, self.per, self.credit, self.at = sem, list(names), len(names), credit, 0

    def next(self, name):
        assert self.names[self.at] == name, (name, self.names[self.at])
        self.at = (self.at + 1) % self.per
        return self.sem, 1

    def after(self, index, name=None):
        n = self.per if name is None else self.names.index(name) + 1
        return self.sem, index * self.per + (n + self.credit * self.per)

    def before(self, index):
        return self.sem, index * self.per + self.credit * self.per


class Front:

    def __init__(self, steps, name):
        self.square = steps(name + "_square", ["squared"], credit=1)
        self.pool = steps(name + "_pool", ["eps", "rstd"], credit=1)
        self.a = steps(name + "_a", ["a"], credit=1)
        self.pe = steps(name + "_pe", ["T_lo", "T_hi"], credit=1)
        self.lo = steps(name + "_lo", ["aT"], credit=1)
        self.hi = steps(name + "_hi", ["aT"], credit=1)


def build(nc, I, out):
    DEPTH, _, SEQ, PLE = I["p"].shape
    D = I["x"].shape[2]
    TILES, KD = SEQ // P, D // P
    SGU = I["sgu_ln_g"].shape[1]
    GROUPS = SGU // HEAD
    TAPS = I["conv_w"].shape[1]
    QR, KVR = I["q_a_norm_g"].shape[1], I["kv_a_norm_g"].shape[1]
    QK = I["q_norm_g"].shape[1]
    HEADS = I["w_uq"].shape[2] // QK
    ROPE = QK - HEAD
    HR = ROPE // 2
    IN = I["w_in"].shape[2]
    MLA_IN = IN - 4 * SGU
    NG, NE = I["router_group_w"].shape[2], I["router_expert_w"].shape[2]
    EPG = NE // NG
    F = I["moe_w_gate"].shape[3]
    TOPK = 2
    MAXB = (SEQ * TOPK - NE) // P + NE
    MAXB1 = MAXB + 1
    SCALE = float(QK) ** -0.5
    HC = HEADS // 2
    PAIRS = TILES // 2
    assert (TILES, KD, D, F, MAXB1 % 3, HC * P) == (8, 8, 1024, 256, 0, 512)

    with ExitStack() as ctx:
        def sb(name, shape, dt=F32):
            return ctx.enter_context(nc.sbuf_tensor(name, shape, dt))

        def sem(name):
            return ctx.enter_context(nc.semaphore(name))

        def steps(name, names, credit=0):
            return Steps(sem(name), names, credit)

        m_dram = nc.dram_tensor("moe_inputs", (SEQ, D), F32).ap()
        y_rows = nc.dram_tensor("choice_outputs", (2 * SEQ + P, D), F32).ap()
        qk_dram = nc.dram_tensor("qk_heads", (2, QK, HEADS, SEQ), F32).ap()

        ps = ctx.enter_context(nc.psum_tensor("ps", [P, 8, 512], F32))

        def bank(n, a=0, b=512):
            return ps[:, n, a:b]

        def banks(n):
            return ps[:, n:n + 2, :].rearrange("p a b -> p (a b)")

        h = sb("h", [P, TILES, D])
        A = sb("region_a", [P, KD * IN])
        B = sb("region_b", [P, 2 * TILES * 640])
        C = sb("region_c", [P, 13312])
        junk = sb("junk", [P, D])
        gains = sb("gains", [P, 3, D])
        MIX, BRANCH, FFN = 0, 1, 2

        def at(region, off, *shape):
            n = int(np.prod(shape))
            v = region[:, off:off + n]
            if len(shape) == 1:
                return v
            names = " ".join("abcd"[:len(shape)])
            return v.rearrange(f"p ({names}) -> p {names}", **dict(zip("abcd", shape)))

        w_in = at(A, 0, KD, IN)
        stage = [at(A, 2048 * u, 2, HEADS, P) for u in range(2)]
        q_ring = [at(A, 4096 + 1024 * u, SEQ) for u in range(2)]
        k_ring = [at(A, 6144 + 1024 * u, SEQ) for u in range(2)]
        prob = [at(A, 8192 + 1024 * u, SEQ) for u in range(2)]
        prob_t = [at(A, 10240, TILES, P), at(A, 0, TILES, P)]
        qk_sq = at(A, 8192, HEADS, QK)
        k_sq = at(A, 8192 + 768, HEADS, HEAD)
        xc = at(A, 9472, HEADS + 1, 2, HR)
        xs = at(A, 9472 + 288, HEADS + 1, 2, HR)
        pe_x = at(A, 10240, HEADS, ROPE)
        x_blk = [at(A, 6144 + 1024 * u, D) for u in range(3)]
        m_buf = [at(A, 1024 * u, D) for u in range(2)]
        mT = at(A, 2048, KD, P)
        junk_m = at(A, 3072, D)
        xT = at(A, 9216, KD, P)
        hid = at(A, 10240, F)
        hid_t = at(A, 10496, 2, P)
        hid_g = at(A, 10752, F)
        w_uq = at(B, 0, 2, HEADS * QK)
        w_ukv = at(B, 1536, HEADS * 2 * HEAD)
        zc = at(B, 2560, TILES, MLA_IN)
        T0 = 2560 + TILES * MLA_IN
        sg_t, sg_uv = at(B, T0, 512), at(B, T0 + 512, 512)
        gl_t, gl = at(B, T0 + 1024, SGU), at(B, T0 + 1280, SGU)
        v_c, v_sq, v_n = (at(B, T0 + 1536 + 256 * i, GROUPS, HEAD) for i in range(3))
        acc = at(B, T0 + 2304, 2, P)
        c_c, c_sq, c_n = (at(B, T0 + 2560 + 256 * i, GROUPS, HEAD) for i in range(3))
        c_th, c_y = at(B, T0 + 3328, SGU), at(B, T0 + 3584, SGU)
        c_yT = at(B, T0 + 3840, 2, P)
        cn = [at(B, T0 + 384 * u, QR + KVR) for u in range(2)]
        cnT = at(B, T0 + 768, 3, P)
        qs = [at(B, T0 + 1152 + 1536 * u, HEADS, QK) for u in range(2)]
        ks = [at(B, T0 + 1920 + 1536 * u, HEADS, QK) for u in range(2)]
        w_o = at(B, 0, KD, D)
        ple_g = at(B, 0, KD, D)
        ple_p = at(B, KD * D, 2, D)
        a_buf = [at(C, 1024 * u, D) for u in range(2)]
        aT = [at(C, 2048 + 1024 * u, KD, P) for u in range(2)]
        vals = at(C, 0, TILES, HEADS, HEAD)
        y = at(C, 4096, TILES, D)
        cin = [at(C, 12288 + 316 * u, 2, P + TAPS - 1) for u in range(2)]
        y_blk = at(C, 12288, D)
        y_got = [[at(C, 4096 + 2048 * u + 1024 * k, D) for k in range(2)] for u in range(2)]
        gate_t, e_buf = at(C, 8192, D), at(C, 9216, D)
        p_tile = [at(C, 10240 + 256 * u, PLE) for u in range(2)]
        junk_e = at(C, 11264, D)
        pT = [at(C, 10752 + 256 * u, 2, P) for u in range(2)]
        slot = [C[:, 0:6144], C[:, 6144:12288], A[:, 0:6144]]
        w_gu = [s[:, 0:KD * 2 * F].rearrange("p (k f) -> p k f", k=KD) for s in slot]
        w_dn = [s[:, KD * 2 * F:6144].rearrange("p (k f) -> p k f", k=2) for s in slot]
        RS = 6144

        def rs(i, *shape):
            return at(A, RS + 256 * i, *shape)

        vec = sb("vecs", [P, 7 * 256])
        names = ["sgu_g", "sgu_b", "cln_g", "cln_b", "pw_b", "qa_g"]
        V = {n: vec[:, 256 * i:256 * i + 256] for i, n in enumerate(names)}
        V["kva_g"] = vec[:, 1536:1536 + KVR]
        qg = sb("q_gain", [P, QK])
        kg = sb("k_gain", [P, QK])
        gq = sb("score_gain", [P, QK])
        ws_raw = at(C, 11264, GROUPS, P)
        wsT = sb("sgu_w_t", [P, GROUPS, P])
        cw_raw = at(C, 11776, SGU)[0:32]
        cw = sb("conv_w_cols", [P, 2, 32])
        sb_raw = at(C, 12032, P)[0:GROUPS]
        s_bias = sb("sgu_b_cols", [P, GROUPS])
        pw = sb("conv_pw", [P, 2, SGU])
        w_r = sb("router_w", [P, KD, NG + NE])
        b_r = sb("router_b", [P, NG + NE])
        lg = sb("logits", [P, TILES, NG + NE])
        wts = sb("moe_weights", [P, 2, TILES])
        idx = sb("block_tokens", [P, MAXB1 + 3], I32)
        out_idx = sb("block_rows", [P, MAXB1 + 3], I32)
        idx_ring = sb("idx_ring", [P, 3], I32)
        out_ring = sb("out_ring", [P, 1], I32)
        cells = sb("cells", [1, 64], I32)
        run = sb("running", [1, 4])
        ms = sb("mean_sq", [P, 2, 3])
        rstd = sb("rstd", [P, 2, 3])
        pool_t = sb("pool_t", [P, 3])
        ms_m, rstd_m, pool_m = sb("mean_sq_m", [P, 2]), sb("rstd_m", [P, 2]), sb("pool_m", [P, 1])
        m_c, r_c, t_c = sb("m_c", [P, 3]), sb("r_c", [P, 3]), sb("t_c", [P, 3])
        m_qk, r_qk, t_qk = sb("m_qk", [P, 24]), sb("r_qk", [P, 2, 24]), sb("t_qk", [P, 24])
        st_v = sb("st_v", [P, 5, GROUPS])
        st_c = sb("st_c", [P, 5, GROUPS])
        m_e = sb("m_e", [P, 3])
        neg_max = sb("neg_max", [P, 2])
        denom = sb("denom", [P, TILES])
        rden = sb("rden", [P, 2])
        ident = sb("ident", [P, P])
        ident_b = sb("ident_b", [P, P], BF16)
        mask_b = sb("mask_b", [P, P], BF16)
        tri_b = sb("tri_b", [P, P], BF16)
        ones_b = sb("ones_b", [P, P], BF16)
        iota = sb("iota", [P, P])
        token = sb("token", [P, TILES, 2])
        padding = sb("padding", [P, 1])
        neg_half = sb("neg_half", [P, 24])
        eps_y = sb("eps_y", [P, 3])
        cos, sin = sb("cos", [P, TILES, HR]), sb("sin", [P, TILES, HR])
        pos_raw = sb("positions", [TILES, P], I32)
        hot_s = A[:, RS + 3072:RS + 3072 + 1024].bitcast(F16).rearrange("p (n s) -> p n s", n=2 * TILES)
        hot_b = A[:, RS + 4096:RS + 4096 + 384].bitcast(F16).rearrange("p (n b) -> p n b", n=2 * TILES)
        picked_b = A[:, RS + 4480:RS + 4480 + 128].bitcast(BF16).rearrange("p (t e) -> p t e", t=TILES)
        nb_col = A[:, RS + 4608:RS + 4608 + 64].bitcast(BF16)

        pos_loaded = sem("pos_loaded")
        h_loaded, w_in_loaded, small_loaded = sem("h_loaded"), sem("w_in_loaded"), sem("small_loaded")
        wo_loaded, ple_loaded = sem("wo_loaded"), sem("ple_loaded")
        qk_stored = [sem(f"qk_stored{u}") for u in range(2)]
        qk_loaded = [sem(f"qk_loaded{u}") for u in range(2)]
        m_stored = [sem(f"m_stored{u}") for u in range(2)]
        gu_loaded = [sem(f"gu_loaded{u}") for u in range(3)]
        dn_loaded = [sem(f"dn_loaded{u}") for u in range(3)]
        x_gathered = [sem(f"x_gathered{u}") for u in range(3)]
        y_stored = sem("y_stored")
        y_fetched = [sem(f"y_fetched{u}") for u in range(2)]
        p_loaded = [sem(f"p_loaded{u}") for u in range(2)]
        out_stored = sem("out_stored")
        h_final = sem("h_final")
        blocks_done = sem("blocks_done")

        S_pool0 = steps("const_pool", ["memsets", "selects"])
        S_vec0 = steps("const_vec", ["casts", "pos", "cols", "ang", "turns", "whole", "r_hi", "r_mid", "r_lo",
                                     "clamped", "neg", "abs", "cosarg"])
        S_pe0, S_act0 = steps("const_pe", ["pos_t"]), steps("const_act", ["sin", "cos"])
        FX, FM = Front(steps, "x"), Front(steps, "m")
        L_pool, L_pe = steps("l_pool", ["sgu_masked"]), steps("l_pe", ["prep_T"])
        L_act = steps("l_act", ["prep_evac"])
        L_vec = steps("l_vec", ["cin_zero", "gq_pe", "gq_nope"])
        Z_pe, ZS_pe = steps("z_pe", ["z_sgu", "z_glu", "z_mla"]), steps("zs_pe", ["s", "gluT"], credit=1)
        Z_act = steps("z_act", ["sgu_square", "sgu_tanh", "glu_tanh", "mla_copied"])
        ZC_act = steps("zc_act", ["cin_body", "cin_head"], credit=1)
        Z_vec = steps("z_vec", ["sgu_poly", "sgu_cubic", "sgu_gated", "glu"], credit=1)
        V_vec = steps("v_vec", ["v_sum", "v_mean", "v_centred", "v_squared", "v_sumsq", "v_scaled", "v_gained", "v_ready"], credit=1)
        Z_pool, ZS_vec = steps("z_pool", ["v_eps", "v_rstd"]), steps("zs_vec", ["s_biased", "y_sgu"], credit=1)
        CO_pe, CY_pe, CW_pe = steps("co_pe", ["coT"], credit=2), steps("cy_pe", ["ybT"], credit=2), steps("cw_pe", ["pw"], credit=3)
        C_act, C_pool = steps("c_act", ["c_tanh", "ybT_evac"], credit=3), steps("c_pool", ["c_eps", "c_rstd"], credit=2)
        taps = [f"tap{k}_{c}" for k in range(TAPS) for c in range(2)]
        CT_vec = steps("ct_vec", taps, credit=2)
        C_vec = steps("c_vec", ["c_sum", "c_mean", "c_centred", "c_squared", "c_sumsq", "c_scaled", "c_gained", "c_normed",
                                "c_silu"], credit=2)
        CY_vec = steps("cy_vec", ["y_conv"], credit=4)
        QC_act, QC_pool, QC_vec = steps("qc_act", ["squared"]), steps("qc_pool", ["eps", "rstd"]), steps("qc_vec", ["cn", "kpe"])
        QM_pe = steps("qm_pe", ["cT", "q_mm", "kv_mm"])
        QM_act = steps("qm_act", ["cnT", "squared", "v_stored"])
        QM_raw, QM_vec, QM_pool = steps("qm_raw", ["raw"]), steps("qm_vec", ["sumsq"]), steps("qm_pool", ["eps", "rstd"])
        Q_vec = steps("q_vec", ["q_nope", "k_nope", "q_pe", "q_gained", "pe_gained", "xc", "xs", "heads"], credit=1)
        R_pe = steps("r_pe", ["q_lo", "q_hi", "k_lo", "k_hi"], credit=2)
        R_act, R_vec = steps("r_act", ["q_lo", "k_lo"], credit=1), steps("r_vec", ["q_hi", "k_hi"], credit=1)
        tiles = range(TILES)
        S_pe, O_pe = steps("s_pe", [f"s{j}" for j in tiles]), steps("o_pe", [f"o{j}" for j in tiles])
        T_pe = steps("t_pe", [n for j in tiles for n in ([f"lo{j}"] + [f"hi{j}"] * (j >= 4))])
        X_act = steps("x_act", [f"exp{j}" for j in tiles], credit=1)
        X_max = steps("x_max", [f"max{j}" for j in tiles])
        X_lo, X_hi = steps("x_lo_t", [f"lo{j}" for j in tiles], credit=1), steps("x_hi_t", [f"hi{j}" for j in tiles if j >= 4], credit=1)
        X_fin = steps("x_fin", [n for j in tiles for n in (f"inv{j}", f"fin{j}")], credit=1)
        W_pe, W_vec = steps("w_pe", ["lo", "hi"]), steps("w_vec", ["lo", "hi"], credit=2)
        G_pe, G_vec = steps("g_pe", ["logits"], credit=1), steps("g_vec", ["logits"], credit=2)
        K_act, K_pe = steps("k_act", ["g_exp", "e_exp"]), steps("k_pe", ["ranks", "starts", "lists"])
        K_vec = steps("k_vec", [
            "g_max", "g_diff", "g_sum", "g_w", "g_miss", "g_cand", "g_first", "g_hot", "g_far", "e_in",
            "m1", "d1", "miss1", "cand1", "i1", "hot1", "rest", "m2", "d2", "miss2", "cand2", "i2", "hot2",
            "picked", "e_diff", "cnt_i", "cnt_up", "cnt_nb", "nb_f", "nb_col", "start_f", "row", "r1", "dest1",
            "r2", "dest2", "dest_i", "blk_i", "blk_f", "slot_f", "hots", "le", "owner", "active", "by_slot",
            "e_den", "e_rden", "w1", "w2", "before", "run_n", "run_slots", "empty", "rows_i",
            "list_i", "owner_i", "cells"])
        M_gu, M_xT, M_dn = steps("m_gu", ["gu"]), steps("m_xT", ["lo", "hi"]), steps("m_dn", ["lo", "hi"])
        M_hT = steps("m_hT", ["hT"])
        M_tanh, M_xlo = steps("m_tanh", ["tanh"]), steps("m_xlo", ["x"])
        M_ylo, M_h = steps("m_ylo", ["y"]), steps("m_h", ["h"])
        M_silu, M_prod = steps("m_silu", ["silu"]), steps("m_prod", ["prod"])
        M_xhi, M_yhi = steps("m_xhi", ["x"]), steps("m_yhi", ["y"])
        M_idx, M_oidx = steps("m_idx", ["idx"]), steps("m_oidx", ["idx"])
        E_comb = steps("e_comb", ["first", "second"], credit=1)
        E_pT_pe, E_pT_act = steps("e_pt_pe", ["pT"], credit=1), steps("e_pt_act", ["pT"])
        E_pe = steps("e_pe", ["e", "g_lo", "g_hi"], credit=1)
        E_act = steps("e_act", ["e_sq", "t_lo", "t_hi"], credit=1)
        E_pool = steps("e_pool", ["eps", "rstd"])
        E_vec = steps("e_vec", ["e_scaled", "gated"], credit=1)

        def guarded(eng, cond, fn):
            if cond is True:
                fn()
            else:
                with eng.If(cond):
                    fn()

        def lag_loop(eng, stages):
            ahead, behind = max(o for o, _ in stages), -min(o for o, _ in stages)

            def apart(t):
                for o, fn in stages:
                    if 0 <= t + o < TILES:
                        fn(t + o, (t + o) % 2, (t + o) // 2)

            for t in range(-ahead, 0):
                apart(t)
            with eng.Fori(0, PAIRS) as i:
                for v in range(2):
                    for o, fn in stages:
                        u, k = (v + o) % 2, (v + o) // 2
                        t = (2 * i + (v + o)).with_bounds(min_val=max(v + o, u), max_val=min(2 * PAIRS - 2 + v + o, TILES - 2 + u))
                        cond = True if k == 0 else (i < PAIRS - k if k > 0 else i > -k - 1)
                        guarded(eng, cond, lambda: fn(t, u, i + k))
            for t in range(TILES, TILES + behind):
                apart(t)

        def block_loop(eng, step):
            with eng.Fori(0, MAXB1 // 3) as i:
                for u in range(3):
                    b = 3 * i + (1 + u)
                    step(b, ((1 + u) % 3, i + (u == 2)), ((2 + u) % 3, i + (u >= 1)), (u, i))

        def settle(eng, passed):
            eng.sem_inc(passed, 1)

        def counters(eng, l, passed):
            eng.wait_ge(*K_vec.after(l, "cells"))
            settle(eng, passed)
            top = 2 * MAXB1
            prev = eng.value_load(cells[0:1, 48:49], min_val=0, max_val=top)
            n = eng.value_load(cells[0:1, 52:53], min_val=0, max_val=MAXB)
            used = [eng.value_load(cells[0:1, 49 + k:50 + k], min_val=0, max_val=top) for k in range(3)]
            return prev, n, used

        block = ctx.enter_context(nc.Block())

        @block.sync
        def _(sp):
            passed = sem("sp_passed")
            for u in range(2):
                sp.sem_inc(qk_stored[u], 32)
                sp.sem_inc(m_stored[u], 16)
            sp.dma_start(pos_raw[:, :], I["positions"][0].rearrange("(t p) -> t p", p=P)).then_inc(pos_loaded, 16)
            sp.dma_start(h[:, :, :], I["x"][0].rearrange("(t p) d -> p t d", p=P)).then_inc(h_loaded, 16)
            with sp.Fori(0, DEPTH) as l:
                sp.wait_ge(blocks_done, l)
                sp.dma_start(w_in, I["w_in"][l].rearrange("(k p) n -> p k n", p=P)).then_inc(w_in_loaded, 16)
                sp.wait_ge(h_final, TILES * l + TILES)
                small = [
                    (gains[:, MIX], I["mix_norm_g"]), (gains[:, BRANCH], I["branch_norm_g"]),
                    (gains[:, FFN], I["ffn_norm_g"]), (V["sgu_g"], I["sgu_ln_g"]), (V["sgu_b"], I["sgu_ln_b"]),
                    (V["cln_g"], I["conv_ln_g"]), (V["cln_b"], I["conv_ln_b"]), (V["pw_b"], I["conv_pw_b"]),
                    (V["qa_g"], I["q_a_norm_g"]), (V["kva_g"], I["kv_a_norm_g"]), (qg[:, :], I["q_norm_g"]),
                    (kg[:, :], I["k_norm_g"]), (b_r[:, 0:NG], I["router_group_b"]),
                    (b_r[:, NG:NG + NE], I["router_expert_b"]),
                ]
                for dst, src in small:
                    sp.dma_start(dst, src[l].partition_broadcast(P)).then_inc(small_loaded, 16)
                sp.dma_start(ws_raw[:, :, :], I["sgu_w"][l].rearrange("h i j -> i h j")).then_inc(small_loaded, 16)
                sp.dma_start(cw_raw[0:TAPS, :], I["conv_w"][l]).then_inc(small_loaded, 16)
                sp.dma_start(cw_raw[TAPS:TAPS + 1, :], I["conv_b"][l].partition_broadcast(1)).then_inc(small_loaded, 16)
                sp.dma_start(sb_raw[:, :], I["sgu_b"][l]).then_inc(small_loaded, 16)
                sp.dma_start(pw[:, :, :], I["conv_pw_w"][l].rearrange("(k p) n -> p k n", p=P)).then_inc(small_loaded, 16)
                with nc.allow_non_contiguous_dma(reason="short rows of the router"):
                    sp.dma_start(w_r[:, :, 0:NG], I["router_group_w"][l].rearrange("(k p) n -> p k n", p=P)).then_inc(small_loaded, 16)
                    sp.dma_start(w_r[:, :, NG:NG + NE], I["router_expert_w"][l].rearrange("(k p) n -> p k n", p=P)).then_inc(small_loaded, 16)
                sp.dma_start(w_uq, I["w_uq"][l].rearrange("(k p) n -> p k n", p=P)).then_inc(small_loaded, 16)
                sp.dma_start(w_ukv, I["w_ukv"][l]).then_inc(small_loaded, 16)

                with sp.Fori(0, PAIRS) as i:
                    for u in range(2):
                        g = TILES * l + 2 * i + u
                        sp.wait_ge(*R_act.after(g))
                        sp.wait_ge(*R_vec.after(g))
                        for s in range(2):
                            sp.dma_start(qk_dram[s][:, :, bass.ds((2 * i + u) * P, P)], stage[u][0:QK, s]).then_inc(qk_stored[u], 16)
                for u in range(2):
                    sp.wait_ge(qk_stored[u], 32 * PAIRS * l + (32 * PAIRS + 32))
                    settle(sp, passed)

                def load_head(head, u):
                    sp.dma_start(q_ring[u][0:QK], qk_dram[0][:, head, :]).then_inc(qk_loaded[u], 16)
                    sp.dma_start(k_ring[u][0:QK], qk_dram[1][:, head, :]).then_inc(qk_loaded[u], 16)

                load_head(0, 0)
                load_head(1, 1)
                sp.dma_start(w_o, I["w_o"][l].rearrange("(k p) n -> p k n", p=P)).then_inc(wo_loaded, 16)
                with sp.Fori(0, HEADS // 2 - 1) as i:
                    for u in range(2):
                        sp.wait_ge(*S_pe.after(HEADS * l + 2 * i + u))
                        load_head(2 * i + (2 + u), u)
                with sp.Fori(0, PAIRS) as i:
                    for u in range(2):
                        sp.wait_ge(*FM.a.after(TILES * l + 2 * i + u))
                        sp.dma_start(m_dram[bass.ds((2 * i + u) * P, P), :], m_buf[u]).then_inc(m_stored[u], 16)

                sp.wait_ge(*W_pe.before(TILES * l + TILES))
                sp.dma_start(ple_g, I["ple_gate_w"][l].rearrange("(k p) n -> p k n", p=P)).then_inc(ple_loaded, 16)
                sp.dma_start(ple_p, I["ple_proj_w"][l].rearrange("(k p) n -> p k n", p=P)).then_inc(ple_loaded, 16)
                sp.dma_start(gains[:, BRANCH], I["ple_post_norm_g"][l].partition_broadcast(P)).then_inc(ple_loaded, 16)
                sp.dma_start(gains[:, MIX], I["ple_norm_g"][l].partition_broadcast(P)).then_inc(ple_loaded, 16)
                for u in range(2):
                    sp.wait_ge(m_stored[u], 16 * PAIRS * l + (16 * PAIRS + 16))
                settle(sp, passed)
                prev, n, used = counters(sp, l, passed)

                def load_gu(b, s):
                    e = sp.value_load(cells[0:1, bass.ds(b, 1)] if not isinstance(b, int) else cells[0:1, b:b + 1], min_val=0, max_val=NE - 1)
                    sp.dma_start(w_gu[s][:, :, 0:F], I["moe_w_gate"][l, e].rearrange("(k p) f -> p k f", p=P)).then_inc(gu_loaded[s], 16)
                    sp.dma_start(w_gu[s][:, :, F:2 * F], I["moe_w_up"][l, e].rearrange("(k p) f -> p k f", p=P)).then_inc(gu_loaded[s], 16)
                    return e

                def load_dn(e, s):
                    sp.dma_start(w_dn[s], I["moe_w_down"][l, e].rearrange("(k p) f -> p k f", p=P)).then_inc(dn_loaded[s], 16)

                for b in range(3):
                    load_dn(load_gu(b, b), b)

                def weights(b, here, nxt, last):
                    def go():
                        sp.wait_ge(*M_gu.after(prev + b - 1))
                        e = load_gu(b + 2, last[0])
                        sp.wait_ge(*M_dn.after(prev + b - 1))
                        load_dn(e, last[0])
                    guarded(sp, b + 2 < n, go)

                block_loop(sp, weights)

            with sp.Fori(0, TILES) as t:
                sp.wait_ge(h_final, TILES * DEPTH + t + 1)
                sp.dma_start(out[0, bass.ds(t * P, P), :], h[:, t, :]).then_inc(out_stored, 16)
            sp.wait_ge(out_stored, 16 * TILES)

        N_SMALL = 16 * 23

        @block.gpsimd
        def _(gp):
            passed = sem("gp_passed")
            for s in (C_pool, FX.pool, FM.pool):
                gp.sem_inc(s.sem, s.per * s.credit)
            for ap, val in ((ident, 0.0), (tri_b, 0.0), (mask_b, 0.0), (ones_b, 1.0), (neg_half, -0.5)):
                nc.gpsimd.memset(ap[:, :], val)
            nc.gpsimd.memset(eps_y[:, 0:1], 4 * EPS)
            nc.gpsimd.memset(eps_y[:, 1:3], EPS)
            nc.gpsimd.iota(iota[:, :], pattern=[[1, P]], base=0, channel_multiplier=0, allow_small_or_imprecise_dtypes=True)
            nc.gpsimd.iota(padding[:, :], pattern=[[1, 1]], base=2 * SEQ + 1, channel_multiplier=1,
                           allow_small_or_imprecise_dtypes=True)
            nc.gpsimd.iota(token[:, :, :], pattern=[[P, TILES], [SEQ, 2]], base=1, channel_multiplier=1,
                           allow_small_or_imprecise_dtypes=True).then_inc(*S_pool0.next("memsets"))
            gp.wait_ge(*S_pool0.after(0, "memsets"))
            nc.gpsimd.affine_select(out=ident[:, :], in_=ident[:, :], pattern=[[-1, P]], compare_op=ALU.not_equal,
                                    fill=1.0, base=0, channel_multiplier=1)
            nc.gpsimd.affine_select(out=tri_b[:, :], in_=tri_b[:, :], pattern=[[-1, P]], compare_op=ALU.is_ge,
                                    fill=1.0, base=0, channel_multiplier=1)
            nc.gpsimd.affine_select(out=mask_b[:, :], in_=mask_b[:, :], pattern=[[-1, P]], compare_op=ALU.is_ge,
                                    fill=-BIG, base=0, channel_multiplier=1).then_inc(*S_pool0.next("selects"))

            def rsqrt(dst, tmp, src, n, eps, own, index, first, second, mul=1.0):
                gp.wait_ge(*own.before(index))
                settle(gp, passed)
                if isinstance(eps, float):
                    i = nc.gpsimd.tensor_scalar(tmp, src, mul, eps, ALU.mult, ALU.add)
                else:
                    i = nc.gpsimd.tensor_tensor(tmp, src, eps, ALU.add)
                i.then_inc(*own.next(first))
                gp.wait_ge(*own.after(index, first))
                nc.gpsimd.tensor_tensor(dst, tmp, neg_half[:, 0:n], ALU.pow).then_inc(*own.next(second))

            with gp.Fori(0, DEPTH) as l:
                gp.wait_ge(small_loaded, N_SMALL * l + N_SMALL)
                settle(gp, passed)
                nc.gpsimd.affine_select(out=ws_raw[:, :, :], in_=ws_raw[:, :, :], pattern=[[0, GROUPS], [-1, P]],
                                        compare_op=ALU.is_ge, fill=0.0, base=0,
                                        channel_multiplier=1).then_inc(*L_pool.next("sgu_masked"))

                def norm(ph):
                    def go(t, u, i):
                        r = 24 * l + t + 8 * ph
                        n = 3 if ph == 1 else 1
                        gp.wait_ge(*FX.square.after(r))
                        rsqrt(rstd[:, u, 0:n], pool_t[:, 0:n], ms[:, u, 0:n], n, eps_y[:, 0:3] if ph == 1 else EPS,
                              FX.pool, r, "eps", "rstd")
                    return go

                def norm_m(t, u, i):
                    g = TILES * l + t
                    gp.wait_ge(*FM.square.after(g))
                    rsqrt(rstd_m[:, u:u + 1], pool_m[:, 0:1], ms_m[:, u:u + 1], 1, EPS, FM.pool, g, "eps", "rstd")

                def sgu_rstd(t, u, i):
                    g = TILES * l + t
                    gp.wait_ge(*V_vec.after(g, "v_sumsq"))
                    rsqrt(st_v[:, 4, :], st_v[:, 3, :], st_v[:, 2, :], GROUPS, 4 * EPS, Z_pool, g, "v_eps", "v_rstd", 1.0 / HEAD)

                def conv_rstd(t, u, i):
                    g = TILES * l + t
                    gp.wait_ge(*C_vec.after(g, "c_sumsq"))
                    rsqrt(st_c[:, 4, :], st_c[:, 3, :], st_c[:, 2, :], GROUPS, EPS, C_pool, g, "c_eps", "c_rstd", 1.0 / HEAD)

                lag_loop(gp, [(-2, conv_rstd), (2, norm(0)), (0, sgu_rstd)])

                def c_rstd(t, u, i):
                    g = TILES * l + t
                    gp.wait_ge(*QC_act.after(g))
                    gp.wait_ge(*QC_vec.before(g))
                    rsqrt(r_c[:, :], t_c[:, :], m_c[:, :], 3, EPS, QC_pool, g, "eps", "rstd")

                def qk_rstd(t, u, i):
                    g = TILES * l + t
                    gp.wait_ge(*QM_vec.after(g))
                    rsqrt(r_qk[:, u, :], t_qk[:, :], m_qk[:, :], 24, EPS, QM_pool, g, "eps", "rstd")

                lag_loop(gp, [(2, c_rstd), (1, qk_rstd)])

                lag_loop(gp, [(-1, norm_m), (2, norm(1))])

                prev, n, used = counters(gp, l, passed)
                for u in range(2):
                    gp.wait_ge(m_stored[u], 16 * PAIRS * l + (16 * PAIRS + 16))
                    settle(gp, passed)

                def gather(b, s, m):
                    col = idx[:, b:b + 1] if isinstance(b, int) else idx[:, bass.ds(b, 1)]
                    nc.gpsimd.tensor_copy(idx_ring[:, s:s + 1], col).then_inc(*M_idx.next("idx"))
                    gp.wait_ge(*M_idx.after(m))
                    settle(gp, passed)
                    nc.gpsimd.indirect_dma_start(
                        out=x_blk[s], out_offset=None, in_=m_dram,
                        in_offset=bass.IndirectOffsetOnAxis(ap=idx_ring[:, s:s + 1], axis=0)).then_inc(x_gathered[s], 16)

                gather(0, 0, prev)
                gather(1, 1, prev + 1)
                gather(2, 2, prev + 2)

                def rows(b, here, nxt, last):
                    def ahead():
                        gp.wait_ge(*M_xT.after(prev + b - 1))
                        settle(gp, passed)
                        gather(b + 2, last[0], prev + b + 2)

                    def store():
                        gp.wait_ge(*M_ylo.after(prev + b - 1))
                        gp.wait_ge(*M_yhi.after(prev + b - 1))
                        settle(gp, passed)
                        nc.gpsimd.tensor_copy(out_ring[:, :], out_idx[:, bass.ds(b - 1, 1)]).then_inc(*M_oidx.next("idx"))
                        gp.wait_ge(*M_oidx.after(prev + b - 1))
                        settle(gp, passed)
                        nc.gpsimd.indirect_dma_start(
                            out=y_rows, out_offset=bass.IndirectOffsetOnAxis(ap=out_ring[:, 0:1], axis=0),
                            in_=y_blk, in_offset=None).then_inc(y_stored, 16)
                    guarded(gp, b + 2 < n, ahead)
                    guarded(gp, b <= n, store)

                block_loop(gp, rows)
                gp.wait_ge(y_stored, (prev + n) * 16)
                settle(gp, passed)

                def rows_of(src, t, base=0):
                    return src[t * P + base:(t + 1) * P + base, :] if isinstance(t, int) else src[bass.ds(t * P + base, P), :]

                def fetch(t, u, i):
                    gp.wait_ge(*E_comb.after(TILES * l + t - 2))
                    settle(gp, passed)
                    for k in range(2):
                        gp.dma_start(y_got[u][k], rows_of(y_rows, t, k * SEQ)).then_inc(y_fetched[u], 16)

                def fetch_p(t, u, i):
                    gp.wait_ge(*E_pT_pe.after(TILES * l + t - 2))
                    settle(gp, passed)
                    gp.dma_start(p_tile[u], rows_of(I["p"][l, 0], t)).then_inc(p_loaded[u], 16)

                def ple_rstd(t, u, i):
                    g = TILES * l + t
                    gp.wait_ge(*E_act.after(g, "e_sq"))
                    rsqrt(m_e[:, 2:3], m_e[:, 1:2], m_e[:, 0:1], 1, 4 * EPS, E_pool, g, "eps", "rstd")

                lag_loop(gp, [(3, fetch), (2, fetch_p), (2, norm(2)), (0, ple_rstd)])

        @block.scalar
        def _(act):
            passed = sem("act_passed")
            for s in (X_act, X_hi, E_act, ZC_act, C_act, R_act, FX.lo, FM.lo, FX.square, FM.square):
                act.sem_inc(s.sem, s.per * s.credit)
            act.wait_ge(*S_vec0.after(0, "cosarg"))
            nc.scalar.activation(sin[:, :, :], sin[:, :, :], ACT.Sin).then_inc(*S_act0.next("sin"))
            nc.scalar.activation(cos[:, :, :], cos[:, :, :], ACT.Sin).then_inc(*S_act0.next("cos"))

            with act.Fori(0, DEPTH) as l:
                act.wait_ge(*L_pe.after(l))
                nc.scalar.copy(wsT[:, :, :], bank(7).rearrange("p (h i) -> p h i", h=GROUPS))
                nc.scalar.activation(cw[:, :, 0:TAPS], bank(6, 0, 64).rearrange("p (c k) -> p c k", c=2)[:, :, 0:TAPS],
                                     ACT.Copy, scale=0.5)
                nc.scalar.copy(cw[:, :, TAPS:32], bank(6, 0, 64).rearrange("p (c k) -> p c k", c=2)[:, :, TAPS:32])
                nc.scalar.copy(s_bias[:, :], bank(6, 64, 64 + GROUPS)).then_inc(*L_act.next("prep_evac"))

                def norm(ph):
                    def go(t, u, i):
                        g = TILES * l + t
                        if ph == 0:
                            act.wait_ge(h_final, g + 1)
                        elif ph == 2:
                            act.wait_ge(*E_comb.after(g))
                        act.wait_ge(*FX.square.before(24 * l + t + 8 * ph))
                        if ph == 1:
                            for k, (a, b) in enumerate(((0, 256), (256, 512), (512, 1024))):
                                i = nc.scalar.activation(junk[:, a:b], y[:, t, a:b], ACT.Square, scale=float(b - a) ** -0.5,
                                                         accum_out=ms[:, u, k:k + 1])
                        else:
                            i = nc.scalar.activation(junk[:, :], h[:, t, :], ACT.Square, scale=float(D) ** -0.5,
                                                     accum_out=ms[:, u, 0:1])
                        i.then_inc(*FX.square.next("squared"))
                    return go

                def norm_m(t, u, i):
                    act.wait_ge(*W_vec.after(TILES * l + t))
                    act.wait_ge(*FM.square.before(TILES * l + t))
                    nc.scalar.activation(junk_m, h[:, t, :], ACT.Square, scale=float(D) ** -0.5,
                                         accum_out=ms_m[:, u:u + 1]).then_inc(*FM.square.next("squared"))

                def turn(ph):
                    def go(t, u, i):
                        act.wait_ge(*FX.pe.after(24 * l + t + 8 * ph, "T_lo"))
                        nc.scalar.copy(aT[u][:, 0:4, :].rearrange("p a b -> p (a b)"), bank(0)).then_inc(*FX.lo.next("aT"))
                    return go

                def turn_m(t, u, i):
                    act.wait_ge(*FM.pe.after(TILES * l + t, "T_lo"))
                    nc.scalar.copy(mT[:, 0:4, :].rearrange("p a b -> p (a b)"), bank(6)).then_inc(*FM.lo.next("aT"))

                def z_square(t, u, i):
                    act.wait_ge(*Z_pe.after(TILES * l + t, "z_sgu"))
                    nc.scalar.activation(sg_t, bank(2), ACT.Square).then_inc(*Z_act.next("sgu_square"))

                def z_tanh(t, u, i):
                    g = TILES * l + t
                    act.wait_ge(*Z_vec.after(g, "sgu_cubic"))
                    nc.scalar.activation(sg_t, sg_t, ACT.Tanh, scale=GELU_C).then_inc(*Z_act.next("sgu_tanh"))
                    act.wait_ge(*Z_pe.after(g, "z_glu"))
                    nc.scalar.activation(gl_t, bank(3, SGU, 2 * SGU), ACT.Tanh, scale=0.5).then_inc(*Z_act.next("glu_tanh"))

                def z_mla(t, u, i):
                    act.wait_ge(*Z_pe.after(TILES * l + t, "z_mla"))
                    nc.scalar.copy(zc[:, t, :], bank(4, 0, MLA_IN)).then_inc(*Z_act.next("mla_copied"))

                def c_tanh(t, u, i):
                    act.wait_ge(*C_vec.after(TILES * l + t, "c_normed"))
                    nc.scalar.activation(c_th, c_n.rearrange("p a b -> p (a b)"), ACT.Tanh, scale=0.5).then_inc(*C_act.next("c_tanh"))

                def z_cin(t, u, i):
                    g = TILES * l + t
                    gt = bank(6, 0, 2 * P).rearrange("p (c s) -> p c s", c=2)
                    act.wait_ge(*ZS_pe.after(g, "gluT"))
                    nc.scalar.copy(cin[u][:, :, TAPS - 1:], gt).then_inc(*ZC_act.next("cin_body"))
                    act.wait_ge(*CT_vec.after(g - 1))
                    nc.scalar.copy(cin[1 - u][:, :, 0:TAPS - 1], gt[:, :, P - TAPS + 1:]).then_inc(*ZC_act.next("cin_head"))

                def c_yT_evac(t, u, i):
                    act.wait_ge(*CY_pe.after(TILES * l + t, "ybT"))
                    nc.scalar.copy(c_yT.rearrange("p a b -> p (a b)"), bank(7, 2 * P, 4 * P)).then_inc(*C_act.next("ybT_evac"))

                lag_loop(act, [(1, turn(0)), (-1, z_cin), (2, norm(0)), (0, z_square), (-2, c_tanh), (0, z_tanh), (0, z_mla),
                               (-2, c_yT_evac)])

                def heads_view(b, lo, hi, width):
                    return ps[:, b:b + 2, 0:HC * width].rearrange("p a (h d) -> p a h d", h=HC)[:, :, :, lo:hi]

                def fold(ap):
                    return ap.rearrange("p (a h) d -> p a h d", a=2)

                act.wait_ge(*Z_act.before(TILES * l + TILES))
                settle(act, passed)

                def c_square(t, u, i):
                    g = TILES * l + t
                    act.wait_ge(*QC_act.before(g))
                    act.wait_ge(*QC_pool.before(g))
                    c0 = 0
                    for k, n in enumerate((QR, KVR, ROPE)):
                        ins = nc.scalar.activation(junk[:, c0:c0 + n], zc[:, t, c0:c0 + n], ACT.Square, scale=float(n) ** -0.5,
                                                   accum_out=m_c[:, k:k + 1])
                        c0 += n
                    ins.then_inc(*QC_act.next("squared"))

                def q_main(t, u, i):
                    g = TILES * l + t
                    act.wait_ge(*QM_pe.after(g, "cT"))
                    nc.scalar.copy(cnT.rearrange("p a b -> p (a b)"), bank(6, 0, 3 * P)).then_inc(*QM_act.next("cnT"))
                    act.wait_ge(*QM_vec.before(g))
                    act.wait_ge(*QM_pe.after(g, "q_mm"))
                    nc.scalar.activation(fold(qk_sq)[:, :, :, 0:HEAD], heads_view(2, 0, HEAD, QK), ACT.Square, scale=float(HEAD) ** -0.5)
                    nc.scalar.activation(fold(qk_sq)[:, :, :, HEAD:QK], heads_view(2, HEAD, QK, QK), ACT.Square, scale=float(ROPE) ** -0.5)
                    act.wait_ge(*QM_pe.after(g, "kv_mm"))
                    nc.scalar.activation(fold(k_sq), heads_view(4, 0, HEAD, P), ACT.Square,
                                         scale=float(HEAD) ** -0.5).then_inc(*QM_act.next("squared"))
                    nc.scalar.copy(vals[:, t].rearrange("p (a h) d -> p a h d", a=2),
                                   heads_view(4, HEAD, P, P)).then_inc(*QM_act.next("v_stored"))

                def q_raw(t, u, i):
                    act.wait_ge(*R_pe.after(TILES * l + t - 2))
                    settle(act, passed)
                    nc.scalar.copy(fold(qs[u]), heads_view(2, 0, QK, QK))
                    nc.scalar.copy(fold(ks[u])[:, :, :, 0:HEAD], heads_view(4, 0, HEAD, P)).then_inc(*QM_raw.next("raw"))

                def q_turned(t, u, i):
                    g = TILES * l + t
                    act.wait_ge(qk_stored[u], 32 * (PAIRS * l + i) + 32)
                    act.wait_ge(*R_pe.after(g, "q_lo"))
                    nc.scalar.copy(stage[u][0:QK, 0, 0:HC].rearrange("p a b -> p (a b)"), ps[0:QK, 0, :]).then_inc(*R_act.next("q_lo"))
                    act.wait_ge(*R_pe.after(g, "k_lo"))
                    nc.scalar.copy(stage[u][0:QK, 1, 0:HC].rearrange("p a b -> p (a b)"), ps[0:QK, 7, :]).then_inc(*R_act.next("k_lo"))

                lag_loop(act, [(2, c_square), (1, q_main), (-1, q_turned), (1, q_raw)])

                def prob_hi(hh, j):
                    if j >= 4:
                        act.wait_ge(*T_pe.after(hh, f"hi{j}"))
                        nc.scalar.copy(prob_t[j % 2][:, 4:j + 1], bank(5, 0, (j - 3) * P).rearrange("p (k q) -> p k q", q=P)
                                       ).then_inc(*X_hi.next(f"hi{j}"))

                def exps(hh, j):
                    n = (j + 1) * P
                    act.wait_ge(*X_max.after(hh, f"max{j}"))
                    nc.scalar.activation(prob[j % 2][:, 0:n], banks(2 * (j % 2))[:, 0:n], ACT.Exp, bias=neg_max[:, j % 2:j % 2 + 1],
                                         accum_out=denom[:, j:j + 1]).then_inc(*X_act.next(f"exp{j}"))

                with act.Fori(0, HEADS // 2) as i:
                    for n in range(2 * TILES):
                        u, j = divmod(n, TILES)
                        if n:
                            prob_hi(HEADS * l + 2 * i + (n - 1) // TILES, (n - 1) % TILES)
                        exps(HEADS * l + 2 * i + u, j)
                    prob_hi(HEADS * l + 2 * i + 1, TILES - 1)

                act.wait_ge(*X_fin.before(HEADS * l + HEADS))
                settle(act, passed)
                lag_loop(act, [(-1, norm_m), (2, norm(1)), (1, turn(1)), (-1, turn_m)])
                act.wait_ge(*K_vec.after(l, "g_diff"))
                nc.scalar.activation(rs(1, TILES, NG), rs(0, TILES, NG), ACT.Exp).then_inc(*K_act.next("g_exp"))
                act.wait_ge(*K_vec.after(l, "e_diff"))
                nc.scalar.activation(rs(9, 2, TILES)[:, 1], rs(9, 2, TILES)[:, 0], ACT.Exp).then_inc(*K_act.next("e_exp"))

                prev, n, used = counters(act, l, passed)

                def x_lo(m):
                    act.wait_ge(*M_xT.after(m, "lo"))
                    nc.scalar.copy(xT[:, 0:4].rearrange("p a b -> p (a b)"), bank(0)).then_inc(*M_xlo.next("x"))

                def tanh(m):
                    act.wait_ge(*M_gu.after(m))
                    nc.scalar.activation(hid_g, bank(2, 0, F), ACT.Tanh, scale=0.5).then_inc(*M_tanh.next("tanh"))

                def h_evac(m):
                    act.wait_ge(*M_hT.after(m))
                    nc.scalar.copy(hid_t.rearrange("p a b -> p (a b)"), bank(3, 0, 2 * P)).then_inc(*M_h.next("h"))

                def y_lo(m):
                    act.wait_ge(y_stored, m * 16)
                    act.wait_ge(*M_dn.after(m, "lo"))
                    nc.scalar.copy(y_blk[:, 0:512], bank(4)).then_inc(*M_ylo.next("y"))

                x_lo(prev)
                tanh(prev)
                x_lo(prev + 1)
                h_evac(prev)

                def expert(b, here, nxt, last):
                    m = prev + b
                    guarded(act, b < n, lambda: tanh(m))
                    guarded(act, b + 1 < n, lambda: x_lo(m + 1))
                    guarded(act, b <= n, lambda: y_lo(m - 1))
                    guarded(act, b < n, lambda: h_evac(m))

                block_loop(act, expert)

                def turn_p(t, u, i):
                    act.wait_ge(*E_pT_pe.after(TILES * l + t))
                    nc.scalar.copy(pT[u].rearrange("p a b -> p (a b)"), bank(6, 0, 2 * P)).then_inc(*E_pT_act.next("pT"))

                def ple_main(t, u, i):
                    g = TILES * l + t
                    act.wait_ge(*E_pe.after(g, "e"))
                    act.wait_ge(*E_act.before(g))
                    nc.scalar.activation(junk_e, banks(4), ACT.Square, scale=2 * float(D) ** -0.5,
                                         accum_out=m_e[:, 0:1]).then_inc(*E_act.next("e_sq"))
                    act.wait_ge(*E_vec.before(g))
                    act.wait_ge(*E_pe.after(g, "g_lo"))
                    nc.scalar.activation(gate_t[:, 0:512], bank(2), ACT.Tanh, scale=0.5).then_inc(*E_act.next("t_lo"))
                    act.wait_ge(*E_pe.after(g, "g_hi"))
                    nc.scalar.activation(gate_t[:, 512:1024], bank(3), ACT.Tanh, scale=0.5).then_inc(*E_act.next("t_hi"))

                lag_loop(act, [(2, norm(2)), (1, turn(2)), (1, turn_p), (0, ple_main)])

        @block.vector
        def _(v):
            passed = sem("v_passed")
            for s in (X_lo, X_fin, W_vec, G_vec, E_comb, E_vec, Z_vec, V_vec, ZS_vec, CT_vec, C_vec, CY_vec, Q_vec, R_vec, FX.hi, FM.hi, FX.a, FM.a):
                v.sem_inc(s.sem, s.per * s.credit)

            def wide(ap, axis, *shape):
                return ap.unsqueeze(axis).to_broadcast([P, *shape])

            def link0(ins, name):
                ins.then_inc(*S_vec0.next(name))
                v.wait_ge(*S_vec0.after(0, name))

            ang, turns = at(B, T0, TILES, HR), at(B, T0 + 128, TILES, HR)
            freq, pos_cols, pos_f = at(B, T0 + 256, HR), at(B, T0 + 272, TILES), at(B, T0 + 280, P)[0:TILES]
            inv_freq = (ROPE_THETA ** (-np.arange(0, ROPE, 2, dtype=np.float64) / ROPE)).astype(np.float32)
            v.memset(run[:, :], 0.0)
            for k in range(HR):
                v.memset(freq[:, k:k + 1], float(inv_freq[k]))
            v.wait_ge(*S_pool0.after(0, "selects"))
            link0(v.tensor_copy(ident_b[:, :], ident[:, :]), "casts")
            v.wait_ge(pos_loaded, 16)
            v.tensor_copy(pos_f, pos_raw[:, :]).then_inc(*S_vec0.next("pos"))
            v.wait_ge(*S_pe0.after(0))
            link0(v.tensor_copy(pos_cols, bank(0, 0, TILES)), "cols")
            link0(v.tensor_tensor(ang, wide(pos_cols, 2, TILES, HR), wide(freq, 1, TILES, HR), ALU.mult), "ang")
            link0(v.tensor_scalar(turns, ang, 1 / (2 * np.pi), ROUND, ALU.mult, ALU.add), "turns")
            link0(v.tensor_scalar(turns, turns, ROUND, None, ALU.subtract), "whole")
            link0(v.scalar_tensor_tensor(ang, turns, -TWO_PI_HI, ang, ALU.mult, ALU.add), "r_hi")
            link0(v.scalar_tensor_tensor(ang, turns, -TWO_PI_MID, ang, ALU.mult, ALU.add), "r_mid")
            link0(v.scalar_tensor_tensor(ang, turns, -TWO_PI_LO, ang, ALU.mult, ALU.add), "r_lo")
            link0(v.tensor_scalar(sin[:, :, :], ang, 3.1415925, -3.1415925, ALU.min, ALU.max), "clamped")
            link0(v.tensor_scalar(cos[:, :, :], sin[:, :, :], -1.0, None, ALU.mult), "neg")
            link0(v.tensor_tensor(cos[:, :, :], cos[:, :, :], sin[:, :, :], ALU.max), "abs")
            v.tensor_scalar(cos[:, :, :], cos[:, :, :], -1.0, np.pi / 2, ALU.mult, ALU.add).then_inc(*S_vec0.next("cosarg"))
            v.wait_ge(h_loaded, 16)
            v.sem_inc(h_final, TILES)

            with v.Fori(0, DEPTH) as l:
                v.wait_ge(small_loaded, N_SMALL * l + N_SMALL)
                v.memset(cin[0][:, :, 0:TAPS - 1], 0.0).then_inc(*L_vec.next("cin_zero"))
                v.tensor_scalar(gq[:, HEAD:QK], qg[:, HEAD:QK], SCALE, None, ALU.mult).then_inc(*L_vec.next("gq_pe"))
                v.scalar_tensor_tensor(gq[:, 0:HEAD], qg[:, 0:HEAD], SCALE, kg[:, 0:HEAD], ALU.mult,
                                       ALU.mult).then_inc(*L_vec.next("gq_nope"))
                v.wait_ge(*L_vec.after(l))
                v.wait_ge(*L_act.after(l))

                def norm(ph):
                    def go(t, u, i):
                        r = 24 * l + t + 8 * ph
                        v.wait_ge(*FX.pool.after(r, "rstd"))
                        cuts = (0, 256, 512, 1024) if ph == 1 else (0, D)
                        src = y if ph == 1 else h
                        for k, (a, b) in enumerate(zip(cuts, cuts[1:])):
                            ins = v.scalar_tensor_tensor(a_buf[u][:, a:b], src[:, t, a:b], rstd[:, u, k:k + 1],
                                                         gains[:, BRANCH if ph == 1 else MIX, a:b], ALU.mult, ALU.mult)
                        ins.then_inc(*FX.a.next("a"))
                    return go

                def norm_m(t, u, i):
                    v.wait_ge(*FM.pool.after(TILES * l + t, "rstd"))
                    v.wait_ge(m_stored[u], 16 * (PAIRS * l + i) + 16)
                    v.scalar_tensor_tensor(m_buf[u], h[:, t, :], rstd_m[:, u:u + 1], gains[:, FFN], ALU.mult,
                                           ALU.mult).then_inc(*FM.a.next("a"))

                def turn(ph):
                    def go(t, u, i):
                        v.wait_ge(*FX.pe.after(24 * l + t + 8 * ph, "T_hi"))
                        v.tensor_copy(aT[u][:, 4:8, :].rearrange("p a b -> p (a b)"), bank(1)).then_inc(*FX.hi.next("aT"))
                    return go

                def turn_m(t, u, i):
                    v.wait_ge(*FM.pe.after(TILES * l + t, "T_hi"))
                    v.tensor_copy(mT[:, 4:8, :].rearrange("p a b -> p (a b)"), bank(7)).then_inc(*FM.hi.next("aT"))

                def conv(t, u, i):
                    q = TILES * l + t
                    v.wait_ge(*ZC_act.after(q, "cin_body"))
                    for k in range(TAPS):
                        for c in range(2):
                            src = cin[u][:, c, k:k + P]
                            if k:
                                v.wait_ge(*CT_vec.after(q, f"tap{k - 1}_{c}"))
                                ins = v.scalar_tensor_tensor(acc[:, c, :], src, cw[:, c, k:k + 1], acc[:, c, :], ALU.mult, ALU.add)
                            else:
                                ins = v.tensor_scalar(acc[:, c, :], src, cw[:, c, 0:1], cw[:, c, TAPS:TAPS + 1], ALU.mult, ALU.add)
                            ins.then_inc(*CT_vec.next(f"tap{k}_{c}"))

                def gelu_cubic(t, u, i):
                    g = TILES * l + t

                    def link(ins, name):
                        ins.then_inc(*Z_vec.next(name))
                        v.wait_ge(*Z_vec.after(g, name))

                    v.wait_ge(*Z_act.after(g, "sgu_square"))
                    link(v.tensor_scalar(sg_t, sg_t, GELU_A, 1.0, ALU.mult, ALU.add), "sgu_poly")
                    v.tensor_tensor(sg_t, sg_t, bank(2), ALU.mult).then_inc(*Z_vec.next("sgu_cubic"))

                def gelu_glu(t, u, i):
                    g = TILES * l + t
                    v.wait_ge(*Z_act.after(g, "sgu_tanh"))
                    v.scalar_tensor_tensor(sg_uv, sg_t, 1.0, bank(2), ALU.add, ALU.mult).then_inc(*Z_vec.next("sgu_gated"))
                    v.wait_ge(*Z_act.after(g, "glu_tanh"))
                    v.scalar_tensor_tensor(gl, gl_t, 1.0, bank(3, 0, SGU), ALU.add, ALU.mult).then_inc(*Z_vec.next("glu"))

                def centre(src, st, centred, squared, link, p):
                    link(v.tensor_reduce(st[:, 0, :], src, AX.X, ALU.add), p + "_sum")
                    link(v.tensor_scalar(st[:, 1, :], st[:, 0, :], 1.0 / HEAD, None, ALU.mult), p + "_mean")
                    link(v.tensor_tensor(centred, src, wide(st[:, 1, :], 2, GROUPS, HEAD), ALU.subtract), p + "_centred")
                    link(v.tensor_tensor(squared, centred, centred, ALU.mult), p + "_squared")
                    v.tensor_reduce(st[:, 2, :], squared, AX.X, ALU.add).then_inc(*{"v": V_vec, "c": C_vec}[p].next(p + "_sumsq"))

                def scaled(st, centred, dst, gain, bias, link, p, last):
                    link(v.tensor_tensor(dst, centred, wide(st[:, 4, :], 2, GROUPS, HEAD), ALU.mult), p + "_scaled")
                    flat = dst.rearrange("p a b -> p (a b)")
                    link(v.tensor_tensor(flat, flat, V[gain], ALU.mult), p + "_gained")
                    v.tensor_tensor(flat, flat, V[bias], ALU.add).then_inc(*{"v": V_vec, "c": C_vec}[p].next(last))

                def link_c(q):
                    def link(ins, name):
                        ins.then_inc(*C_vec.next(name))
                        v.wait_ge(*C_vec.after(q, name))
                    return link

                def link_v(g):
                    def link(ins, name):
                        ins.then_inc(*V_vec.next(name))
                        v.wait_ge(*V_vec.after(g, name))
                    return link

                def conv_centre(t, u, i):
                    q = TILES * l + t
                    v.wait_ge(*CO_pe.after(q, "coT"))
                    centre(bank(7, 0, 256).rearrange("p (a b) -> p a b", a=GROUPS), st_c, c_c, c_sq, link_c(q), "c")

                def conv_scale(t, u, i):
                    q = TILES * l + t
                    v.wait_ge(*C_pool.after(q, "c_rstd"))
                    scaled(st_c, c_c, c_n, "cln_g", "cln_b", link_c(q), "c", "c_normed")

                def gate_centre(t, u, i):
                    g = TILES * l + t
                    v.wait_ge(*Z_vec.after(g, "glu"))
                    centre(sg_uv[:, 256:512].rearrange("p (a b) -> p a b", a=GROUPS), st_v, v_c, v_sq, link_v(g), "v")

                def gate_scale(t, u, i):
                    g = TILES * l + t
                    v.wait_ge(*Z_pool.after(g, "v_rstd"))
                    scaled(st_v, v_c, v_n, "sgu_g", "sgu_b", link_v(g), "v", "v_ready")

                def sgu_out(t, u, i):
                    g = TILES * l + t
                    v.wait_ge(*ZS_pe.after(g, "s"))
                    v.tensor_tensor(v_sq, bank(5, 0, 256).rearrange("p (a b) -> p a b", a=GROUPS),
                                    wide(s_bias[:, :], 2, GROUPS, HEAD), ALU.add).then_inc(*ZS_vec.next("s_biased"))
                    v.wait_ge(*ZS_vec.after(g, "s_biased"))
                    v.tensor_tensor(y[:, t, 0:SGU], v_sq.rearrange("p a b -> p (a b)"), sg_uv[:, 0:SGU],
                                    ALU.mult).then_inc(*ZS_vec.next("y_sgu"))

                def conv_silu(t, u, i):
                    v.wait_ge(*C_act.after(TILES * l + t, "c_tanh"))
                    v.scalar_tensor_tensor(c_y, c_th, 1.0, c_n.rearrange("p a b -> p (a b)"), ALU.add,
                                           ALU.mult).then_inc(*C_vec.next("c_silu"))

                def conv_out(t, u, i):
                    v.wait_ge(*CW_pe.after(TILES * l + t, "pw"))
                    v.scalar_tensor_tensor(y[:, t, SGU:2 * SGU], bank(5, 256, 512), 0.5, V["pw_b"], ALU.mult,
                                           ALU.add).then_inc(*CY_vec.next("y_conv"))

                lag_loop(v, [(1, turn(0)), (-1, sgu_out), (-2, conv_centre), (-1, conv), (-3, conv_out), (-2, conv_scale),
                             (0, gelu_cubic), (2, norm(0)), (0, gelu_glu), (0, gate_centre), (-2, conv_silu), (0, gate_scale)])

                def heads_view(b, lo, hi, width):
                    return ps[:, b:b + 2, 0:HC * width].rearrange("p a (h d) -> p a h d", h=HC)[:, :, :, lo:hi]

                def fold(ap):
                    return ap.rearrange("p (a h) d -> p a h d", a=2)

                def per_head(ap, d):
                    return ap.rearrange("p (a h) -> p a h", a=2).unsqueeze(3).to_broadcast([P, 2, HC, d])

                def c_norm(t, u, i):
                    g = TILES * l + t
                    v.wait_ge(*QC_pool.after(g))
                    v.scalar_tensor_tensor(cn[u][:, 0:QR], zc[:, t, 0:QR], r_c[:, 0:1], V["qa_g"], ALU.mult, ALU.mult)
                    v.scalar_tensor_tensor(cn[u][:, QR:QR + KVR], zc[:, t, QR:QR + KVR], r_c[:, 1:2], V["kva_g"], ALU.mult,
                                           ALU.mult).then_inc(*QC_vec.next("cn"))
                    v.scalar_tensor_tensor(zc[:, t, QR + KVR:MLA_IN], zc[:, t, QR + KVR:MLA_IN], r_c[:, 2:3], kg[:, HEAD:QK],
                                           ALU.mult, ALU.mult).then_inc(*QC_vec.next("kpe"))

                def q_sums(t, u, i):
                    g = TILES * l + t
                    v.wait_ge(*QM_act.after(g, "squared"))
                    v.wait_ge(*QM_pool.before(g))
                    v.tensor_reduce(m_qk[:, 0:8], qk_sq[:, :, 0:HEAD], AX.X, ALU.add)
                    v.tensor_reduce(m_qk[:, 8:16], qk_sq[:, :, HEAD:QK], AX.X, ALU.add)
                    v.tensor_reduce(m_qk[:, 16:24], k_sq, AX.X, ALU.add).then_inc(*QM_vec.next("sumsq"))

                def q_scale(t, u, i):
                    g = TILES * l + t

                    def link(ins, name):
                        ins.then_inc(*Q_vec.next(name))
                        v.wait_ge(*Q_vec.after(g, name))

                    def scaled(dst, src, r0, d):
                        return v.tensor_tensor(dst, src, wide(r_qk[:, u, r0:r0 + HEADS], 2, HEADS, d), ALU.mult)

                    v.wait_ge(*QM_pool.after(g))
                    v.wait_ge(*QM_raw.after(g))
                    scaled(qs[u][:, :, 0:HEAD], qs[u][:, :, 0:HEAD], 0, HEAD).then_inc(*Q_vec.next("q_nope"))
                    scaled(ks[u][:, :, 0:HEAD], ks[u][:, :, 0:HEAD], 16, HEAD).then_inc(*Q_vec.next("k_nope"))
                    scaled(pe_x, qs[u][:, :, HEAD:QK], 8, ROPE).then_inc(*Q_vec.next("q_pe"))
                    v.wait_ge(*Q_vec.after(g, "q_pe"))
                    v.tensor_tensor(qs[u][:, :, 0:HEAD], qs[u][:, :, 0:HEAD], wide(gq[:, 0:HEAD], 1, HEADS, HEAD),
                                    ALU.mult).then_inc(*Q_vec.next("q_gained"))
                    link(v.tensor_tensor(pe_x, pe_x, wide(gq[:, HEAD:QK], 1, HEADS, ROPE), ALU.mult), "pe_gained")
                    halves = pe_x.rearrange("p h (a r) -> p h a r", a=2)
                    k_halves = zc[:, t, QR + KVR:MLA_IN].rearrange("p (a r) -> p a r", a=2)
                    for tab, dst, name in ((cos, xc, "xc"), (sin, xs, "xs")):
                        v.tensor_tensor(dst[:, 0:HEADS], halves, tab[:, t, :].unsqueeze(1).unsqueeze(1).to_broadcast([P, HEADS, 2, HR]),
                                        ALU.mult)
                        v.tensor_tensor(dst[:, HEADS], k_halves, tab[:, t, :].unsqueeze(1).to_broadcast([P, 2, HR]),
                                        ALU.mult).then_inc(*Q_vec.next(name))
                    v.wait_ge(*Q_vec.after(g, "xs"))
                    for dst, src in ((qs[u], slice(0, HEADS)), (ks[u], None)):
                        def pick(x, half):
                            if src is None:
                                return x[:, HEADS:HEADS + 1, half, :].to_broadcast([P, HEADS, HR])
                            return x[:, 0:HEADS, half, :]
                        v.tensor_tensor(dst[:, :, HEAD:HEAD + HR], pick(xc, 0), pick(xs, 1), ALU.subtract)
                        ins = v.tensor_tensor(dst[:, :, HEAD + HR:QK], pick(xc, 1), pick(xs, 0), ALU.add)
                    ins.then_inc(*Q_vec.next("heads"))

                def q_turned(t, u, i):
                    g = TILES * l + t
                    v.wait_ge(qk_stored[u], 32 * (PAIRS * l + i) + 32)
                    v.wait_ge(*R_pe.after(g, "q_hi"))
                    v.tensor_copy(stage[u][0:QK, 0, HC:].rearrange("p a b -> p (a b)"), ps[0:QK, 1, :]).then_inc(*R_vec.next("q_hi"))
                    v.wait_ge(*R_pe.after(g, "k_hi"))
                    v.tensor_copy(stage[u][0:QK, 1, HC:].rearrange("p a b -> p (a b)"), ps[0:QK, 0, :]).then_inc(*R_vec.next("k_hi"))

                lag_loop(v, [(2, c_norm), (-1, q_turned), (1, q_sums), (0, q_scale)])

                def row_max(hh, j):
                    v.wait_ge(*S_pe.after(hh, f"s{j}"))
                    v.tensor_reduce(neg_max[:, j % 2:j % 2 + 1], banks(2 * (j % 2))[:, 0:(j + 1) * P], AX.X, ALU.max,
                                    negate=True).then_inc(*X_max.next(f"max{j}"))

                def prob_lo(hh, j):
                    w = min(j + 1, 4)
                    v.wait_ge(*T_pe.after(hh, f"lo{j}"))
                    v.tensor_copy(prob_t[j % 2][:, 0:w], bank(4, 0, w * P).rearrange("p (k q) -> p k q", q=P)
                                  ).then_inc(*X_lo.next(f"lo{j}"))

                def finish(hh, head, j):
                    v.wait_ge(*O_pe.after(hh, f"o{j}"))
                    v.reciprocal(rden[:, j % 2:j % 2 + 1], denom[:, j:j + 1]).then_inc(*X_fin.next(f"inv{j}"))
                    v.wait_ge(*X_fin.after(hh, f"inv{j}"))
                    v.tensor_scalar(y[:, j, bass.ds(head * HEAD + 2 * SGU, HEAD)], bank(6 + j % 2, 0, HEAD), rden[:, j % 2:j % 2 + 1],
                                    None, ALU.mult).then_inc(*X_fin.next(f"fin{j}"))

                row_max(HEADS * l, 0)
                with v.Fori(0, HEADS // 2) as i:
                    hh = HEADS * l + 2 * i
                    for n in range(2 * TILES):
                        if n + 1 < 2 * TILES:
                            row_max(hh + (n + 1) // TILES, (n + 1) % TILES)
                        else:
                            guarded(v, i < HEADS // 2 - 1, lambda: row_max(hh + 2, 0))
                        prob_lo(hh + n // TILES, n % TILES)
                        if n:
                            finish(hh + (n - 1) // TILES, 2 * i + (n - 1) // TILES, (n - 1) % TILES)
                    finish(hh + 1, 2 * i + 1, TILES - 1)

                def w_main(t, u, i):
                    g = TILES * l + t
                    for k, half in enumerate(("lo", "hi")):
                        v.wait_ge(*W_pe.after(g, half))
                        hv = h[:, t, 512 * k:512 * k + 512]
                        v.tensor_tensor(hv, hv, bank(2 + k), ALU.add).then_inc(*W_vec.next(half))

                def g_main(t, u, i):
                    v.wait_ge(*G_pe.after(TILES * l + t))
                    v.tensor_tensor(lg[:, t, :], bank(4 + u, 0, NG + NE), b_r[:, :], ALU.add).then_inc(*G_vec.next("logits"))

                lag_loop(v, [(-1, norm_m), (2, norm(1)), (1, turn(1)), (-1, turn_m), (0, w_main), (-1, g_main)])
                v.wait_ge(*G_vec.before(TILES * l + TILES))

                def link(ins, name):
                    ins.then_inc(*K_vec.next(name))
                    v.wait_ge(*K_vec.after(l, name))

                def sm(i):
                    return at(A, RS + 2560 + 8 * i, TILES)

                def bc(ap, n):
                    return ap.unsqueeze(2).to_broadcast([P, TILES, n])

                def row(n):
                    return iota[:, 0:n].unsqueeze(1).to_broadcast([P, TILES, n])

                gl_ = lg[:, :, 0:NG]
                el = lg[:, :, NG:NG + NE]
                link(v.tensor_reduce(sm(0), gl_, AX.X, ALU.max), "g_max")
                link(v.tensor_tensor(rs(0, TILES, NG), gl_, bc(sm(0), NG), ALU.subtract), "g_diff")
                v.wait_ge(*K_act.after(l, "g_exp"))
                link(v.tensor_reduce(sm(1), rs(1, TILES, NG), AX.X, ALU.add), "g_sum")
                link(v.reciprocal(sm(2), sm(1)), "g_w")
                link(v.tensor_scalar(rs(2, TILES, NG), rs(0, TILES, NG), 0.0, 64.0, ALU.is_lt, ALU.mult), "g_miss")
                link(v.tensor_tensor(rs(3, TILES, NG), rs(2, TILES, NG), row(NG), ALU.add), "g_cand")
                link(v.tensor_reduce(sm(3), rs(3, TILES, NG), AX.X, ALU.min), "g_first")
                link(v.tensor_tensor(rs(4, TILES, NG), row(NG), bc(sm(3), NG), ALU.is_equal), "g_hot")
                link(v.tensor_scalar(rs(5, TILES, NG), rs(4, TILES, NG), 1.0, BIG, ALU.subtract, ALU.mult), "g_far")
                link(v.tensor_tensor(rs(6, TILES, NG, EPG), el.rearrange("p t (g e) -> p t g e", g=NG),
                                     rs(5, TILES, NG).unsqueeze(3).to_broadcast([P, TILES, NG, EPG]), ALU.add), "e_in")

                def largest(src, top, where, hot, n):
                    link(v.tensor_reduce(top, src, AX.X, ALU.max), f"m{n}")
                    link(v.tensor_tensor(rs(7, TILES, NE), src, bc(top, NE), ALU.subtract), f"d{n}")
                    link(v.tensor_scalar(rs(8, TILES, NE), rs(7, TILES, NE), 0.0, 64.0, ALU.is_lt, ALU.mult), f"miss{n}")
                    link(v.tensor_tensor(rs(7, TILES, NE), rs(8, TILES, NE), row(NE), ALU.add), f"cand{n}")
                    link(v.tensor_reduce(where, rs(7, TILES, NE), AX.X, ALU.min), f"i{n}")
                    link(v.tensor_tensor(hot, row(NE), bc(where, NE), ALU.is_equal), f"hot{n}")

                hot1, hot2, rest = rs(2, TILES, NE), rs(4, TILES, NE), rs(3, TILES, NE)
                largest(rs(6, TILES, NE), sm(4), sm(5), hot1, 1)
                link(v.scalar_tensor_tensor(rest, hot1, -2 * BIG, rs(6, TILES, NE), ALU.mult, ALU.add), "rest")
                largest(rest, sm(6), sm(7), hot2, 2)
                link(v.tensor_tensor(picked_b, hot1, hot2, ALU.add), "picked")
                e2 = rs(9, 2, TILES)
                link(v.tensor_tensor(e2[:, 0], sm(6), sm(4), ALU.subtract), "e_diff")
                cnt = at(A, RS + 2816, 4).bitcast(I32)[0:NE]
                v.wait_ge(*K_pe.after(l, "ranks"))
                link(v.tensor_copy(cnt[:, 0:1], ps[0:NE, 6, 0:1]), "cnt_i")
                link(v.tensor_scalar(cnt[:, 1:2], cnt[:, 0:1], P - 1, None, ALU.add), "cnt_up")
                link(v.tensor_scalar(cnt[:, 2:3], cnt[:, 1:2], 7, None, ALU.logical_shift_right), "cnt_nb")
                nb_f = at(A, RS + 2824, 1)[0:NE]
                link(v.tensor_copy(nb_f, cnt[:, 2:3]), "nb_f")
                link(v.tensor_scalar(nb_col[0:NE, :], ones_b[0:NE, :], nb_f, None, ALU.mult), "nb_col")
                v.wait_ge(*K_pe.after(l, "starts"))
                ends = rs(5, 2, NE)
                link(v.tensor_copy(ends, bank(6, 64, 64 + 2 * NE).rearrange("p (a e) -> p a e", a=2)), "start_f")
                link(v.scalar_tensor_tensor(rs(6, TILES, NE), ends[:, 0].unsqueeze(1).to_broadcast([P, TILES, NE]), float(P),
                                            bank(7, 0, TILES * NE).rearrange("p (t e) -> p t e", t=TILES), ALU.mult, ALU.add), "row")
                dest_f, dest = at(A, RS + 2832, TILES, 2), at(A, RS + 2896, TILES, 2).bitcast(I32)
                for k, hot in enumerate((hot1, hot2)):
                    link(v.tensor_tensor(rs(7 + k, TILES, NE), hot, rs(6, TILES, NE), ALU.mult), f"r{k + 1}")
                    link(v.tensor_reduce(dest_f[:, :, k], rs(7 + k, TILES, NE), AX.X, ALU.add), f"dest{k + 1}")
                link(v.tensor_copy(dest, dest_f), "dest_i")
                blk_i = at(A, RS + 2848, TILES, 2).bitcast(I32)
                blk_f, slot_f = at(A, RS + 2864, TILES, 2), at(A, RS + 2880, TILES, 2)
                link(v.tensor_scalar(blk_i, dest, 7, None, ALU.logical_shift_right), "blk_i")
                link(v.tensor_copy(blk_f, blk_i), "blk_f")
                link(v.scalar_tensor_tensor(slot_f, blk_f, -float(P), dest_f, ALU.mult, ALU.add), "slot_f")
                for c in range(2 * TILES):
                    t, k = divmod(c, 2)
                    v.tensor_scalar(hot_s[:, c, :], iota[:, :], slot_f[:, t, k:k + 1], None, ALU.is_equal)
                    ins = v.tensor_scalar(hot_b[:, c, :], iota[:, 0:MAXB1], blk_f[:, t, k:k + 1], token[:, t, k:k + 1],
                                          ALU.is_equal, ALU.mult)
                ins.then_inc(*K_vec.next("hots"))
                le = at(C, 4096, MAXB1, NE)[0:1]
                owner = at(C, 4096 + 2048, MAXB1)[0:1]
                active = at(C, 4096 + 2112, MAXB1)[0:1]
                by_slot = at(C, 4096 + 2176, 3)[0:1]
                total = ends[0:1, 1, NE - 1:NE]
                link(v.tensor_tensor(le, ends[0:1, 1].unsqueeze(1).to_broadcast([1, MAXB1, NE]),
                                     iota[0:1, 0:MAXB1].unsqueeze(2).to_broadcast([1, MAXB1, NE]), ALU.is_le), "le")
                link(v.tensor_reduce(owner, le, AX.X, ALU.add), "owner")
                link(v.tensor_scalar(active, iota[0:1, 0:MAXB1], total, None, ALU.is_lt), "active")
                link(v.tensor_reduce(by_slot, active.rearrange("p (i u) -> p u i", u=3), AX.X, ALU.add), "by_slot")
                v.wait_ge(*K_act.after(l, "e_exp"))
                link(v.tensor_scalar(sm(8), e2[:, 1], 1.0, None, ALU.add), "e_den")
                link(v.reciprocal(sm(9), sm(8)), "e_rden")
                link(v.scalar_tensor_tensor(wts[:, 0], sm(2), 0.5, sm(9), ALU.mult, ALU.mult), "w1")
                link(v.tensor_tensor(wts[:, 1], wts[:, 0], e2[:, 1], ALU.mult), "w2")
                link(v.tensor_copy(cells[0:1, 48:52], run[:, :]), "before")
                link(v.tensor_tensor(run[:, 0:1], run[:, 0:1], total, ALU.add), "run_n")
                link(v.tensor_tensor(run[:, 1:4], run[:, 1:4], by_slot, ALU.add), "run_slots")
                v.wait_ge(*K_pe.after(l, "lists"))
                spare = rs(0, MAXB1)
                link(v.tensor_scalar(spare, bank(6, 128, 128 + MAXB1), 0.0, padding[:, :], ALU.is_equal, ALU.mult), "empty")
                link(v.scalar_tensor_tensor(out_idx[:, 0:MAXB1], bank(6, 128, 128 + MAXB1), -1.0, spare, ALU.add, ALU.add), "rows_i")
                v.tensor_scalar(idx[:, 0:MAXB1], out_idx[:, 0:MAXB1], SEQ - 1, None, ALU.bitwise_and).then_inc(*K_vec.next("list_i"))
                v.tensor_copy(cells[0:1, 0:MAXB1], owner).then_inc(*K_vec.next("owner_i"))
                v.tensor_copy(cells[0:1, 52:53], total).then_inc(*K_vec.next("cells"))

                prev, n, used = counters(v, l, passed)

                def x_hi(m):
                    v.wait_ge(*M_xT.after(m, "hi"))
                    v.tensor_copy(xT[:, 4:8].rearrange("p a b -> p (a b)"), bank(1)).then_inc(*M_xhi.next("x"))

                def hidden(m):
                    v.wait_ge(*M_tanh.after(m))
                    v.scalar_tensor_tensor(hid, hid_g, 1.0, bank(2, 0, F), ALU.add, ALU.mult).then_inc(*M_silu.next("silu"))
                    v.wait_ge(*M_silu.after(m))
                    v.tensor_tensor(hid, hid, bank(2, F, 2 * F), ALU.mult).then_inc(*M_prod.next("prod"))

                def y_hi(m):
                    v.wait_ge(y_stored, m * 16)
                    v.wait_ge(*M_dn.after(m, "hi"))
                    v.tensor_copy(y_blk[:, 512:1024], bank(5)).then_inc(*M_yhi.next("y"))

                x_hi(prev)
                hidden(prev)
                x_hi(prev + 1)

                def expert(b, here, nxt, last):
                    m = prev + b
                    guarded(v, b < n, lambda: hidden(m))
                    guarded(v, b + 1 < n, lambda: x_hi(m + 1))
                    guarded(v, b <= n, lambda: y_hi(m - 1))

                block_loop(v, expert)
                v.drain().then_inc(blocks_done, 1)

                v.wait_ge(ple_loaded, 64 * l + 64)
                settle(v, passed)

                def ple_front(t, u, i):
                    g = TILES * l + t
                    v.wait_ge(y_fetched[u], 32 * (PAIRS * l + i) + 32)
                    v.scalar_tensor_tensor(h[:, t, :], y_got[u][0], wts[:, 0, t:t + 1] if isinstance(t, int) else wts[:, 0, bass.ds(t, 1)],
                                           h[:, t, :], ALU.mult, ALU.add).then_inc(*E_comb.next("first"))
                    v.wait_ge(*E_comb.after(g, "first"))
                    v.scalar_tensor_tensor(h[:, t, :], y_got[u][1], wts[:, 1, t:t + 1] if isinstance(t, int) else wts[:, 1, bass.ds(t, 1)],
                                           h[:, t, :], ALU.mult, ALU.add).then_inc(*E_comb.next("second"))
                    norm(2)(t, u, i)

                def ple_main(t, u, i):
                    g = TILES * l + t
                    v.wait_ge(*E_pool.after(g, "rstd"))
                    v.wait_ge(h_final, g + TILES)
                    v.scalar_tensor_tensor(e_buf, banks(4), m_e[:, 2:3], gains[:, BRANCH], ALU.mult, ALU.mult).then_inc(*E_vec.next("e_scaled"))
                    v.wait_ge(*E_vec.after(g, "e_scaled"))
                    v.wait_ge(*E_act.after(g, "t_hi"))
                    v.scalar_tensor_tensor(e_buf, gate_t, 1.0, e_buf, ALU.add, ALU.mult).then_inc(*E_vec.next("gated"))
                    v.wait_ge(*E_vec.after(g, "gated"))
                    v.tensor_tensor(h[:, t, :], h[:, t, :], e_buf, ALU.add).then_inc(h_final, 1)

                lag_loop(v, [(2, ple_front), (1, turn(2)), (0, ple_main)])

        @block.tensor
        def _(pe):
            passed = sem("pe_passed")
            for s in (ZS_pe, CO_pe, CY_pe, CW_pe, R_pe, G_pe, E_pe, E_pT_pe, FX.pe, FM.pe):
                pe.sem_inc(s.sem, s.per * s.credit)
            T = nc.tensor.transpose
            mm = nc.tensor.matmul
            pe.wait_ge(*S_pool0.after(0, "selects"))
            pe.wait_ge(*S_vec0.after(0, "pos"))
            T(bank(0, 0, TILES), at(B, T0 + 280, P)[0:TILES], ident[0:TILES, 0:TILES]).then_inc(*S_pe0.next("pos_t"))
            pe.wait_ge(*S_vec0.after(0, "cols"))

            with pe.Fori(0, DEPTH) as l:
                pe.wait_ge(*L_pool.after(l))
                pe.wait_ge(*E_act.before(TILES * l))
                pe.wait_ge(*E_vec.before(TILES * l))
                for k in range(GROUPS):
                    T(bank(7, P * k, P * k + P), ws_raw[:, k, :], ident[:, :])
                for c in range(2):
                    T(bank(6, 32 * c, 32 * c + 32), cw_raw[:, P * c:P * c + P], ident[0:32, 0:32])
                T(bank(6, 64, 64 + GROUPS), sb_raw[:, :], ident[0:GROUPS, 0:GROUPS]).then_inc(*L_pe.next("prep_T"))
                pe.wait_ge(*L_act.after(l))

                def turns(b, src, steps_):
                    for k in range(KD):
                        ins = T(bank(b + k // 4, P * (k % 4), P * (k % 4) + P), src[:, P * k:P * k + P], ident[:, :])
                        if k % 4 == 3:
                            ins.then_inc(*steps_.next(("T_lo", "T_hi")[k // 4]))

                def turn(ph):
                    def go(t, u, i):
                        r = 24 * l + t + 8 * ph
                        pe.wait_ge(*FX.lo.before(r))
                        pe.wait_ge(*FX.hi.before(r))
                        pe.wait_ge(*FX.a.after(r))
                        turns(0, a_buf[u], FX.pe)
                    return go

                def turn_m(t, u, i):
                    g = TILES * l + t
                    pe.wait_ge(*FM.lo.before(g))
                    pe.wait_ge(*FM.hi.before(g))
                    pe.wait_ge(*FM.a.after(g))
                    turns(6, m_buf[u], FM.pe)

                def turned(ph, t):
                    r = 24 * l + t + 8 * ph
                    pe.wait_ge(*FX.lo.after(r))
                    pe.wait_ge(*FX.hi.after(r))

                def product(dst, lhsT, w, a, b):
                    for k in range(KD):
                        ins = mm(dst, lhsT[:, k, :], w[:, k, a:b], start=(k == 0), stop=(k == KD - 1))
                    return ins

                pe.wait_ge(w_in_loaded, 16 * l + 16)
                settle(pe, passed)

                def z_first(t, u, i):
                    g = TILES * l + t
                    turned(0, t)
                    pe.wait_ge(*Z_vec.after(g - 1, "sgu_gated"))
                    product(bank(2), aT[u], w_in, 0, 512).then_inc(*Z_pe.next("z_sgu"))

                def z_second(t, u, i):
                    g = TILES * l + t
                    pe.wait_ge(*Z_vec.after(g - 1, "glu"))
                    product(bank(3), aT[u], w_in, 512, 1024).then_inc(*Z_pe.next("z_glu"))
                    pe.wait_ge(*Z_act.before(g))
                    product(bank(4, 0, MLA_IN), aT[u], w_in, 1024, IN).then_inc(*Z_pe.next("z_mla"))

                def conv_back(t, u, i):
                    pe.wait_ge(*CT_vec.after(TILES * l + t))
                    pe.wait_ge(*C_act.after(TILES * l + t - 1, "ybT_evac"))
                    for c in range(2):
                        ins = T(bank(7, P * c, P * c + P), acc[:, c, :], ident[:, :])
                    ins.then_inc(*CO_pe.next("coT"))

                def mix_tokens(t, u, i):
                    g = TILES * l + t
                    pe.wait_ge(*V_vec.after(g, "v_ready"))
                    pe.wait_ge(*CY_vec.after(g - 3))
                    for k in range(GROUPS):
                        ins = mm(bank(5, HEAD * k, HEAD * k + HEAD), wsT[:, k, :], v_n[:, k, :], start=True, stop=True)
                    ins.then_inc(*ZS_pe.next("s"))
                    pe.wait_ge(*Z_vec.after(g, "glu"))
                    pe.wait_ge(*ZC_act.before(g))
                    for c in range(2):
                        ins = T(bank(6, P * c, P * c + P), gl[:, P * c:P * c + P], ident[:, :])
                    ins.then_inc(*ZS_pe.next("gluT"))

                def conv_turn(t, u, i):
                    pe.wait_ge(*C_vec.after(TILES * l + t, "c_silu"))
                    for c in range(2):
                        ins = T(bank(7, 256 + P * c, 256 + P * c + P), c_y[:, P * c:P * c + P], ident[:, :])
                    ins.then_inc(*CY_pe.next("ybT"))

                def pointwise(t, u, i):
                    q = TILES * l + t
                    pe.wait_ge(*C_act.after(q, "ybT_evac"))
                    pe.wait_ge(*ZS_vec.after(TILES * l + (min(t + 2, TILES - 1) if isinstance(t, int) else t + 2)))
                    for c in range(2):
                        ins = mm(bank(5, 256, 512), c_yT[:, c, :], pw[:, c, :], start=(c == 0), stop=(c == 1))
                    ins.then_inc(*CW_pe.next("pw"))

                lag_loop(pe, [(1, turn(0)), (-2, conv_back), (-1, mix_tokens), (0, z_first), (-3, pointwise), (0, z_second),
                              (-2, conv_turn)])

                end = TILES * l + TILES
                for s in (Z_vec, ZS_vec, V_vec, C_vec, CY_vec, Z_act, C_act):
                    pe.wait_ge(*s.before(end))
                settle(pe, passed)

                def q_main(t, u, i):
                    g = TILES * l + t
                    pe.wait_ge(*QC_vec.after(g, "cn"))
                    for k in range(3):
                        ins = T(bank(6, P * k, P * k + P), cn[u][:, P * k:P * k + P], ident[:, :])
                    ins.then_inc(*QM_pe.next("cT"))
                    pe.wait_ge(*QM_act.after(g, "cnT"))
                    pe.wait_ge(*QM_raw.before(g))
                    for half in range(2):
                        w = HC * QK
                        for k in range(2):
                            ins = mm(bank(2 + half, 0, w), cnT[:, k, :], w_uq[:, k, w * half:w * half + w], start=(k == 0), stop=(k == 1))
                    ins.then_inc(*QM_pe.next("q_mm"))
                    for half in range(2):
                        ins = mm(bank(4 + half), cnT[:, 2, :], w_ukv[:, 512 * half:512 * half + 512], start=True, stop=True)
                    ins.then_inc(*QM_pe.next("kv_mm"))

                def q_turn(t, u, i):
                    g = TILES * l + t
                    pe.wait_ge(*R_act.before(g))
                    pe.wait_ge(*R_vec.before(g))
                    pe.wait_ge(*Q_vec.after(g, "heads"))
                    for name, b, src in (("q_lo", 0, qs[u][:, 0:HC]), ("q_hi", 1, qs[u][:, HC:]), ("k_lo", 7, ks[u][:, 0:HC]),
                                         ("k_hi", 0, ks[u][:, HC:])):
                        if name == "k_hi":
                            pe.wait_ge(*R_act.after(g, "q_lo"))
                        for k in range(HC):
                            ins = T(ps[0:QK, b, P * k:P * k + P], src[:, k, :], ident[:, :])
                        ins.then_inc(*R_pe.next(name))

                lag_loop(pe, [(1, q_main), (-1, q_turn)])

                for s in (Q_vec, QM_raw, R_act, R_vec):
                    pe.wait_ge(*s.before(end))
                settle(pe, passed)

                def before(hh, j, back):
                    return (hh, j - back) if j >= back else (hh - 1, j - back + TILES)

                def scores(hh, u, j, i):
                    if j == 0:
                        pe.wait_ge(qk_loaded[u], 32 * (HEADS // 2 * l + i) + 32)
                    h2, j2 = before(hh, j, 2)
                    pe.wait_ge(*X_act.after(h2, f"exp{j2}"))
                    settle(pe, passed)
                    q = q_ring[u][0:QK, P * j:P * j + P]
                    b = 2 * (j % 2)
                    cols = (j + 1) * P
                    for c in range(0, cols, 512):
                        w = min(512, cols - c)
                        last = c + 512 >= cols
                        mm(bank(b + c // 512, 0, w), q, k_ring[u][0:QK, c:c + w], start=True, stop=not last, skip_group_check=True)
                    d = (j * P) % 512
                    mm(bank(b + j // 4, d, d + P), ident_b[:, :], mask_b[:, :], start=False, stop=True,
                       skip_group_check=True).then_inc(*S_pe.next(f"s{j}"))

                def transposed(hh, j):
                    h1, j1 = before(hh, j, 1)
                    pe.wait_ge(*X_lo.after(h1, f"lo{j1}"))
                    if j1 >= 4:
                        pe.wait_ge(*X_hi.after(h1, f"hi{j1}"))
                    pe.wait_ge(*X_act.after(hh, f"exp{j}"))
                    for k in range(j + 1):
                        ins = T(bank(4 + k // 4, P * (k % 4), P * (k % 4) + P), prob[j % 2][:, P * k:P * k + P], ident[:, :])
                        if k == min(j, 3):
                            ins.then_inc(*T_pe.next(f"lo{j}"))
                    if j >= 4:
                        ins.then_inc(*T_pe.next(f"hi{j}"))

                def outputs(hh, head, j):
                    pe.wait_ge(*X_lo.after(hh, f"lo{j}"))
                    if j >= 4:
                        pe.wait_ge(*X_hi.after(hh, f"hi{j}"))
                    h2, j2 = before(hh, j, 2)
                    pe.wait_ge(*X_fin.after(h2, f"fin{j2}"))
                    for k in range(j + 1):
                        ins = mm(bank(6 + j % 2, 0, HEAD), prob_t[j % 2][:, k, :], vals[:, k, head, :], start=(k == 0), stop=(k == j))
                    ins.then_inc(*O_pe.next(f"o{j}"))

                scores(HEADS * l, 0, 0, 0)
                with pe.Fori(0, HEADS // 2) as i:
                    hh = HEADS * l + 2 * i
                    for n in range(2 * TILES):
                        if n + 1 < 2 * TILES:
                            scores(hh + (n + 1) // TILES, (n + 1) // TILES, (n + 1) % TILES, i)
                        else:
                            guarded(pe, i < HEADS // 2 - 1, lambda: scores(hh + 2, 0, 0, i + 1))
                        transposed(hh + n // TILES, n % TILES)
                        if n:
                            outputs(hh + (n - 1) // TILES, 2 * i + (n - 1) // TILES, (n - 1) % TILES)
                    outputs(hh + 1, 2 * i + 1, TILES - 1)

                pe.wait_ge(*X_fin.before(HEADS * l + HEADS))
                pe.wait_ge(wo_loaded, 16 * l + 16)
                settle(pe, passed)

                def w_half(k):
                    def go(t, u, i):
                        g = TILES * l + t
                        if k == 0:
                            turned(1, t)
                        pe.wait_ge(*W_vec.after(g - 1, ("lo", "hi")[k]))
                        product(bank(2 + k), aT[u], w_o, 512 * k, 512 * k + 512).then_inc(*W_pe.next(("lo", "hi")[k]))
                    return go

                def g_main(t, u, i):
                    g = TILES * l + t
                    pe.wait_ge(*FM.lo.after(g))
                    pe.wait_ge(*FM.hi.after(g))
                    pe.wait_ge(*G_vec.after(g - 2))
                    product(bank(4 + u, 0, NG + NE), mT, w_r, 0, NG + NE).then_inc(*G_pe.next("logits"))

                lag_loop(pe, [(1, turn(1)), (0, w_half(0)), (-1, turn_m), (0, w_half(1)), (-1, g_main)])

                pe.wait_ge(*K_vec.after(l, "picked"))
                settle(pe, passed)
                for t in range(TILES):
                    mm(ps[0:NE, 6, 0:1], picked_b[:, t, :], ones_b[:, 0:1], start=(t == 0), stop=(t == TILES - 1))
                for t in range(TILES):
                    for s in range(t + 1):
                        lhs = tri_b if s == t else ones_b
                        ins = mm(bank(7, NE * t, NE * t + NE), lhs[:, :], picked_b[:, s, :], start=(s == 0), stop=(s == t))
                ins.then_inc(*K_pe.next("ranks"))
                pe.wait_ge(*K_vec.after(l, "nb_col"))
                settle(pe, passed)
                mm(bank(6, 64, 64 + NE), nb_col[0:NE, :], tri_b[0:NE, 0:NE], start=True, stop=True)
                mm(bank(6, 64 + NE, 64 + 2 * NE), nb_col[0:NE, :], tri_b[0:NE, 0:NE], start=True, stop=False)
                mm(bank(6, 64 + NE, 64 + 2 * NE), nb_col[0:NE, :], ident_b[0:NE, 0:NE], start=False,
                   stop=True).then_inc(*K_pe.next("starts"))
                pe.wait_ge(*K_vec.after(l, "hots"))
                settle(pe, passed)
                for c in range(2 * TILES):
                    ins = mm(bank(6, 128, 128 + MAXB1), hot_s[:, c, :], hot_b[:, c, :], start=(c == 0), stop=(c == 2 * TILES - 1))
                ins.then_inc(*K_pe.next("lists"))

                prev, n, used = counters(pe, l, passed)

                def turn_x(m, s, use):
                    pe.wait_ge(x_gathered[s], (used[s] + use) * 16 + 16)
                    pe.wait_ge(*M_xlo.before(m))
                    pe.wait_ge(*M_xhi.before(m))
                    for k in range(KD):
                        ins = T(bank(k // 4, P * (k % 4), P * (k % 4) + P), x_blk[s][:, P * k:P * k + P], ident[:, :])
                        if k % 4 == 3:
                            ins.then_inc(*M_xT.next(("lo", "hi")[k // 4]))

                def gate_up(m, s, use):
                    pe.wait_ge(gu_loaded[s], (used[s] + use) * 32 + 32)
                    pe.wait_ge(*M_xlo.after(m))
                    pe.wait_ge(*M_xhi.after(m))
                    for k in range(KD):
                        ins = mm(bank(2), xT[:, k, :], w_gu[s][:, k, :], start=(k == 0), stop=(k == KD - 1))
                    ins.then_inc(*M_gu.next("gu"))

                def down(m, s, use):
                    pe.wait_ge(dn_loaded[s], (used[s] + use) * 16 + 16)
                    pe.wait_ge(*M_h.after(m))
                    pe.wait_ge(*M_ylo.before(m))
                    pe.wait_ge(*M_yhi.before(m))
                    for half in range(2):
                        for k in range(2):
                            ins = mm(bank(4 + half), hid_t[:, k, :], w_dn[s][:, k, 512 * half:512 * half + 512], start=(k == 0),
                                     stop=(k == 1))
                        ins.then_inc(*M_dn.next(("lo", "hi")[half]))

                def turn_h(m):
                    pe.wait_ge(*M_prod.after(m))
                    for k in range(2):
                        ins = T(bank(3, P * k, P * k + P), hid[:, P * k:P * k + P], ident[:, :])
                    ins.then_inc(*M_hT.next("hT"))

                turn_x(prev, 0, 0)
                gate_up(prev, 0, 0)
                turn_x(prev + 1, 1, 0)
                turn_h(prev)

                def expert(b, here, nxt, last):
                    m = prev + b
                    guarded(pe, b < n, lambda: gate_up(m, *here))
                    guarded(pe, b + 1 < n, lambda: turn_x(m + 1, *nxt))
                    guarded(pe, b <= n, lambda: down(m - 1, *last))
                    guarded(pe, b < n, lambda: turn_h(m))

                block_loop(pe, expert)

                pe.wait_ge(ple_loaded, 64 * l + 64)
                settle(pe, passed)

                def turn_p(t, u, i):
                    g = TILES * l + t
                    pe.wait_ge(p_loaded[u], 16 * (PAIRS * l + i) + 16)
                    pe.wait_ge(*E_pT_act.before(g))
                    for k in range(2):
                        ins = T(bank(6, P * k, P * k + P), p_tile[u][:, P * k:P * k + P], ident[:, :])
                    ins.then_inc(*E_pT_pe.next("pT"))

                def ple_main(t, u, i):
                    g = TILES * l + t
                    pe.wait_ge(*E_pT_act.after(g))
                    pe.wait_ge(*E_vec.after(g - 1, "e_scaled"))
                    for half in range(2):
                        for k in range(2):
                            ins = mm(bank(4 + half), pT[u][:, k, :], ple_p[:, k, 512 * half:512 * half + 512], start=(k == 0), stop=(k == 1))
                    ins.then_inc(*E_pe.next("e"))
                    turned(2, t)
                    for k, half in enumerate(("g_lo", "g_hi")):
                        pe.wait_ge(*E_act.after(g - 1, ("t_lo", "t_hi")[k]))
                        product(bank(2 + k), aT[u], ple_g, 512 * k, 512 * k + 512).then_inc(*E_pe.next(half))

                lag_loop(pe, [(1, turn(2)), (1, turn_p), (0, ple_main)])


_INS = ["x", "p", "positions", "mix_norm_g", "w_in", "sgu_ln_g", "sgu_ln_b", "sgu_w", "sgu_b", "conv_w", "conv_b",
        "conv_ln_g", "conv_ln_b", "conv_pw_w", "conv_pw_b", "q_a_norm_g", "w_uq", "kv_a_norm_g", "w_ukv", "q_norm_g",
        "k_norm_g", "branch_norm_g", "w_o", "ffn_norm_g", "router_group_w", "router_group_b", "router_expert_w",
        "router_expert_b", "moe_w_gate", "moe_w_up", "moe_w_down", "ple_norm_g", "ple_gate_w", "ple_proj_w",
        "ple_post_norm_g"]


def kernel(**inputs):
    import numpy as _np
    import concourse.bacc as _bacc
    from concourse import mybir as _mybir
    from concourse.bass_utils import run_bass_kernel_spmd as _run

    nc = _bacc.Bacc("TRN2", target_bir_lowering=False, num_devices=1)
    arrays, args = {}, {}
    for name in _INS:
        a = _np.ascontiguousarray(inputs[name])
        arrays[f"in_{name}_dram"] = a
        args[name] = nc.dram_tensor(f"in_{name}_dram", a.shape, _mybir.dt.from_np(a.dtype), kind="ExternalInput").ap()
    out = nc.dram_tensor("out_0_dram", inputs["x"].shape, _mybir.dt.from_np(_np.dtype("float32")), kind="ExternalOutput").ap()
    build(nc, args, out)
    r = _run(nc, [arrays], core_ids=[0])
    return r.results[0]["out_0_dram"]
```

```python
from contextlib import ExitStack

import numpy as np

import concourse.bass as bass
from concourse import mybir

F32 = mybir.dt.float32
BF16 = mybir.dt.bfloat16
F16 = mybir.dt.float16
I32 = mybir.dt.int32
ALU = mybir.AluOpType
ACT = mybir.ActivationFunctionType
AX = mybir.AxisListType

P = 128
HEAD = 64
EPS = 1e-6
ROPE_THETA = 10000.0
BIG = 1e30
GELU_C = 0.7978845608028654
GELU_A = 0.044715
ROUND = 12582912.0
TWO_PI_HI = 6.28125
TWO_PI_MID = round((2 * np.pi - TWO_PI_HI) * 2 ** 20) / 2 ** 20
TWO_PI_LO = float(np.float32(2 * np.pi - TWO_PI_HI - TWO_PI_MID))


class Steps:

    def __init__(self, sem, names, credit=0):
        self.sem, self.names, self.per, self.credit, self.at = sem, list(names), len(names), credit, 0

    def next(self, name):
        assert self.names[self.at] == name, (name, self.names[self.at])
        self.at = (self.at + 1) % self.per
        return self.sem, 1

    def after(self, index, name=None):
        n = self.per if name is None else self.names.index(name) + 1
        return self.sem, index * self.per + (n + self.credit * self.per)

    def before(self, index):
        return self.sem, index * self.per + self.credit * self.per


class Front:

    def __init__(self, steps, name):
        self.square = steps(name + "_square", ["squared"], credit=1)
        self.pool = steps(name + "_pool", ["eps", "rstd"], credit=1)
        self.a = steps(name + "_a", ["a"], credit=1)
        self.pe = steps(name + "_pe", ["T_lo", "T_hi"], credit=1)
        self.lo = steps(name + "_lo", ["aT"], credit=1)
        self.hi = steps(name + "_hi", ["aT"], credit=1)


def build(nc, I, out):
    DEPTH, _, SEQ, PLE = I["p"].shape
    D = I["x"].shape[2]
    TILES, KD = SEQ // P, D // P
    SGU = I["sgu_ln_g"].shape[1]
    GROUPS = SGU // HEAD
    TAPS = I["conv_w"].shape[1]
    QR, KVR = I["q_a_norm_g"].shape[1], I["kv_a_norm_g"].shape[1]
    QK = I["q_norm_g"].shape[1]
    HEADS = I["w_uq"].shape[2] // QK
    ROPE = QK - HEAD
    HR = ROPE // 2
    IN = I["w_in"].shape[2]
    MLA_IN = IN - 4 * SGU
    NG, NE = I["router_group_w"].shape[2], I["router_expert_w"].shape[2]
    EPG = NE // NG
    F = I["moe_w_gate"].shape[3]
    TOPK = 2
    MAXB = (SEQ * TOPK - NE) // P + NE
    MAXB1 = MAXB + 1
    SCALE = float(QK) ** -0.5
    HC = HEADS // 2
    PAIRS = TILES // 2
    EARLY = 6
    SPLIT = 9
    assert (TILES, KD, D, F, MAXB1 % 3, HC * P) == (8, 8, 1024, 256, 0, 512)

    with ExitStack() as ctx:
        def sb(name, shape, dt=F32):
            return ctx.enter_context(nc.sbuf_tensor(name, shape, dt))

        def sem(name):
            return ctx.enter_context(nc.semaphore(name))

        def steps(name, names, credit=0):
            return Steps(sem(name), names, credit)

        m_dram = nc.dram_tensor("moe_inputs", (SEQ, D), F32).ap()
        y_rows = nc.dram_tensor("choice_outputs", (2 * SEQ + P, D), F32).ap()
        e_dram = nc.dram_tensor("projected", (SEQ, D), F32).ap()
        qk_dram = nc.dram_tensor("qk_heads", (2, QK, HEADS, SEQ), F32).ap()

        ps = ctx.enter_context(nc.psum_tensor("ps", [P, 8, 512], F32))

        def bank(n, a=0, b=512):
            return ps[:, n, a:b]

        def banks(n):
            return ps[:, n:n + 2, :].rearrange("p a b -> p (a b)")

        h = sb("h", [P, TILES, D])
        A = sb("region_a", [P, KD * IN])
        B = sb("region_b", [P, 2 * TILES * 640])
        C = sb("region_c", [P, 13312])
        junk = sb("junk", [P, D])
        gains = sb("gains", [P, 3, D])
        MIX, BRANCH, FFN = 0, 1, 2
        prods = sb("tap_products", [P, 3, 2 * P])

        def at(region, off, *shape):
            n = int(np.prod(shape))
            v = region[:, off:off + n]
            if len(shape) == 1:
                return v
            names = " ".join("abcd"[:len(shape)])
            return v.rearrange(f"p ({names}) -> p {names}", **dict(zip("abcd", shape)))

        w_in = at(A, 0, KD, IN)
        w_in_cols = (slice(0, 2 * SGU), slice(2 * SGU, 4 * SGU), slice(4 * SGU, IN))
        stage = [at(A, 2048 * u, 2, HEADS, P) for u in range(2)]
        q_ring = [at(B, 9216, SEQ), at(A, 4096, SEQ)]
        k_ring = [at(C, 12288, SEQ), at(A, 6144, SEQ)]
        prob = [at(A, 8192 + 1024 * u, SEQ) for u in range(2)]
        prob_t = [at(A, 10240, TILES, P), at(A, 7168, TILES, P)]
        qk_sq = at(A, 8192, HEADS, QK)
        k_sq = at(A, 8192 + 768, HEADS, HEAD)
        xc = at(A, 9472, HEADS + 1, 2, HR)
        xs = at(A, 9472 + 288, HEADS + 1, 2, HR)
        pe_x = at(A, 10240, HEADS, ROPE)
        x_blk = [at(A, 6144 + 1024 * u, D) for u in range(3)]
        m_buf = [at(A, 1024 * u, D) for u in range(2)]
        mT = at(A, 2048, KD, P)
        junk_m = at(A, 3072, D)
        xT = at(A, 9216, KD, P)
        hid = at(A, 10240, F)
        hid_t = at(A, 10496, 2, P)
        hid_g = at(A, 10752, F)
        w_uq = at(B, 0, 2, HEADS * QK)
        w_ukv = at(B, 1536, HEADS * 2 * HEAD)
        zc = at(B, 2560, TILES, MLA_IN)
        T0 = 2560 + TILES * MLA_IN
        sg_t, sg_uv = at(B, T0, 512), at(B, T0 + 512, 512)
        gl_t, gl = at(B, T0 + 1024, SGU), at(B, T0 + 1280, SGU)
        v_c, v_sq, v_n = (at(B, T0 + 1536 + 256 * i, GROUPS, HEAD) for i in range(3))
        WIDE = SEQ + TAPS - 1
        later = gains[:, 1:3].rearrange("p a d -> p (a d)")
        cin = [later[:, 0:WIDE], at(C, 13312 - WIDE, WIDE)]
        acc = [later[:, WIDE + 2 * P * c:WIDE + 2 * P * c + 2 * P] for c in range(2)]
        product_ring = [prods[:, k] for k in range(3)]
        acc_pool = at(B, T0 + 2304, 2 * P)
        acc_odd = later[:, WIDE + 4 * P:WIDE + 6 * P]
        c_c, c_sq, c_n = (at(B, T0 + 2560 + 256 * i, GROUPS, HEAD) for i in range(3))
        c_th, c_y = at(B, T0 + 3328, SGU), at(B, T0 + 3584, SGU)
        c_yT = at(B, T0 + 3840, 2, P)
        cn = [at(B, T0 + 384 * u, QR + KVR) for u in range(2)]
        cnT = at(B, T0 + 768, 3, P)
        qs = [at(A, 4096 + 2048 * u, HEADS, QK) for u in range(2)]
        ks = [at(A, 4864 + 2048 * u, HEADS, QK) for u in range(2)]
        w_o = at(B, 0, KD, D)
        ple_g = at(B, 0, KD, D)
        ple_p = at(B, KD * D, 2, D)
        a_buf = [at(C, 1024 * u, D) for u in range(2)]
        aT = [at(C, 2048 + 1024 * u, KD, P) for u in range(2)]
        vals = at(C, 0, TILES, HEADS, HEAD)
        y = at(C, 4096, TILES, D)
        y_blk = at(C, 12288, D)
        y_got = [[at(C, 4096 + 2048 * u + 1024 * k, D) for k in range(2)] for u in range(2)]
        gate_t, e_buf = at(C, 8192, D), at(C, 9216, D)
        e_got = [at(C, 10240 + 1024 * u, D) for u in range(2)]
        p_all = at(C, 6144, TILES, PLE)
        e_out = [at(C, 10240 + 1024 * u, D) for u in range(2)]
        pT = at(C, 8192, PAIRS, 2, 2, P)
        slot = [C[:, 0:6144], C[:, 6144:12288], A[:, 0:6144]]
        w_gu = [s[:, 0:KD * 2 * F].rearrange("p (k f) -> p k f", k=KD) for s in slot]
        w_dn = [s[:, KD * 2 * F:6144].rearrange("p (k f) -> p k f", k=2) for s in slot]
        RS = 6144

        def rs(i, *shape):
            return at(A, RS + 256 * i, *shape)

        vec = sb("vecs", [P, 7 * 256])
        names = ["sgu_g", "sgu_b", "cln_g", "cln_b", "pw_b", "qa_g"]
        V = {n: vec[:, 256 * i:256 * i + 256] for i, n in enumerate(names)}
        V["kva_g"] = vec[:, 1536:1536 + KVR]
        qg = sb("q_gain", [P, QK])
        kg = sb("k_gain", [P, QK])
        gq = sb("score_gain", [P, QK])
        ws_raw = at(B, 8192, GROUPS, P)
        wsT = sb("sgu_w_t", [P, GROUPS, P])
        cw_raw = at(B, 8704, SGU)[0:32]
        cw = sb("conv_w_cols", [P, 2, 32])
        sb_raw = at(B, 8960, P)[0:GROUPS]
        s_bias = sb("sgu_b_cols", [P, GROUPS])
        pw = sb("conv_pw", [P, 2, SGU])
        w_r = sb("router_w", [P, KD, NG + NE])
        b_r = sb("router_b", [P, NG + NE])
        lg = at(A, 4096, TILES, NG + NE)
        wts = sb("moe_weights", [P, 2, TILES])
        idx = sb("block_tokens", [P, MAXB1 + 3], I32)
        out_idx = sb("block_rows", [P, MAXB1 + 3], I32)
        idx_ring = sb("idx_ring", [P, 3], I32)
        out_ring = sb("out_ring", [P, 1], I32)
        cells = sb("cells", [1, 64], I32)
        run = sb("running", [1, 4])
        ms = sb("mean_sq", [P, 2, 3])
        rstd = sb("rstd", [P, 2, 3])
        pool_t = sb("pool_t", [P, 3])
        ms_m, rstd_m, pool_m = sb("mean_sq_m", [P, 2]), sb("rstd_m", [P, 2]), sb("pool_m", [P, 1])
        m_c, r_c, t_c = sb("m_c", [P, 3]), sb("r_c", [P, 3]), sb("t_c", [P, 3])
        m_qk, r_qk, t_qk = sb("m_qk", [P, 24]), sb("r_qk", [P, 2, 24]), sb("t_qk", [P, 24])
        st_v = sb("st_v", [P, 5, GROUPS])
        st_c = sb("st_c", [P, 5, GROUPS])
        m_e = sb("m_e", [P, 3, TILES])
        neg_max = sb("neg_max", [P, 2])
        denom = sb("denom", [P, TILES])
        rden = sb("rden", [P, 2])
        ident = sb("ident", [P, P])
        ident_b = sb("ident_b", [P, P], BF16)
        mask_b = sb("mask_b", [P, P], BF16)
        tri_b = sb("tri_b", [P, P], BF16)
        ones_b = sb("ones_b", [P, P], BF16)
        iota = sb("iota", [P, P])
        token = sb("token", [P, TILES, 2])
        padding = sb("padding", [P, 1])
        neg_half = sb("neg_half", [P, 24])
        eps_y = sb("eps_y", [P, 3])
        cos, sin = sb("cos", [P, TILES, HR]), sb("sin", [P, TILES, HR])
        pos_raw = at(B, T0 + 4096, P).bitcast(I32)[0:TILES]
        hot_s = A[:, RS + 3072:RS + 3072 + 1024].bitcast(F16).rearrange("p (n s) -> p n s", n=2 * TILES)
        hot_b = A[:, RS + 4096:RS + 4096 + 384].bitcast(F16).rearrange("p (n b) -> p n b", n=2 * TILES)
        picked_b = A[:, RS + 4480:RS + 4480 + 128].bitcast(BF16).rearrange("p (t e) -> p t e", t=TILES)
        nb_col = A[:, RS + 4608:RS + 4608 + 64].bitcast(BF16)

        pos_loaded = sem("pos_loaded")
        h_loaded, w_in_loaded = [sem(f"h_loaded{k}") for k in range(2)], [sem(f"w_in_loaded{k}") for k in range(3)]
        mix_loaded, small_loaded, mla_loaded, late_loaded = (sem(n + "_loaded") for n in ("mix", "small", "mla", "late"))
        wo_loaded, ple_loaded, proj_loaded = sem("wo_loaded"), sem("ple_loaded"), sem("proj_loaded")
        qk_stored = [sem(f"qk_stored{u}") for u in range(2)]
        qk_loaded = [[sem(f"qk_loaded{part}_{u}") for u in range(2)] for part in range(2)]
        m_stored = [sem(f"m_stored{u}") for u in range(2)]
        gu_loaded = [sem(f"gu_loaded{u}") for u in range(3)]
        dn_loaded = [sem(f"dn_loaded{u}") for u in range(3)]
        x_gathered = [sem(f"x_gathered{u}") for u in range(3)]
        y_stored = sem("y_stored")
        y_fetched = [sem(f"y_fetched{u}") for u in range(2)]
        p_loaded = sem("p_loaded")
        e_stored = [sem(f"e_stored{u}") for u in range(2)]
        e_fetched = [sem(f"e_fetched{u}") for u in range(2)]
        out_stored = sem("out_stored")
        h_final = sem("h_final")
        blocks_done = sem("blocks_done")

        S_pool0 = steps("const_pool", ["memsets", "selects"])
        S_vec0 = steps("const_vec", ["casts", "pos", "cols", "ang", "turns", "whole", "r_hi", "r_mid", "r_lo",
                                     "clamped", "neg", "abs", "cosarg"])
        S_pe0, S_act0 = steps("const_pe", ["pos_t"]), steps("const_act", ["sin", "cos"])
        FX, FM = Front(steps, "x"), Front(steps, "m")
        L_pool, L_pe = steps("l_pool", ["sgu_masked"]), steps("l_pe", ["prep_T"])
        L_act = steps("l_act", ["prep_evac"])
        L_vec = steps("l_vec", ["cin_zero", "gq_pe", "gq_nope"])
        Z_pe, ZS_pe = steps("z_pe", ["z_sgu", "z_glu", "z_mla"]), steps("zs_pe", ["s"], credit=1)
        ZG_pe = steps("zg_pe", ["gluT"], credit=1)
        Z_act = steps("z_act", ["sgu_square", "sgu_tanh", "glu_tanh", "mla_copied"])
        ZC_act = steps("zc_act", ["cin0", "cin1"], credit=2)
        Z_vec = steps("z_vec", ["sgu_cubic", "sgu_gated", "glu"], credit=1)
        V_vec = steps("v_vec", ["v_sum", "v_mean", "v_centred", "v_squared", "v_sumsq", "v_scaled", "v_gained", "v_ready"], credit=1)
        Z_pool, ZS_vec = steps("z_pool", ["v_eps", "v_rstd"]), steps("zs_vec", ["s_biased", "y_sgu"], credit=2)
        CO_pe, CY_pe, CW_pe = steps("co_pe", ["coT"], credit=2), steps("cy_pe", ["ybT"], credit=4), steps("cw_pe", ["pw"], credit=5)
        C_act, C_pool = steps("c_act", ["c_tanh", "ybT_evac"], credit=5), steps("c_pool", ["c_eps", "c_rstd"], credit=4)
        vec_taps = [0] + list(range(SPLIT + 1, TAPS))
        CP_act = steps("cp_act", [f"product{k}" for k in range(1, SPLIT + 1)], credit=2)
        CP_pool = steps("cp_pool", [f"sum{k}" for k in range(2, SPLIT + 1)], credit=2)
        CT_vec = steps("ct_vec", [f"tap{k}" for k in vec_taps] + ["joined", "merged"], credit=4)
        C_vec = steps("c_vec", ["c_sum", "c_mean", "c_centred", "c_squared", "c_sumsq", "c_scaled", "c_gained", "c_normed",
                                "c_silu"], credit=4)
        CY_vec = steps("cy_vec", ["y_conv"], credit=6)
        QC_act, QC_pool, QC_vec = steps("qc_act", ["squared"]), steps("qc_pool", ["eps", "rstd"]), steps("qc_vec", ["cn", "kpe"])
        QM_pe = steps("qm_pe", ["cT", "q_mm", "kv_mm"])
        QT_act, QM_act = steps("qt_act", ["cnT"]), steps("qm_act", ["squared", "v_stored"])
        QM_raw, QM_vec, QM_pool = steps("qm_raw", ["raw"]), steps("qm_vec", ["sumsq"]), steps("qm_pool", ["eps", "rstd"])
        Q_vec = steps("q_vec", ["q_nope", "k_nope", "q_pe", "q_gained", "pe_gained", "xc", "xs", "heads"], credit=1)
        R_pe = steps("r_pe", ["q_lo", "q_hi", "k_lo", "k_hi"], credit=2)
        R_act, R_vec = steps("r_act", ["q_lo", "k_lo"], credit=1), steps("r_vec", ["q_hi", "k_hi"], credit=3)
        tiles = range(TILES)
        S_pe, O_pe = steps("s_pe", [f"s{j}" for j in tiles]), steps("o_pe", [f"o{j}" for j in tiles])
        T_pe = steps("t_pe", [n for j in tiles for n in ([f"lo{j}"] + [f"hi{j}"] * (j >= 4))])
        X_act = steps("x_act", [f"exp{j}" for j in tiles], credit=1)
        X_max = steps("x_max", [f"max{j}" for j in tiles])
        X_lo, X_hi = steps("x_lo_t", [f"lo{j}" for j in tiles], credit=1), steps("x_hi_t", [f"hi{j}" for j in tiles if j >= 4], credit=1)
        X_fin = steps("x_fin", [n for j in tiles for n in (f"inv{j}", f"fin{j}")], credit=1)
        W_pe, W_vec = steps("w_pe", ["lo", "hi"]), steps("w_vec", ["lo", "hi"], credit=2)
        G_pe, G_vec = steps("g_pe", ["logits"], credit=1), steps("g_vec", ["logits"], credit=2)
        K_act, K_pe = steps("k_act", ["g_exp", "e_exp"]), steps("k_pe", ["ranks", "starts", "lists"])
        K_vec = steps("k_vec", [
            "g_max", "g_diff", "g_sum", "g_w", "g_miss", "g_cand", "g_first", "g_hot", "g_far", "e_in",
            "m1", "d1", "miss1", "cand1", "i1", "hot1", "rest", "m2", "d2", "miss2", "cand2", "i2", "hot2",
            "picked", "e_diff", "cnt_i", "cnt_up", "cnt_nb", "nb_f", "nb_col", "start_f", "row", "r1", "dest1",
            "r2", "dest2", "dest_i", "blk_i", "blk_f", "slot_f", "hots", "le", "owner", "active", "by_slot",
            "e_den", "e_rden", "w1", "w2", "before", "run_n", "run_slots", "empty", "rows_i",
            "list_i", "owner_i", "cells"])
        M_gu, M_xT, M_dn = steps("m_gu", ["gu"]), steps("m_xT", ["lo", "hi"]), steps("m_dn", ["lo", "hi"])
        M_hT = steps("m_hT", ["hT"])
        M_tanh, M_xlo = steps("m_tanh", ["tanh"]), steps("m_xlo", ["x"])
        M_ylo, M_h = steps("m_ylo", ["y"]), steps("m_h", ["h"])
        M_silu, M_prod = steps("m_silu", ["silu"]), steps("m_prod", ["prod"])
        M_xhi, M_yhi = steps("m_xhi", ["x"]), steps("m_yhi", ["y"])
        M_idx, M_oidx = steps("m_idx", ["idx"]), steps("m_oidx", ["idx"])
        E_comb = steps("e_comb", ["first", "second"], credit=1)
        PT_pe, PT_act = (steps(n, [f"pair{k}" for k in range(TILES // 2)]) for n in ("pt_pe", "pt_act"))
        P_pe, P_act = steps("p_pe", ["e"]), steps("p_act", ["squared", "copied"], credit=2)
        E_pe = steps("e_pe", ["g_lo", "g_hi"], credit=1)
        E_act = steps("e_act", ["t_lo", "t_hi"], credit=1)
        E_pool = steps("e_pool", ["eps", "rstd"])
        E_vec = steps("e_vec", ["e_scaled", "gated"], credit=2)

        def guarded(eng, cond, fn):
            if cond is True:
                fn()
            else:
                with eng.If(cond):
                    fn()

        def step(stages, t):
            for o, fn, *parity in stages:
                if 0 <= t + o < TILES and (t + o) % 2 in (parity or (0, 1)):
                    fn(t + o, (t + o) % 2, (t + o) // 2)

        def lag_loop(eng, stages, before=True, after=True, start=0):
            ahead, behind = max(s[0] for s in stages), -min(s[0] for s in stages)
            for t in range(-ahead, 0):
                if before:
                    step(stages, t)
            with eng.Fori(start, PAIRS) as i:
                for v in range(2):
                    for o, fn, *parity in stages:
                        u, k = (v + o) % 2, (v + o) // 2
                        if u not in (parity or (0, 1)):
                            continue
                        t = (2 * i + (v + o)).with_bounds(min_val=max(v + o, u), max_val=min(2 * PAIRS - 2 + v + o, TILES - 2 + u))
                        cond = True if -start <= k <= 0 else (i < PAIRS - k if k > 0 else i > -k - 1)
                        guarded(eng, cond, lambda: fn(t, u, i + k))
            for t in range(TILES, TILES + behind):
                if after:
                    step(stages, t)

        def handover(mix, norm, project, square, scale, turn, banks_free=None):
            def mla(stage, t):
                for fn in stage:
                    fn(t, t % 2, t // 2)

            step(mix, TILES)
            mla(norm, 0)
            step(mix, TILES + 1)
            mla(norm, 1)
            if banks_free:
                banks_free()
            mla(project, 0)
            mla(square, 0)
            step(mix, TILES + 2)
            mla(project, 1)
            mla(norm, 2)
            mla(scale, 0)
            mla(square, 1)
            mla(project, 2)
            step(mix, TILES + 3)
            mla(turn, 0)
            mla(norm, 3)
            mla(square, 2)
            mla(scale, 1)
            step(mix, TILES + 4)

        def rows_of(src, t, base=0):
            return src[t * P + base:(t + 1) * P + base, :] if isinstance(t, int) else src[bass.ds(t * P + base, P), :]

        def span(x, start, n):
            return x[:, start:start + n] if isinstance(start, int) else x[:, bass.ds(start, n)]

        def block_loop(eng, n, step):
            with eng.Fori(0, MAXB1 // 3) as i:
                def three():
                    for u in range(3):
                        b = 3 * i + (1 + u)
                        step(b, ((1 + u) % 3, i + (u == 2)), ((2 + u) % 3, i + (u >= 1)), (u, i))
                guarded(eng, 3 * i < n, three)

        def settle(eng, passed):
            eng.sem_inc(passed, 1)

        def counters(eng, l, passed):
            eng.wait_ge(*K_vec.after(l, "cells"))
            settle(eng, passed)
            top = 2 * MAXB1
            prev = eng.value_load(cells[0:1, 48:49], min_val=0, max_val=top)
            n = eng.value_load(cells[0:1, 52:53], min_val=0, max_val=MAXB)
            used = [eng.value_load(cells[0:1, 49 + k:50 + k], min_val=0, max_val=top) for k in range(3)]
            return prev, n, used

        block = ctx.enter_context(nc.Block())

        @block.sync
        def _(sp):
            passed = sem("sp_passed")
            for u in range(2):
                sp.sem_inc(qk_stored[u], 32)
                sp.sem_inc(m_stored[u], 16)
                sp.sem_inc(e_stored[u], 16)
            sp.dma_start(pos_raw[:, :], I["positions"][0].rearrange("(t p) -> t p", p=P)).then_inc(pos_loaded, 16)

            def load_h(some, a, b):
                sp.dma_start(h[:, a:b, :], I["x"][0, a * P:b * P, :].rearrange("(t p) d -> p t d", p=P)).then_inc(some, 16)

            def load_w_in(l, *parts):
                for k in parts:
                    cols = w_in_cols[k]
                    sp.dma_start(w_in[:, :, cols], I["w_in"][l, :, cols].rearrange("(k p) n -> p k n", p=P)).then_inc(w_in_loaded[k], 16)

            def load_mix(l):
                sp.dma_start(gains[:, MIX], I["mix_norm_g"][l].partition_broadcast(P)).then_inc(mix_loaded, 16)

            def load_small(l):
                rows = ((V["sgu_g"], I["sgu_ln_g"]), (V["sgu_b"], I["sgu_ln_b"]), (V["cln_g"], I["conv_ln_g"]),
                        (V["cln_b"], I["conv_ln_b"]), (V["pw_b"], I["conv_pw_b"]), (V["qa_g"], I["q_a_norm_g"]),
                        (V["kva_g"], I["kv_a_norm_g"]), (qg[:, :], I["q_norm_g"]), (kg[:, :], I["k_norm_g"]))
                sp.dma_start(ws_raw[:, :, :], I["sgu_w"][l].rearrange("h i j -> i h j")).then_inc(small_loaded, 16)
                sp.dma_start(cw_raw[0:TAPS, :], I["conv_w"][l]).then_inc(small_loaded, 16)
                sp.dma_start(cw_raw[TAPS:TAPS + 1, :], I["conv_b"][l].partition_broadcast(1)).then_inc(small_loaded, 16)
                sp.dma_start(sb_raw[:, :], I["sgu_b"][l]).then_inc(small_loaded, 16)
                for dst, src in rows:
                    sp.dma_start(dst, src[l].partition_broadcast(P)).then_inc(small_loaded, 16)
                sp.dma_start(pw[:, :, :], I["conv_pw_w"][l].rearrange("(k p) n -> p k n", p=P)).then_inc(small_loaded, 16)

            load_h(h_loaded[0], 0, 2)
            load_mix(0)
            load_small(0)
            load_w_in(0, 0)
            load_h(h_loaded[1], 2, TILES)
            load_w_in(0, 1, 2)
            sp.wait_ge(h_loaded[0], 16)
            sp.sem_inc(h_final, 2)
            sp.wait_ge(h_loaded[1], 16)
            sp.sem_inc(h_final, TILES - 2)

            with sp.Fori(0, DEPTH) as l:
                sp.wait_ge(h_final, TILES * l + TILES)
                settle(sp, passed)
                sp.dma_start(w_uq, I["w_uq"][l].rearrange("(k p) n -> p k n", p=P)).then_inc(mla_loaded, 16)
                sp.dma_start(w_ukv, I["w_ukv"][l]).then_inc(mla_loaded, 16)
                with nc.allow_non_contiguous_dma(reason="short rows of the router"):
                    sp.dma_start(w_r[:, :, 0:NG], I["router_group_w"][l].rearrange("(k p) n -> p k n", p=P)).then_inc(late_loaded, 16)
                    sp.dma_start(w_r[:, :, NG:NG + NE], I["router_expert_w"][l].rearrange("(k p) n -> p k n", p=P)).then_inc(late_loaded, 16)
                for dst, src in ((b_r[:, 0:NG], I["router_group_b"]), (b_r[:, NG:NG + NE], I["router_expert_b"])):
                    sp.dma_start(dst, src[l].partition_broadcast(P)).then_inc(late_loaded, 16)

                def store_tile(t, u):
                    g = TILES * l + t
                    sp.wait_ge(*R_act.after(g))
                    settle(sp, passed)
                    sp.wait_ge(*R_vec.after(g))
                    settle(sp, passed)
                    cols = slice(t * P, (t + 1) * P) if isinstance(t, int) else bass.ds(t * P, P)
                    for s in range(2):
                        sp.dma_start(qk_dram[s][:, :, cols], stage[u][0:QK, s]).then_inc(qk_stored[u], 16)

                def load_head(head, u, part):
                    cols = slice(0, EARLY * P) if part == 0 else slice(EARLY * P, SEQ)
                    for s, ring in enumerate((q_ring, k_ring)):
                        sp.dma_start(ring[u][0:QK, cols], qk_dram[s][:, head, cols]).then_inc(qk_loaded[part][u], 16)

                with sp.Fori(0, EARLY // 2) as i:
                    for u in range(2):
                        store_tile(2 * i + u, u)
                for u in range(2):
                    sp.wait_ge(qk_stored[u], 32 * PAIRS * l + (16 * EARLY + 32))
                    settle(sp, passed)
                load_head(0, 0, 0)
                for t in range(EARLY, TILES):
                    store_tile(t, t % 2)
                for u in range(2):
                    sp.wait_ge(qk_stored[u], 32 * PAIRS * l + (32 * PAIRS + 32))
                    settle(sp, passed)
                load_head(0, 0, 1)
                load_head(1, 1, 0)
                load_head(1, 1, 1)
                sp.dma_start(w_o, I["w_o"][l].rearrange("(k p) n -> p k n", p=P)).then_inc(wo_loaded, 16)
                for dst, src in ((gains[:, BRANCH], I["branch_norm_g"]), (gains[:, FFN], I["ffn_norm_g"])):
                    sp.dma_start(dst, src[l].partition_broadcast(P)).then_inc(late_loaded, 16)
                with sp.Fori(0, HEADS // 2 - 1) as i:
                    for u in range(2):
                        sp.wait_ge(*S_pe.after(HEADS * l + 2 * i + u))
                        for part in range(2):
                            load_head(2 * i + (2 + u), u, part)
                sp.wait_ge(*S_pe.after(HEADS * l + (HEADS - 1)))
                sp.dma_start(ple_p, I["ple_proj_w"][l].rearrange("(k p) n -> p k n", p=P)).then_inc(proj_loaded, 16)
                def load_p():
                    sp.wait_ge(*FX.a.before(24 * l + 2 * TILES))
                    settle(sp, passed)
                    sp.dma_start(p_all, I["p"][l, 0].rearrange("(t p) d -> p t d", p=P)).then_inc(p_loaded, 16)

                with sp.Fori(0, PAIRS) as i:
                    guarded(sp, i > PAIRS - 2, load_p)
                    for u in range(2):
                        sp.wait_ge(*FM.a.after(TILES * l + 2 * i + u))
                        sp.dma_start(m_dram[bass.ds((2 * i + u) * P, P), :], m_buf[u]).then_inc(m_stored[u], 16)

                sp.wait_ge(*W_pe.before(TILES * l + TILES))
                sp.dma_start(ple_g, I["ple_gate_w"][l].rearrange("(k p) n -> p k n", p=P)).then_inc(ple_loaded, 16)
                sp.dma_start(gains[:, BRANCH], I["ple_post_norm_g"][l].partition_broadcast(P)).then_inc(ple_loaded, 16)
                sp.dma_start(gains[:, MIX], I["ple_norm_g"][l].partition_broadcast(P)).then_inc(ple_loaded, 16)
                for u in range(2):
                    sp.wait_ge(m_stored[u], 16 * PAIRS * l + (16 * PAIRS + 16))
                settle(sp, passed)
                prev, n, used = counters(sp, l, passed)

                def load_gu(b, s):
                    e = sp.value_load(cells[0:1, bass.ds(b, 1)] if not isinstance(b, int) else cells[0:1, b:b + 1], min_val=0, max_val=NE - 1)
                    sp.dma_start(w_gu[s][:, :, 0:F], I["moe_w_gate"][l, e].rearrange("(k p) f -> p k f", p=P)).then_inc(gu_loaded[s], 16)
                    sp.dma_start(w_gu[s][:, :, F:2 * F], I["moe_w_up"][l, e].rearrange("(k p) f -> p k f", p=P)).then_inc(gu_loaded[s], 16)
                    return e

                def load_dn(e, s):
                    sp.dma_start(w_dn[s], I["moe_w_down"][l, e].rearrange("(k p) f -> p k f", p=P)).then_inc(dn_loaded[s], 16)

                for b in range(3):
                    if b == 1:
                        for u in range(2):
                            sp.wait_ge(e_stored[u], 16 * PAIRS * l + 16 * PAIRS + 16)
                        settle(sp, passed)
                    load_dn(load_gu(b, b), b)

                def weights(b, here, nxt, last):
                    def go():
                        sp.wait_ge(*M_gu.after(prev + b - 1))
                        e = load_gu(b + 2, last[0])
                        sp.wait_ge(*M_dn.after(prev + b - 1))
                        load_dn(e, last[0])
                    guarded(sp, b + 2 < n, go)

                block_loop(sp, n, weights)

                sp.wait_ge(y_stored, (prev + n) * 16)
                settle(sp, passed)

                def fetch(t, u, i):
                    sp.wait_ge(*E_comb.after(TILES * l + t - 2))
                    settle(sp, passed)
                    for k in range(2):
                        sp.dma_start(y_got[u][k], rows_of(y_rows, t, k * SEQ)).then_inc(y_fetched[u], 16)

                def fetch_e(t, u, i):
                    sp.wait_ge(*E_vec.after(TILES * l + t - 2, "e_scaled"))
                    settle(sp, passed)
                    sp.dma_start(e_got[u], rows_of(e_dram, t)).then_inc(e_fetched[u], 16)

                def prefetch(t, u, i):
                    def part(k):
                        if k < 3:
                            sp.wait_ge(blocks_done, l + 1)
                            settle(sp, passed)
                            load_w_in((l + 1).with_bounds(max_val=DEPTH - 1), k)
                        else:
                            load_small((l + 1).with_bounds(max_val=DEPTH - 1))

                    for k in range(PAIRS):
                        guarded(sp, l < DEPTH - 1, lambda: guarded(sp, i < k + 1, lambda: guarded(
                            sp, i > k - 1 if k else True, lambda: part(k))))

                lag_loop(sp, [(3, fetch), (1, fetch_e), (0, prefetch, 0)])

                def next_mix():
                    sp.wait_ge(*FX.a.before(24 * l + 24))
                    settle(sp, passed)
                    load_mix((l + 1).with_bounds(max_val=DEPTH - 1))

                guarded(sp, l < DEPTH - 1, next_mix)

            with sp.Fori(0, TILES) as t:
                sp.wait_ge(h_final, TILES * DEPTH + t + 1)
                sp.dma_start(out[0, bass.ds(t * P, P), :], h[:, t, :]).then_inc(out_stored, 16)
            sp.wait_ge(out_stored, 16 * TILES)

        N_SMALL, N_LATE = 16 * 14, 16 * 6

        @block.gpsimd
        def _(gp):
            passed = sem("gp_passed")
            for s in (CP_pool, C_pool, FX.pool, FM.pool):
                gp.sem_inc(s.sem, s.per * s.credit)
            for ap, val in ((ident, 0.0), (tri_b, 0.0), (mask_b, 0.0), (ones_b, 1.0), (neg_half, -0.5)):
                nc.gpsimd.memset(ap[:, :], val)
            nc.gpsimd.memset(eps_y[:, 0:1], 4 * EPS)
            nc.gpsimd.memset(eps_y[:, 1:3], EPS)
            nc.gpsimd.iota(iota[:, :], pattern=[[1, P]], base=0, channel_multiplier=0, allow_small_or_imprecise_dtypes=True)
            nc.gpsimd.iota(padding[:, :], pattern=[[1, 1]], base=2 * SEQ + 1, channel_multiplier=1,
                           allow_small_or_imprecise_dtypes=True)
            nc.gpsimd.iota(token[:, :, :], pattern=[[P, TILES], [SEQ, 2]], base=1, channel_multiplier=1,
                           allow_small_or_imprecise_dtypes=True).then_inc(*S_pool0.next("memsets"))
            gp.wait_ge(*S_pool0.after(0, "memsets"))
            nc.gpsimd.affine_select(out=ident[:, :], in_=ident[:, :], pattern=[[-1, P]], compare_op=ALU.not_equal,
                                    fill=1.0, base=0, channel_multiplier=1)
            nc.gpsimd.affine_select(out=tri_b[:, :], in_=tri_b[:, :], pattern=[[-1, P]], compare_op=ALU.is_ge,
                                    fill=1.0, base=0, channel_multiplier=1)
            nc.gpsimd.affine_select(out=mask_b[:, :], in_=mask_b[:, :], pattern=[[-1, P]], compare_op=ALU.is_ge,
                                    fill=-BIG, base=0, channel_multiplier=1).then_inc(*S_pool0.next("selects"))

            def rsqrt(dst, tmp, src, n, eps, own, index, first, second, mul=1.0):
                gp.wait_ge(*own.before(index))
                settle(gp, passed)
                if isinstance(eps, float):
                    i = nc.gpsimd.tensor_scalar(tmp, src, mul, eps, ALU.mult, ALU.add)
                else:
                    i = nc.gpsimd.tensor_tensor(tmp, src, eps, ALU.add)
                i.then_inc(*own.next(first))
                gp.wait_ge(*own.after(index, first))
                nc.gpsimd.tensor_tensor(dst, tmp, neg_half[:, 0:n], ALU.pow).then_inc(*own.next(second))

            with gp.Fori(0, DEPTH) as l:
                gp.wait_ge(small_loaded, N_SMALL * l + N_SMALL)
                settle(gp, passed)
                nc.gpsimd.affine_select(out=ws_raw[:, :, :], in_=ws_raw[:, :, :], pattern=[[0, GROUPS], [-1, P]],
                                        compare_op=ALU.is_ge, fill=0.0, base=0,
                                        channel_multiplier=1).then_inc(*L_pool.next("sgu_masked"))

                def norm(ph):
                    def go(t, u, i):
                        r = 24 * l + t + 8 * ph
                        n = 3 if ph == 1 else 1
                        gp.wait_ge(*FX.square.after(r))
                        rsqrt(rstd[:, u, 0:n], pool_t[:, 0:n], ms[:, u, 0:n], n, eps_y[:, 0:3] if ph == 1 else EPS,
                              FX.pool, r, "eps", "rstd")
                    return go

                def norm_m(t, u, i):
                    g = TILES * l + t
                    gp.wait_ge(*FM.square.after(g))
                    rsqrt(rstd_m[:, u:u + 1], pool_m[:, 0:1], ms_m[:, u:u + 1], 1, EPS, FM.pool, g, "eps", "rstd")

                def sgu_rstd(t, u, i):
                    g = TILES * l + t
                    gp.wait_ge(*V_vec.after(g, "v_sumsq"))
                    rsqrt(st_v[:, 4, :], st_v[:, 3, :], st_v[:, 2, :], GROUPS, 4 * EPS, Z_pool, g, "v_eps", "v_rstd", 1.0 / HEAD)

                def conv_rstd(t, u, i):
                    g = TILES * l + t
                    gp.wait_ge(*C_vec.after(g, "c_sumsq"))
                    rsqrt(st_c[:, 4, :], st_c[:, 3, :], st_c[:, 2, :], GROUPS, EPS, C_pool, g, "c_eps", "c_rstd", 1.0 / HEAD)

                def conv_sums(t, u, i):
                    q = TILES * l + t
                    gp.wait_ge(*CT_vec.before(q))
                    for k in range(2, SPLIT + 1):
                        one = product_ring[0] if k == 2 else acc_pool
                        if k > 2:
                            gp.wait_ge(*CP_pool.after(q, f"sum{k - 1}"))
                        gp.wait_ge(*CP_act.after(q, f"product{k}"))
                        nc.gpsimd.tensor_tensor(acc_pool, one, product_ring[(k - 1) % 3], ALU.add).then_inc(*CP_pool.next(f"sum{k}"))

                mix = [(-4, conv_rstd), (2, norm(0)), (-2, conv_sums), (0, sgu_rstd)]
                lag_loop(gp, mix, after=False)

                def c_rstd(t, u, i):
                    g = TILES * l + t
                    gp.wait_ge(*QC_act.after(g))
                    gp.wait_ge(*QC_vec.before(g))
                    rsqrt(r_c[:, :], t_c[:, :], m_c[:, :], 3, EPS, QC_pool, g, "eps", "rstd")

                def qk_rstd(t, u, i):
                    g = TILES * l + t
                    gp.wait_ge(*QM_vec.after(g))
                    rsqrt(r_qk[:, u, :], t_qk[:, :], m_qk[:, :], 24, EPS, QM_pool, g, "eps", "rstd")

                mla = [(2, c_rstd), (1, qk_rstd)]
                handover(mix, [c_rstd], [], [qk_rstd], [], [])
                lag_loop(gp, mla, before=False, start=1)

                lag_loop(gp, [(-1, norm_m), (2, norm(1))])

                prev, n, used = counters(gp, l, passed)
                for u in range(2):
                    gp.wait_ge(m_stored[u], 16 * PAIRS * l + (16 * PAIRS + 16))
                    settle(gp, passed)

                def gather(b, s, m):
                    col = idx[:, b:b + 1] if isinstance(b, int) else idx[:, bass.ds(b, 1)]
                    nc.gpsimd.tensor_copy(idx_ring[:, s:s + 1], col).then_inc(*M_idx.next("idx"))
                    gp.wait_ge(*M_idx.after(m))
                    settle(gp, passed)
                    nc.gpsimd.indirect_dma_start(
                        out=x_blk[s], out_offset=None, in_=m_dram,
                        in_offset=bass.IndirectOffsetOnAxis(ap=idx_ring[:, s:s + 1], axis=0)).then_inc(x_gathered[s], 16)

                gather(0, 0, prev)
                gather(1, 1, prev + 1)
                gather(2, 2, prev + 2)

                gp.wait_ge(*P_act.before(TILES * l + TILES))
                rsqrt(m_e[:, 2, :], m_e[:, 1, :], m_e[:, 0, :], TILES, 4 * EPS, E_pool, l, "eps", "rstd")

                def rows(b, here, nxt, last):
                    def ahead():
                        gp.wait_ge(*M_xT.after(prev + b - 1))
                        settle(gp, passed)
                        gather(b + 2, last[0], prev + b + 2)

                    def store():
                        gp.wait_ge(*M_ylo.after(prev + b - 1))
                        gp.wait_ge(*M_yhi.after(prev + b - 1))
                        settle(gp, passed)
                        nc.gpsimd.tensor_copy(out_ring[:, :], out_idx[:, bass.ds(b - 1, 1)]).then_inc(*M_oidx.next("idx"))
                        gp.wait_ge(*M_oidx.after(prev + b - 1))
                        settle(gp, passed)
                        nc.gpsimd.indirect_dma_start(
                            out=y_rows, out_offset=bass.IndirectOffsetOnAxis(ap=out_ring[:, 0:1], axis=0),
                            in_=y_blk, in_offset=None).then_inc(y_stored, 16)
                    guarded(gp, b + 2 < n, ahead)
                    guarded(gp, b <= n, store)

                block_loop(gp, n, rows)
                lag_loop(gp, [(2, norm(2))])

        @block.scalar
        def _(act):
            passed = sem("act_passed")
            for s in (P_act, X_act, X_hi, CP_act, E_act, ZC_act, C_act, R_act, FX.lo, FM.lo, FX.square, FM.square):
                act.sem_inc(s.sem, s.per * s.credit)
            act.wait_ge(*S_vec0.after(0, "cosarg"))
            nc.scalar.activation(sin[:, :, :], sin[:, :, :], ACT.Sin).then_inc(*S_act0.next("sin"))
            nc.scalar.activation(cos[:, :, :], cos[:, :, :], ACT.Sin).then_inc(*S_act0.next("cos"))

            with act.Fori(0, DEPTH) as l:
                act.wait_ge(*L_pe.after(l))
                nc.scalar.copy(wsT[:, :, :], bank(7).rearrange("p (h i) -> p h i", h=GROUPS))
                nc.scalar.activation(cw[:, :, 0:TAPS], bank(6, 0, 64).rearrange("p (c k) -> p c k", c=2)[:, :, 0:TAPS],
                                     ACT.Copy, scale=0.5)
                nc.scalar.copy(cw[:, :, TAPS:32], bank(6, 0, 64).rearrange("p (c k) -> p c k", c=2)[:, :, TAPS:32])
                nc.scalar.copy(s_bias[:, :], bank(6, 64, 64 + GROUPS)).then_inc(*L_act.next("prep_evac"))

                def norm(ph):
                    def go(t, u, i):
                        g = TILES * l + t
                        if ph == 0:
                            act.wait_ge(h_final, g + 1)
                        elif ph == 2:
                            act.wait_ge(*E_comb.after(g))
                        act.wait_ge(*FX.square.before(24 * l + t + 8 * ph))
                        if ph == 1:
                            for k, (a, b) in enumerate(((0, 256), (256, 512), (512, 1024))):
                                i = nc.scalar.activation(junk[:, a:b], y[:, t, a:b], ACT.Square, scale=float(b - a) ** -0.5,
                                                         accum_out=ms[:, u, k:k + 1])
                        else:
                            i = nc.scalar.activation(junk[:, :], h[:, t, :], ACT.Square, scale=float(D) ** -0.5,
                                                     accum_out=ms[:, u, 0:1])
                        i.then_inc(*FX.square.next("squared"))
                    return go

                def norm_m(t, u, i):
                    act.wait_ge(*W_vec.after(TILES * l + t))
                    act.wait_ge(*FM.square.before(TILES * l + t))
                    nc.scalar.activation(junk_m, h[:, t, :], ACT.Square, scale=float(D) ** -0.5,
                                         accum_out=ms_m[:, u:u + 1]).then_inc(*FM.square.next("squared"))

                def turn(ph):
                    def go(t, u, i):
                        act.wait_ge(*FX.pe.after(24 * l + t + 8 * ph, "T_lo"))
                        nc.scalar.copy(aT[u][:, 0:4, :].rearrange("p a b -> p (a b)"), bank(0)).then_inc(*FX.lo.next("aT"))
                    return go

                def turn_m(t, u, i):
                    act.wait_ge(*FM.pe.after(TILES * l + t, "T_lo"))
                    nc.scalar.copy(mT[:, 0:4, :].rearrange("p a b -> p (a b)"), bank(6)).then_inc(*FM.lo.next("aT"))

                def z_square(t, u, i):
                    act.wait_ge(*Z_pe.after(TILES * l + t, "z_sgu"))
                    nc.scalar.activation(sg_t, bank(2), ACT.Square, scale=GELU_A ** 0.5).then_inc(*Z_act.next("sgu_square"))

                def z_tanh(t, u, i):
                    g = TILES * l + t
                    act.wait_ge(*Z_vec.after(g, "sgu_cubic"))
                    nc.scalar.activation(sg_t, sg_t, ACT.Tanh, scale=GELU_C).then_inc(*Z_act.next("sgu_tanh"))
                    act.wait_ge(*Z_pe.after(g, "z_glu"))
                    nc.scalar.activation(gl_t, bank(3, SGU, 2 * SGU), ACT.Tanh, scale=0.5).then_inc(*Z_act.next("glu_tanh"))

                def z_mla(t, u, i):
                    act.wait_ge(*Z_pe.after(TILES * l + t, "z_mla"))
                    nc.scalar.copy(zc[:, t, :], bank(4, 0, MLA_IN)).then_inc(*Z_act.next("mla_copied"))

                def c_tanh(t, u, i):
                    act.wait_ge(*C_vec.after(TILES * l + t, "c_normed"))
                    nc.scalar.activation(c_th, c_n.rearrange("p a b -> p (a b)"), ACT.Tanh, scale=0.5).then_inc(*C_act.next("c_tanh"))

                def z_cin(t, u, i):
                    act.wait_ge(*ZG_pe.after(TILES * l + t, "gluT"))
                    for c in range(2):
                        nc.scalar.copy(span(cin[c], t * P + (TAPS - 1), P), bank(6, P * c, P * c + P)).then_inc(*ZC_act.next(f"cin{c}"))

                def conv_products(t, u, i):
                    q = TILES * l + t
                    act.wait_ge(*ZC_act.after(q + (1 - u), f"cin{u}"))
                    for k in range(1, SPLIT + 1):
                        if k <= 3:
                            act.wait_ge(*CP_pool.before(q))
                        else:
                            act.wait_ge(*CP_pool.after(q, f"sum{max(k - 3, 2)}"))
                        settle(act, passed)
                        nc.scalar.activation(product_ring[(k - 1) % 3], span(cin[u], (t - u) * P + k, 2 * P), ACT.Copy,
                                             scale=cw[:, u, k:k + 1]).then_inc(*CP_act.next(f"product{k}"))

                def c_yT_evac(t, u, i):
                    act.wait_ge(*CY_pe.after(TILES * l + t, "ybT"))
                    nc.scalar.copy(c_yT.rearrange("p a b -> p (a b)"), bank(6, 2 * P, 4 * P)).then_inc(*C_act.next("ybT_evac"))

                mix = [(1, turn(0)), (-1, z_cin), (2, norm(0)), (-2, conv_products), (0, z_square), (-4, c_tanh), (0, z_tanh), (0, z_mla),
                       (-4, c_yT_evac)]
                lag_loop(act, mix, after=False)

                def heads_view(b, lo, hi, width):
                    return ps[:, b:b + 2, 0:HC * width].rearrange("p a (h d) -> p a h d", h=HC)[:, :, :, lo:hi]

                def fold(ap):
                    return ap.rearrange("p (a h) d -> p a h d", a=2)

                act.wait_ge(*Z_act.before(TILES * l + TILES))
                settle(act, passed)

                def c_square(t, u, i):
                    g = TILES * l + t
                    act.wait_ge(*QC_act.before(g))
                    act.wait_ge(*QC_pool.before(g))
                    c0 = 0
                    for k, n in enumerate((QR, KVR, ROPE)):
                        ins = nc.scalar.activation(junk[:, c0:c0 + n], zc[:, t, c0:c0 + n], ACT.Square, scale=float(n) ** -0.5,
                                                   accum_out=m_c[:, k:k + 1])
                        c0 += n
                    ins.then_inc(*QC_act.next("squared"))

                def q_cnT(t, u, i):
                    act.wait_ge(*QM_pe.after(TILES * l + t, "cT"))
                    nc.scalar.copy(cnT.rearrange("p a b -> p (a b)"), bank(1, 0, 3 * P)).then_inc(*QT_act.next("cnT"))

                def q_main(t, u, i):
                    g = TILES * l + t
                    act.wait_ge(*QM_vec.before(g))
                    act.wait_ge(*QM_pe.after(g, "q_mm"))
                    nc.scalar.activation(fold(qk_sq)[:, :, :, 0:HEAD], heads_view(2, 0, HEAD, QK), ACT.Square, scale=float(HEAD) ** -0.5)
                    nc.scalar.activation(fold(qk_sq)[:, :, :, HEAD:QK], heads_view(2, HEAD, QK, QK), ACT.Square, scale=float(ROPE) ** -0.5)
                    act.wait_ge(*QM_pe.after(g, "kv_mm"))
                    nc.scalar.activation(fold(k_sq), heads_view(4, 0, HEAD, P), ACT.Square,
                                         scale=float(HEAD) ** -0.5).then_inc(*QM_act.next("squared"))
                    nc.scalar.copy(vals[:, t].rearrange("p (a h) d -> p a h d", a=2),
                                   heads_view(4, HEAD, P, P)).then_inc(*QM_act.next("v_stored"))

                def q_raw(t, u, i):
                    act.wait_ge(*R_pe.after(TILES * l + t - 2))
                    settle(act, passed)
                    nc.scalar.copy(fold(qs[u]), heads_view(2, 0, QK, QK))
                    nc.scalar.copy(fold(ks[u])[:, :, :, 0:HEAD], heads_view(4, 0, HEAD, P)).then_inc(*QM_raw.next("raw"))

                def q_turned(t, u, i):
                    g = TILES * l + t
                    act.wait_ge(qk_stored[u], 32 * (PAIRS * l + i) + 32)
                    act.wait_ge(*R_pe.after(g, "q_lo"))
                    nc.scalar.copy(stage[u][0:QK, 0, 0:HC].rearrange("p a b -> p (a b)"), ps[0:QK, 0, :]).then_inc(*R_act.next("q_lo"))
                    act.wait_ge(*R_pe.after(g, "k_lo"))
                    nc.scalar.copy(stage[u][0:QK, 1, 0:HC].rearrange("p a b -> p (a b)"), ps[0:QK, 0, :]).then_inc(*R_act.next("k_lo"))

                mla = [(1, q_cnT), (2, c_square), (1, q_main), (-1, q_turned), (1, q_raw)]
                handover(mix, [c_square], [q_cnT], [q_main, q_raw], [], [q_turned])
                lag_loop(act, mla, before=False, start=1)

                def prob_hi(hh, j):
                    if j >= 4:
                        act.wait_ge(*T_pe.after(hh, f"hi{j}"))
                        nc.scalar.copy(prob_t[j % 2][:, 4:j + 1], bank(5, 0, (j - 3) * P).rearrange("p (k q) -> p k q", q=P)
                                       ).then_inc(*X_hi.next(f"hi{j}"))

                def exps(hh, j):
                    n = (j + 1) * P
                    act.wait_ge(*X_max.after(hh, f"max{j}"))
                    nc.scalar.activation(prob[j % 2][:, 0:n], banks(2 * (j % 2))[:, 0:n], ACT.Exp, bias=neg_max[:, j % 2:j % 2 + 1],
                                         accum_out=denom[:, j:j + 1]).then_inc(*X_act.next(f"exp{j}"))

                with act.Fori(0, HEADS // 2) as i:
                    for n in range(2 * TILES):
                        u, j = divmod(n, TILES)
                        if n:
                            prob_hi(HEADS * l + 2 * i + (n - 1) // TILES, (n - 1) % TILES)
                        exps(HEADS * l + 2 * i + u, j)
                    prob_hi(HEADS * l + 2 * i + 1, TILES - 1)

                act.wait_ge(*X_fin.before(HEADS * l + HEADS))
                settle(act, passed)
                lag_loop(act, [(-1, norm_m), (2, norm(1)), (1, turn(1)), (-1, turn_m)])
                act.wait_ge(*K_vec.after(l, "g_diff"))
                nc.scalar.activation(rs(1, TILES, NG), rs(0, TILES, NG), ACT.Exp).then_inc(*K_act.next("g_exp"))

                def project(i):
                    for u in range(2):
                        g = TILES * l + (2 * i + u)
                        act.wait_ge(*P_pe.after(g))
                        act.wait_ge(*P_act.after(g - 1, "squared"))
                        nc.scalar.activation(junk[:, :], banks(2 + 2 * u), ACT.Square, scale=2 * float(D) ** -0.5,
                                             accum_out=m_e[:, 0, 2 * i + u:2 * i + u + 1]).then_inc(*P_act.next("squared"))
                        act.wait_ge(e_stored[u], 16 * PAIRS * l + 16 * i + 16)
                        nc.scalar.copy(e_out[u], banks(2 + 2 * u)).then_inc(*P_act.next("copied"))
                        act.wait_ge(*P_act.after(g, "copied"))
                        settle(act, passed)
                        act.dma_start(rows_of(e_dram, 2 * i + u), e_out[u]).then_inc(e_stored[u], 16)

                act.wait_ge(*FX.square.before(24 * l + 2 * TILES))
                for k in range(PAIRS):
                    act.wait_ge(*PT_pe.after(l, f"pair{k}"))
                    nc.scalar.copy(pT[:, k].rearrange("p a b c -> p (a b c)"), bank(k % 2)).then_inc(*PT_act.next(f"pair{k}"))
                project(0)
                act.wait_ge(*K_vec.after(l, "e_diff"))
                nc.scalar.activation(rs(9, 2, TILES)[:, 1], rs(9, 2, TILES)[:, 0], ACT.Exp).then_inc(*K_act.next("e_exp"))
                for i in range(1, PAIRS):
                    project(i)

                prev, n, used = counters(act, l, passed)

                def x_lo(m):
                    act.wait_ge(*M_xT.after(m, "lo"))
                    nc.scalar.copy(xT[:, 0:4].rearrange("p a b -> p (a b)"), bank(0)).then_inc(*M_xlo.next("x"))

                def tanh(m):
                    act.wait_ge(*M_gu.after(m))
                    nc.scalar.activation(hid_g, bank(2, 0, F), ACT.Tanh, scale=0.5).then_inc(*M_tanh.next("tanh"))

                def h_evac(m):
                    act.wait_ge(*M_hT.after(m))
                    nc.scalar.copy(hid_t.rearrange("p a b -> p (a b)"), bank(3, 0, 2 * P)).then_inc(*M_h.next("h"))

                def y_lo(m):
                    act.wait_ge(y_stored, m * 16)
                    act.wait_ge(*M_dn.after(m, "lo"))
                    nc.scalar.copy(y_blk[:, 0:512], bank(4)).then_inc(*M_ylo.next("y"))

                x_lo(prev)
                tanh(prev)
                x_lo(prev + 1)
                h_evac(prev)

                def expert(b, here, nxt, last):
                    m = prev + b
                    guarded(act, b < n, lambda: tanh(m))
                    guarded(act, b + 1 < n, lambda: x_lo(m + 1))
                    guarded(act, b <= n, lambda: y_lo(m - 1))
                    guarded(act, b < n, lambda: h_evac(m))

                block_loop(act, n, expert)

                def ple_main(t, u, i):
                    g = TILES * l + t
                    act.wait_ge(*E_vec.before(g))
                    act.wait_ge(*E_pe.after(g, "g_lo"))
                    nc.scalar.activation(gate_t[:, 0:512], bank(2), ACT.Tanh, scale=0.5).then_inc(*E_act.next("t_lo"))
                    act.wait_ge(*E_pe.after(g, "g_hi"))
                    nc.scalar.activation(gate_t[:, 512:1024], bank(3), ACT.Tanh, scale=0.5).then_inc(*E_act.next("t_hi"))

                lag_loop(act, [(2, norm(2)), (1, turn(2)), (0, ple_main)])

        @block.vector
        def _(v):
            passed = sem("v_passed")
            for s in (X_lo, X_fin, W_vec, G_vec, E_comb, E_vec, Z_vec, V_vec, ZS_vec, CT_vec, C_vec, CY_vec, Q_vec, R_vec, FX.hi, FM.hi, FX.a, FM.a):
                v.sem_inc(s.sem, s.per * s.credit)

            def wide(ap, axis, *shape):
                return ap.unsqueeze(axis).to_broadcast([P, *shape])

            def link0(ins, name):
                ins.then_inc(*S_vec0.next(name))
                v.wait_ge(*S_vec0.after(0, name))

            ang, turns = at(B, T0, TILES, HR), at(B, T0 + 128, TILES, HR)
            freq, pos_cols, pos_f = at(B, T0 + 256, HR), at(B, T0 + 272, TILES), at(B, T0 + 280, P)[0:TILES]
            inv_freq = (ROPE_THETA ** (-np.arange(0, ROPE, 2, dtype=np.float64) / ROPE)).astype(np.float32)
            v.memset(run[:, :], 0.0)
            for k in range(HR):
                v.memset(freq[:, k:k + 1], float(inv_freq[k]))
            v.wait_ge(*S_pool0.after(0, "selects"))
            link0(v.tensor_copy(ident_b[:, :], ident[:, :]), "casts")
            v.wait_ge(pos_loaded, 16)
            v.tensor_copy(pos_f, pos_raw[:, :]).then_inc(*S_vec0.next("pos"))
            v.wait_ge(*S_pe0.after(0))
            link0(v.tensor_copy(pos_cols, bank(0, 0, TILES)), "cols")
            link0(v.tensor_tensor(ang, wide(pos_cols, 2, TILES, HR), wide(freq, 1, TILES, HR), ALU.mult), "ang")
            link0(v.tensor_scalar(turns, ang, 1 / (2 * np.pi), ROUND, ALU.mult, ALU.add), "turns")
            link0(v.tensor_scalar(turns, turns, ROUND, None, ALU.subtract), "whole")
            link0(v.scalar_tensor_tensor(ang, turns, -TWO_PI_HI, ang, ALU.mult, ALU.add), "r_hi")
            link0(v.scalar_tensor_tensor(ang, turns, -TWO_PI_MID, ang, ALU.mult, ALU.add), "r_mid")
            link0(v.scalar_tensor_tensor(ang, turns, -TWO_PI_LO, ang, ALU.mult, ALU.add), "r_lo")
            link0(v.tensor_scalar(sin[:, :, :], ang, 3.1415925, -3.1415925, ALU.min, ALU.max), "clamped")
            link0(v.tensor_scalar(cos[:, :, :], sin[:, :, :], -1.0, None, ALU.mult), "neg")
            link0(v.tensor_tensor(cos[:, :, :], cos[:, :, :], sin[:, :, :], ALU.max), "abs")
            v.tensor_scalar(cos[:, :, :], cos[:, :, :], -1.0, np.pi / 2, ALU.mult, ALU.add).then_inc(*S_vec0.next("cosarg"))

            with v.Fori(0, DEPTH) as l:
                v.wait_ge(small_loaded, N_SMALL * l + N_SMALL)
                v.wait_ge(mix_loaded, 16 * l + 16)
                for c in range(2):
                    ins = v.memset(cin[c][:, 0:TAPS - 1], 0.0)
                ins.then_inc(*L_vec.next("cin_zero"))
                v.tensor_scalar(gq[:, HEAD:QK], qg[:, HEAD:QK], SCALE, None, ALU.mult).then_inc(*L_vec.next("gq_pe"))
                v.scalar_tensor_tensor(gq[:, 0:HEAD], qg[:, 0:HEAD], SCALE, kg[:, 0:HEAD], ALU.mult,
                                       ALU.mult).then_inc(*L_vec.next("gq_nope"))
                v.wait_ge(*L_vec.after(l))
                v.wait_ge(*L_act.after(l))

                def norm(ph):
                    def go(t, u, i):
                        r = 24 * l + t + 8 * ph
                        v.wait_ge(*FX.pool.after(r, "rstd"))
                        cuts = (0, 256, 512, 1024) if ph == 1 else (0, D)
                        src = y if ph == 1 else h
                        for k, (a, b) in enumerate(zip(cuts, cuts[1:])):
                            ins = v.scalar_tensor_tensor(a_buf[u][:, a:b], src[:, t, a:b], rstd[:, u, k:k + 1],
                                                         gains[:, BRANCH if ph == 1 else MIX, a:b], ALU.mult, ALU.mult)
                        ins.then_inc(*FX.a.next("a"))
                    return go

                def norm_m(t, u, i):
                    v.wait_ge(*FM.pool.after(TILES * l + t, "rstd"))
                    v.wait_ge(m_stored[u], 16 * (PAIRS * l + i) + 16)
                    v.scalar_tensor_tensor(m_buf[u], h[:, t, :], rstd_m[:, u:u + 1], gains[:, FFN], ALU.mult,
                                           ALU.mult).then_inc(*FM.a.next("a"))

                def turn(ph):
                    def go(t, u, i):
                        v.wait_ge(*FX.pe.after(24 * l + t + 8 * ph, "T_hi"))
                        v.tensor_copy(aT[u][:, 4:8, :].rearrange("p a b -> p (a b)"), bank(1)).then_inc(*FX.hi.next("aT"))
                    return go

                def turn_m(t, u, i):
                    v.wait_ge(*FM.pe.after(TILES * l + t, "T_hi"))
                    v.tensor_copy(mT[:, 4:8, :].rearrange("p a b -> p (a b)"), bank(7)).then_inc(*FM.hi.next("aT"))

                def conv(t, u, i):
                    q = TILES * l + t
                    v.wait_ge(*ZC_act.after(q + (1 - u), f"cin{u}"))
                    v.wait_ge(*CO_pe.before(PAIRS * l + i))
                    for n, k in enumerate(vec_taps):
                        dst = (acc[u], acc_odd)[n % 2]
                        src = span(cin[u], (t - u) * P + k, 2 * P)
                        if n == 0:
                            ins = v.tensor_scalar(dst, src, cw[:, u, 0:1], cw[:, u, TAPS:TAPS + 1], ALU.mult, ALU.add)
                        elif n == 1:
                            ins = v.tensor_scalar(dst, src, cw[:, u, k:k + 1], None, ALU.mult)
                        else:
                            v.wait_ge(*CT_vec.after(q, f"tap{vec_taps[n - 2]}"))
                            ins = v.scalar_tensor_tensor(dst, src, cw[:, u, k:k + 1], dst, ALU.mult, ALU.add)
                        ins.then_inc(*CT_vec.next(f"tap{k}"))
                    v.wait_ge(*CT_vec.after(q, f"tap{TAPS - 1}"))
                    v.tensor_tensor(acc[u], acc[u], acc_odd, ALU.add).then_inc(*CT_vec.next("joined"))
                    v.wait_ge(*CT_vec.after(q, "joined"))
                    v.wait_ge(*CP_pool.after(q))
                    v.tensor_tensor(acc[u], acc[u], acc_pool, ALU.add).then_inc(*CT_vec.next("merged"))

                def gelu_cubic(t, u, i):
                    g = TILES * l + t
                    v.wait_ge(*Z_act.after(g, "sgu_square"))
                    v.scalar_tensor_tensor(sg_t, sg_t, 1.0, bank(2), ALU.add, ALU.mult).then_inc(*Z_vec.next("sgu_cubic"))

                def gelu_glu(t, u, i):
                    g = TILES * l + t
                    v.wait_ge(*Z_act.after(g, "sgu_tanh"))
                    v.scalar_tensor_tensor(sg_uv, sg_t, 1.0, bank(2), ALU.add, ALU.mult).then_inc(*Z_vec.next("sgu_gated"))
                    v.wait_ge(*Z_act.after(g, "glu_tanh"))
                    v.scalar_tensor_tensor(gl, gl_t, 1.0, bank(3, 0, SGU), ALU.add, ALU.mult).then_inc(*Z_vec.next("glu"))

                def centre(src, st, centred, squared, link, p):
                    link(v.tensor_reduce(st[:, 0, :], src, AX.X, ALU.add), p + "_sum")
                    link(v.tensor_scalar(st[:, 1, :], st[:, 0, :], 1.0 / HEAD, None, ALU.mult), p + "_mean")
                    link(v.tensor_tensor(centred, src, wide(st[:, 1, :], 2, GROUPS, HEAD), ALU.subtract), p + "_centred")
                    link(v.tensor_tensor(squared, centred, centred, ALU.mult), p + "_squared")
                    v.tensor_reduce(st[:, 2, :], squared, AX.X, ALU.add).then_inc(*{"v": V_vec, "c": C_vec}[p].next(p + "_sumsq"))

                def scaled(st, centred, dst, gain, bias, link, p, last):
                    link(v.tensor_tensor(dst, centred, wide(st[:, 4, :], 2, GROUPS, HEAD), ALU.mult), p + "_scaled")
                    flat = dst.rearrange("p a b -> p (a b)")
                    link(v.tensor_tensor(flat, flat, V[gain], ALU.mult), p + "_gained")
                    v.tensor_tensor(flat, flat, V[bias], ALU.add).then_inc(*{"v": V_vec, "c": C_vec}[p].next(last))

                def link_c(q):
                    def link(ins, name):
                        ins.then_inc(*C_vec.next(name))
                        v.wait_ge(*C_vec.after(q, name))
                    return link

                def link_v(g):
                    def link(ins, name):
                        ins.then_inc(*V_vec.next(name))
                        v.wait_ge(*V_vec.after(g, name))
                    return link

                def conv_centre(t, u, i):
                    q = TILES * l + t
                    v.wait_ge(*CO_pe.after(PAIRS * l + i))
                    centre(bank(7, 256 * u, 256 * u + 256).rearrange("p (a b) -> p a b", a=GROUPS), st_c, c_c, c_sq, link_c(q), "c")

                def conv_scale(t, u, i):
                    q = TILES * l + t
                    v.wait_ge(*C_pool.after(q, "c_rstd"))
                    scaled(st_c, c_c, c_n, "cln_g", "cln_b", link_c(q), "c", "c_normed")

                def gate_centre(t, u, i):
                    g = TILES * l + t
                    v.wait_ge(*Z_vec.after(g, "glu"))
                    centre(sg_uv[:, 256:512].rearrange("p (a b) -> p a b", a=GROUPS), st_v, v_c, v_sq, link_v(g), "v")

                def gate_scale(t, u, i):
                    g = TILES * l + t
                    v.wait_ge(*Z_pool.after(g, "v_rstd"))
                    scaled(st_v, v_c, v_n, "sgu_g", "sgu_b", link_v(g), "v", "v_ready")

                def sgu_out(t, u, i):
                    g = TILES * l + t
                    v.wait_ge(*ZS_pe.after(g, "s"))
                    v.tensor_tensor(v_sq, bank(5, 0, 256).rearrange("p (a b) -> p a b", a=GROUPS),
                                    wide(s_bias[:, :], 2, GROUPS, HEAD), ALU.add).then_inc(*ZS_vec.next("s_biased"))
                    v.wait_ge(*ZS_vec.after(g, "s_biased"))
                    v.tensor_tensor(y[:, t, 0:SGU], v_sq.rearrange("p a b -> p (a b)"), sg_uv[:, 0:SGU],
                                    ALU.mult).then_inc(*ZS_vec.next("y_sgu"))

                def conv_silu(t, u, i):
                    v.wait_ge(*C_act.after(TILES * l + t, "c_tanh"))
                    v.scalar_tensor_tensor(c_y, c_th, 1.0, c_n.rearrange("p a b -> p (a b)"), ALU.add,
                                           ALU.mult).then_inc(*C_vec.next("c_silu"))

                def conv_out(t, u, i):
                    v.wait_ge(*CW_pe.after(TILES * l + t, "pw"))
                    v.scalar_tensor_tensor(y[:, t, SGU:2 * SGU], bank(6, 0, 256), 0.5, V["pw_b"], ALU.mult,
                                           ALU.add).then_inc(*CY_vec.next("y_conv"))

                mix = [(1, turn(0)), (-5, conv_out), (-4, conv_centre), (-2, conv), (-4, conv_scale), (-1, sgu_out),
                       (0, gelu_cubic), (2, norm(0)), (0, gelu_glu), (0, gate_centre), (-4, conv_silu), (0, gate_scale)]
                lag_loop(v, mix, after=False)

                def heads_view(b, lo, hi, width):
                    return ps[:, b:b + 2, 0:HC * width].rearrange("p a (h d) -> p a h d", h=HC)[:, :, :, lo:hi]

                def fold(ap):
                    return ap.rearrange("p (a h) d -> p a h d", a=2)

                def per_head(ap, d):
                    return ap.rearrange("p (a h) -> p a h", a=2).unsqueeze(3).to_broadcast([P, 2, HC, d])

                def c_norm(t, u, i):
                    g = TILES * l + t
                    v.wait_ge(*QC_pool.after(g))
                    v.scalar_tensor_tensor(cn[u][:, 0:QR], zc[:, t, 0:QR], r_c[:, 0:1], V["qa_g"], ALU.mult, ALU.mult)
                    v.scalar_tensor_tensor(cn[u][:, QR:QR + KVR], zc[:, t, QR:QR + KVR], r_c[:, 1:2], V["kva_g"], ALU.mult,
                                           ALU.mult).then_inc(*QC_vec.next("cn"))
                    v.scalar_tensor_tensor(zc[:, t, QR + KVR:MLA_IN], zc[:, t, QR + KVR:MLA_IN], r_c[:, 2:3], kg[:, HEAD:QK],
                                           ALU.mult, ALU.mult).then_inc(*QC_vec.next("kpe"))

                def q_sums(t, u, i):
                    g = TILES * l + t
                    v.wait_ge(*QM_act.after(g, "squared"))
                    v.wait_ge(*QM_pool.before(g))
                    v.tensor_reduce(m_qk[:, 0:8], qk_sq[:, :, 0:HEAD], AX.X, ALU.add)
                    v.tensor_reduce(m_qk[:, 8:16], qk_sq[:, :, HEAD:QK], AX.X, ALU.add)
                    v.tensor_reduce(m_qk[:, 16:24], k_sq, AX.X, ALU.add).then_inc(*QM_vec.next("sumsq"))

                def q_scale(t, u, i):
                    g = TILES * l + t

                    def link(ins, name):
                        ins.then_inc(*Q_vec.next(name))
                        v.wait_ge(*Q_vec.after(g, name))

                    def scaled(dst, src, r0, d):
                        return v.tensor_tensor(dst, src, wide(r_qk[:, u, r0:r0 + HEADS], 2, HEADS, d), ALU.mult)

                    v.wait_ge(*QM_pool.after(g))
                    v.wait_ge(*QM_raw.after(g))
                    scaled(qs[u][:, :, 0:HEAD], qs[u][:, :, 0:HEAD], 0, HEAD).then_inc(*Q_vec.next("q_nope"))
                    scaled(ks[u][:, :, 0:HEAD], ks[u][:, :, 0:HEAD], 16, HEAD).then_inc(*Q_vec.next("k_nope"))
                    scaled(pe_x, qs[u][:, :, HEAD:QK], 8, ROPE).then_inc(*Q_vec.next("q_pe"))
                    v.wait_ge(*Q_vec.after(g, "q_pe"))
                    v.tensor_tensor(qs[u][:, :, 0:HEAD], qs[u][:, :, 0:HEAD], wide(gq[:, 0:HEAD], 1, HEADS, HEAD),
                                    ALU.mult).then_inc(*Q_vec.next("q_gained"))
                    link(v.tensor_tensor(pe_x, pe_x, wide(gq[:, HEAD:QK], 1, HEADS, ROPE), ALU.mult), "pe_gained")
                    halves = pe_x.rearrange("p h (a r) -> p h a r", a=2)
                    k_halves = zc[:, t, QR + KVR:MLA_IN].rearrange("p (a r) -> p a r", a=2)
                    for tab, dst, name in ((cos, xc, "xc"), (sin, xs, "xs")):
                        v.tensor_tensor(dst[:, 0:HEADS], halves, tab[:, t, :].unsqueeze(1).unsqueeze(1).to_broadcast([P, HEADS, 2, HR]),
                                        ALU.mult)
                        v.tensor_tensor(dst[:, HEADS], k_halves, tab[:, t, :].unsqueeze(1).to_broadcast([P, 2, HR]),
                                        ALU.mult).then_inc(*Q_vec.next(name))
                    v.wait_ge(*Q_vec.after(g, "xs"))
                    for dst, src in ((qs[u], slice(0, HEADS)), (ks[u], None)):
                        def pick(x, half):
                            if src is None:
                                return x[:, HEADS:HEADS + 1, half, :].to_broadcast([P, HEADS, HR])
                            return x[:, 0:HEADS, half, :]
                        v.tensor_tensor(dst[:, :, HEAD:HEAD + HR], pick(xc, 0), pick(xs, 1), ALU.subtract)
                        ins = v.tensor_tensor(dst[:, :, HEAD + HR:QK], pick(xc, 1), pick(xs, 0), ALU.add)
                    ins.then_inc(*Q_vec.next("heads"))

                def q_turned(t, u, i):
                    g = TILES * l + t
                    v.wait_ge(qk_stored[u], 32 * (PAIRS * l + i) + 32)
                    v.wait_ge(*R_pe.after(g, "q_hi"))
                    v.tensor_copy(stage[u][0:QK, 0, HC:].rearrange("p a b -> p (a b)"), ps[0:QK, 7, :]).then_inc(*R_vec.next("q_hi"))
                    v.wait_ge(*R_pe.after(g, "k_hi"))
                    v.tensor_copy(stage[u][0:QK, 1, HC:].rearrange("p a b -> p (a b)"), ps[0:QK, 7, :]).then_inc(*R_vec.next("k_hi"))

                mla = [(2, c_norm), (-1, q_turned), (1, q_sums), (0, q_scale)]
                handover(mix, [c_norm], [], [q_sums], [q_scale], [q_turned])
                lag_loop(v, mla, before=False, start=1)

                def row_max(hh, j):
                    v.wait_ge(*S_pe.after(hh, f"s{j}"))
                    v.tensor_reduce(neg_max[:, j % 2:j % 2 + 1], banks(2 * (j % 2))[:, 0:(j + 1) * P], AX.X, ALU.max,
                                    negate=True).then_inc(*X_max.next(f"max{j}"))

                def prob_lo(hh, j):
                    w = min(j + 1, 4)
                    v.wait_ge(*T_pe.after(hh, f"lo{j}"))
                    v.tensor_copy(prob_t[j % 2][:, 0:w], bank(4, 0, w * P).rearrange("p (k q) -> p k q", q=P)
                                  ).then_inc(*X_lo.next(f"lo{j}"))

                def finish(hh, head, j):
                    v.wait_ge(*O_pe.after(hh, f"o{j}"))
                    v.reciprocal(rden[:, j % 2:j % 2 + 1], denom[:, j:j + 1]).then_inc(*X_fin.next(f"inv{j}"))
                    v.wait_ge(*X_fin.after(hh, f"inv{j}"))
                    v.tensor_scalar(y[:, j, bass.ds(head * HEAD + 2 * SGU, HEAD)], bank(6 + j % 2, 0, HEAD), rden[:, j % 2:j % 2 + 1],
                                    None, ALU.mult).then_inc(*X_fin.next(f"fin{j}"))

                row_max(HEADS * l, 0)
                with v.Fori(0, HEADS // 2) as i:
                    hh = HEADS * l + 2 * i
                    for n in range(2 * TILES):
                        if n + 1 < 2 * TILES:
                            row_max(hh + (n + 1) // TILES, (n + 1) % TILES)
                        else:
                            guarded(v, i < HEADS // 2 - 1, lambda: row_max(hh + 2, 0))
                        prob_lo(hh + n // TILES, n % TILES)
                        if n:
                            finish(hh + (n - 1) // TILES, 2 * i + (n - 1) // TILES, (n - 1) % TILES)
                    finish(hh + 1, 2 * i + 1, TILES - 1)

                v.wait_ge(late_loaded, N_LATE * l + N_LATE)
                settle(v, passed)

                def w_main(t, u, i):
                    g = TILES * l + t
                    for k, half in enumerate(("lo", "hi")):
                        v.wait_ge(*W_pe.after(g, half))
                        hv = h[:, t, 512 * k:512 * k + 512]
                        v.tensor_tensor(hv, hv, bank(2 + k), ALU.add).then_inc(*W_vec.next(half))

                def g_main(t, u, i):
                    v.wait_ge(*G_pe.after(TILES * l + t))
                    v.tensor_tensor(lg[:, t, :], bank(4 + u, 0, NG + NE), b_r[:, :], ALU.add).then_inc(*G_vec.next("logits"))

                lag_loop(v, [(-1, norm_m), (2, norm(1)), (1, turn(1)), (-1, turn_m), (0, w_main), (-1, g_main)])
                v.wait_ge(*G_vec.before(TILES * l + TILES))

                def link(ins, name):
                    ins.then_inc(*K_vec.next(name))
                    v.wait_ge(*K_vec.after(l, name))

                def sm(i):
                    return at(A, RS + 2560 + 8 * i, TILES)

                def bc(ap, n):
                    return ap.unsqueeze(2).to_broadcast([P, TILES, n])

                def row(n):
                    return iota[:, 0:n].unsqueeze(1).to_broadcast([P, TILES, n])

                gl_ = lg[:, :, 0:NG]
                el = lg[:, :, NG:NG + NE]
                link(v.tensor_reduce(sm(0), gl_, AX.X, ALU.max), "g_max")
                link(v.tensor_tensor(rs(0, TILES, NG), gl_, bc(sm(0), NG), ALU.subtract), "g_diff")
                v.wait_ge(*K_act.after(l, "g_exp"))
                link(v.tensor_reduce(sm(1), rs(1, TILES, NG), AX.X, ALU.add), "g_sum")
                link(v.reciprocal(sm(2), sm(1)), "g_w")
                link(v.tensor_scalar(rs(2, TILES, NG), rs(0, TILES, NG), 0.0, 64.0, ALU.is_lt, ALU.mult), "g_miss")
                link(v.tensor_tensor(rs(3, TILES, NG), rs(2, TILES, NG), row(NG), ALU.add), "g_cand")
                link(v.tensor_reduce(sm(3), rs(3, TILES, NG), AX.X, ALU.min), "g_first")
                link(v.tensor_tensor(rs(4, TILES, NG), row(NG), bc(sm(3), NG), ALU.is_equal), "g_hot")
                link(v.tensor_scalar(rs(5, TILES, NG), rs(4, TILES, NG), 1.0, BIG, ALU.subtract, ALU.mult), "g_far")
                link(v.tensor_tensor(rs(6, TILES, NG, EPG), el.rearrange("p t (g e) -> p t g e", g=NG),
                                     rs(5, TILES, NG).unsqueeze(3).to_broadcast([P, TILES, NG, EPG]), ALU.add), "e_in")

                def largest(src, top, where, hot, n):
                    link(v.tensor_reduce(top, src, AX.X, ALU.max), f"m{n}")
                    link(v.tensor_tensor(rs(7, TILES, NE), src, bc(top, NE), ALU.subtract), f"d{n}")
                    link(v.tensor_scalar(rs(8, TILES, NE), rs(7, TILES, NE), 0.0, 64.0, ALU.is_lt, ALU.mult), f"miss{n}")
                    link(v.tensor_tensor(rs(7, TILES, NE), rs(8, TILES, NE), row(NE), ALU.add), f"cand{n}")
                    link(v.tensor_reduce(where, rs(7, TILES, NE), AX.X, ALU.min), f"i{n}")
                    link(v.tensor_tensor(hot, row(NE), bc(where, NE), ALU.is_equal), f"hot{n}")

                hot1, hot2, rest = rs(2, TILES, NE), rs(4, TILES, NE), rs(3, TILES, NE)
                largest(rs(6, TILES, NE), sm(4), sm(5), hot1, 1)
                link(v.scalar_tensor_tensor(rest, hot1, -2 * BIG, rs(6, TILES, NE), ALU.mult, ALU.add), "rest")
                largest(rest, sm(6), sm(7), hot2, 2)
                link(v.tensor_tensor(picked_b, hot1, hot2, ALU.add), "picked")
                e2 = rs(9, 2, TILES)
                link(v.tensor_tensor(e2[:, 0], sm(6), sm(4), ALU.subtract), "e_diff")
                cnt = at(A, RS + 2816, 4).bitcast(I32)[0:NE]
                v.wait_ge(*K_pe.after(l, "ranks"))
                link(v.tensor_copy(cnt[:, 0:1], ps[0:NE, 6, 0:1]), "cnt_i")
                link(v.tensor_scalar(cnt[:, 1:2], cnt[:, 0:1], P - 1, None, ALU.add), "cnt_up")
                link(v.tensor_scalar(cnt[:, 2:3], cnt[:, 1:2], 7, None, ALU.logical_shift_right), "cnt_nb")
                nb_f = at(A, RS + 2824, 1)[0:NE]
                link(v.tensor_copy(nb_f, cnt[:, 2:3]), "nb_f")
                link(v.tensor_scalar(nb_col[0:NE, :], ones_b[0:NE, :], nb_f, None, ALU.mult), "nb_col")
                v.wait_ge(*K_pe.after(l, "starts"))
                ends = rs(5, 2, NE)
                link(v.tensor_copy(ends, bank(6, 64, 64 + 2 * NE).rearrange("p (a e) -> p a e", a=2)), "start_f")
                link(v.scalar_tensor_tensor(rs(6, TILES, NE), ends[:, 0].unsqueeze(1).to_broadcast([P, TILES, NE]), float(P),
                                            bank(7, 0, TILES * NE).rearrange("p (t e) -> p t e", t=TILES), ALU.mult, ALU.add), "row")
                dest_f, dest = at(A, RS + 2832, TILES, 2), at(A, RS + 2896, TILES, 2).bitcast(I32)
                for k, hot in enumerate((hot1, hot2)):
                    link(v.tensor_tensor(rs(7 + k, TILES, NE), hot, rs(6, TILES, NE), ALU.mult), f"r{k + 1}")
                    link(v.tensor_reduce(dest_f[:, :, k], rs(7 + k, TILES, NE), AX.X, ALU.add), f"dest{k + 1}")
                link(v.tensor_copy(dest, dest_f), "dest_i")
                blk_i = at(A, RS + 2848, TILES, 2).bitcast(I32)
                blk_f, slot_f = at(A, RS + 2864, TILES, 2), at(A, RS + 2880, TILES, 2)
                link(v.tensor_scalar(blk_i, dest, 7, None, ALU.logical_shift_right), "blk_i")
                link(v.tensor_copy(blk_f, blk_i), "blk_f")
                link(v.scalar_tensor_tensor(slot_f, blk_f, -float(P), dest_f, ALU.mult, ALU.add), "slot_f")
                for c in range(2 * TILES):
                    t, k = divmod(c, 2)
                    v.tensor_scalar(hot_s[:, c, :], iota[:, :], slot_f[:, t, k:k + 1], None, ALU.is_equal)
                    ins = v.tensor_scalar(hot_b[:, c, :], iota[:, 0:MAXB1], blk_f[:, t, k:k + 1], token[:, t, k:k + 1],
                                          ALU.is_equal, ALU.mult)
                ins.then_inc(*K_vec.next("hots"))
                le = at(C, 4096, MAXB1, NE)[0:1]
                owner = at(C, 4096 + 2048, MAXB1)[0:1]
                active = at(C, 4096 + 2112, MAXB1)[0:1]
                by_slot = at(C, 4096 + 2176, 3)[0:1]
                total = ends[0:1, 1, NE - 1:NE]
                link(v.tensor_tensor(le, ends[0:1, 1].unsqueeze(1).to_broadcast([1, MAXB1, NE]),
                                     iota[0:1, 0:MAXB1].unsqueeze(2).to_broadcast([1, MAXB1, NE]), ALU.is_le), "le")
                link(v.tensor_reduce(owner, le, AX.X, ALU.add), "owner")
                link(v.tensor_scalar(active, iota[0:1, 0:MAXB1], total, None, ALU.is_lt), "active")
                link(v.tensor_reduce(by_slot, active.rearrange("p (i u) -> p u i", u=3), AX.X, ALU.add), "by_slot")
                v.wait_ge(*K_act.after(l, "e_exp"))
                link(v.tensor_scalar(sm(8), e2[:, 1], 1.0, None, ALU.add), "e_den")
                link(v.reciprocal(sm(9), sm(8)), "e_rden")
                link(v.scalar_tensor_tensor(wts[:, 0], sm(2), 0.5, sm(9), ALU.mult, ALU.mult), "w1")
                link(v.tensor_tensor(wts[:, 1], wts[:, 0], e2[:, 1], ALU.mult), "w2")
                link(v.tensor_copy(cells[0:1, 48:52], run[:, :]), "before")
                link(v.tensor_tensor(run[:, 0:1], run[:, 0:1], total, ALU.add), "run_n")
                link(v.tensor_tensor(run[:, 1:4], run[:, 1:4], by_slot, ALU.add), "run_slots")
                v.wait_ge(*K_pe.after(l, "lists"))
                spare = rs(0, MAXB1)
                link(v.tensor_scalar(spare, bank(6, 128, 128 + MAXB1), 0.0, padding[:, :], ALU.is_equal, ALU.mult), "empty")
                link(v.scalar_tensor_tensor(out_idx[:, 0:MAXB1], bank(6, 128, 128 + MAXB1), -1.0, spare, ALU.add, ALU.add), "rows_i")
                v.tensor_scalar(idx[:, 0:MAXB1], out_idx[:, 0:MAXB1], SEQ - 1, None, ALU.bitwise_and).then_inc(*K_vec.next("list_i"))
                v.tensor_copy(cells[0:1, 0:MAXB1], owner).then_inc(*K_vec.next("owner_i"))
                v.tensor_copy(cells[0:1, 52:53], total).then_inc(*K_vec.next("cells"))

                prev, n, used = counters(v, l, passed)

                def x_hi(m):
                    v.wait_ge(*M_xT.after(m, "hi"))
                    v.tensor_copy(xT[:, 4:8].rearrange("p a b -> p (a b)"), bank(1)).then_inc(*M_xhi.next("x"))

                def hidden(m):
                    v.wait_ge(*M_tanh.after(m))
                    v.scalar_tensor_tensor(hid, hid_g, 1.0, bank(2, 0, F), ALU.add, ALU.mult).then_inc(*M_silu.next("silu"))
                    v.wait_ge(*M_silu.after(m))
                    v.tensor_tensor(hid, hid, bank(2, F, 2 * F), ALU.mult).then_inc(*M_prod.next("prod"))

                def y_hi(m):
                    v.wait_ge(y_stored, m * 16)
                    v.wait_ge(*M_dn.after(m, "hi"))
                    v.tensor_copy(y_blk[:, 512:1024], bank(5)).then_inc(*M_yhi.next("y"))

                x_hi(prev)
                hidden(prev)
                x_hi(prev + 1)

                def expert(b, here, nxt, last):
                    m = prev + b
                    guarded(v, b < n, lambda: hidden(m))
                    guarded(v, b + 1 < n, lambda: x_hi(m + 1))
                    guarded(v, b <= n, lambda: y_hi(m - 1))

                block_loop(v, n, expert)
                v.drain().then_inc(blocks_done, 1)

                v.wait_ge(ple_loaded, 48 * l + 48)
                settle(v, passed)

                def ple_front(t, u, i):
                    g = TILES * l + t
                    v.wait_ge(y_fetched[u], 32 * (PAIRS * l + i) + 32)
                    v.scalar_tensor_tensor(h[:, t, :], y_got[u][0], wts[:, 0, t:t + 1] if isinstance(t, int) else wts[:, 0, bass.ds(t, 1)],
                                           h[:, t, :], ALU.mult, ALU.add).then_inc(*E_comb.next("first"))
                    v.wait_ge(*E_comb.after(g, "first"))
                    v.scalar_tensor_tensor(h[:, t, :], y_got[u][1], wts[:, 1, t:t + 1] if isinstance(t, int) else wts[:, 1, bass.ds(t, 1)],
                                           h[:, t, :], ALU.mult, ALU.add).then_inc(*E_comb.next("second"))
                    norm(2)(t, u, i)

                def ple_main(t, u, i):
                    g = TILES * l + t
                    v.wait_ge(*E_pool.after(l))
                    v.wait_ge(e_fetched[u], 16 * (PAIRS * l + i) + 16)
                    v.wait_ge(h_final, g + TILES)
                    v.scalar_tensor_tensor(e_buf, e_got[u], span(m_e[:, 2, :], t, 1), gains[:, BRANCH], ALU.mult,
                                           ALU.mult).then_inc(*E_vec.next("e_scaled"))
                    v.wait_ge(*E_vec.after(g, "e_scaled"))
                    v.wait_ge(*E_act.after(g, "t_hi"))
                    v.scalar_tensor_tensor(e_buf, gate_t, 1.0, e_buf, ALU.add, ALU.mult).then_inc(*E_vec.next("gated"))
                    v.wait_ge(*E_vec.after(g, "gated"))
                    v.tensor_tensor(h[:, t, :], h[:, t, :], e_buf, ALU.add).then_inc(h_final, 1)

                lag_loop(v, [(2, ple_front), (1, turn(2)), (0, ple_main)])

        @block.tensor
        def _(pe):
            passed = sem("pe_passed")
            for s in (ZS_pe, ZG_pe, CO_pe, CY_pe, CW_pe, R_pe, G_pe, E_pe, FX.pe, FM.pe):
                pe.sem_inc(s.sem, s.per * s.credit)
            T = nc.tensor.transpose
            mm = nc.tensor.matmul
            pe.wait_ge(*S_pool0.after(0, "selects"))
            pe.wait_ge(*S_vec0.after(0, "pos"))
            T(bank(0, 0, TILES), at(B, T0 + 280, P)[0:TILES], ident[0:TILES, 0:TILES]).then_inc(*S_pe0.next("pos_t"))
            pe.wait_ge(*S_vec0.after(0, "cols"))

            with pe.Fori(0, DEPTH) as l:
                pe.wait_ge(*L_pool.after(l))
                pe.wait_ge(*E_act.before(TILES * l))
                pe.wait_ge(*E_vec.before(TILES * l))
                for k in range(GROUPS):
                    T(bank(7, P * k, P * k + P), ws_raw[:, k, :], ident[:, :])
                for c in range(2):
                    T(bank(6, 32 * c, 32 * c + 32), cw_raw[:, P * c:P * c + P], ident[0:32, 0:32])
                T(bank(6, 64, 64 + GROUPS), sb_raw[:, :], ident[0:GROUPS, 0:GROUPS]).then_inc(*L_pe.next("prep_T"))
                pe.wait_ge(*L_act.after(l))

                def turns(b, src, steps_):
                    for k in range(KD):
                        ins = T(bank(b + k // 4, P * (k % 4), P * (k % 4) + P), src[:, P * k:P * k + P], ident[:, :])
                        if k % 4 == 3:
                            ins.then_inc(*steps_.next(("T_lo", "T_hi")[k // 4]))

                def turn(ph):
                    def go(t, u, i):
                        r = 24 * l + t + 8 * ph
                        pe.wait_ge(*FX.lo.before(r))
                        pe.wait_ge(*FX.hi.before(r))
                        pe.wait_ge(*FX.a.after(r))
                        turns(0, a_buf[u], FX.pe)
                    return go

                def turn_m(t, u, i):
                    g = TILES * l + t
                    pe.wait_ge(*FM.lo.before(g))
                    pe.wait_ge(*FM.hi.before(g))
                    pe.wait_ge(*FM.a.after(g))
                    turns(6, m_buf[u], FM.pe)

                def turned(ph, t):
                    r = 24 * l + t + 8 * ph
                    pe.wait_ge(*FX.lo.after(r))
                    pe.wait_ge(*FX.hi.after(r))

                def product(dst, lhsT, w, a, b):
                    for k in range(KD):
                        ins = mm(dst, lhsT[:, k, :], w[:, k, a:b], start=(k == 0), stop=(k == KD - 1))
                    return ins


                def z_first(t, u, i):
                    g = TILES * l + t
                    turned(0, t)
                    pe.wait_ge(*Z_vec.after(g - 1, "sgu_gated"))
                    pe.wait_ge(w_in_loaded[0], 16 * l + 16)
                    product(bank(2), aT[u], w_in, 0, 512).then_inc(*Z_pe.next("z_sgu"))

                def z_second(t, u, i):
                    g = TILES * l + t
                    pe.wait_ge(*Z_vec.after(g - 1, "glu"))
                    pe.wait_ge(w_in_loaded[1], 16 * l + 16)
                    product(bank(3), aT[u], w_in, 512, 1024).then_inc(*Z_pe.next("z_glu"))
                    pe.wait_ge(*Z_act.before(g))
                    pe.wait_ge(w_in_loaded[2], 16 * l + 16)
                    product(bank(4, 0, MLA_IN), aT[u], w_in, 1024, IN).then_inc(*Z_pe.next("z_mla"))

                def upto(t, ahead):
                    return TILES * l + (min(t + ahead, TILES - 1) if isinstance(t, int) else t + ahead)

                def conv_back(t, u, i):
                    pe.wait_ge(*CT_vec.after(TILES * l + t + 1))
                    pe.wait_ge(*C_vec.before(TILES * l + t))
                    for j in range(2):
                        for c in range(2):
                            ins = T(bank(7, 256 * j + P * c, 256 * j + P * c + P), acc[c][:, P * j:P * j + P], ident[:, :])
                    ins.then_inc(*CO_pe.next("coT"))

                def mix_tokens(t, u, i):
                    g = TILES * l + t
                    pe.wait_ge(*V_vec.after(g, "v_ready"))
                    pe.wait_ge(*ZS_vec.before(g))
                    for k in range(GROUPS):
                        ins = mm(bank(5, HEAD * k, HEAD * k + HEAD), wsT[:, k, :], v_n[:, k, :], start=True, stop=True)
                    ins.then_inc(*ZS_pe.next("s"))

                def glu_turn(t, u, i):
                    g = TILES * l + t
                    pe.wait_ge(*Z_vec.after(g, "glu"))
                    pe.wait_ge(*ZC_act.before(g))
                    pe.wait_ge(*C_act.after(g - 4, "ybT_evac"))
                    pe.wait_ge(*CY_vec.after(g - 5))
                    for c in range(2):
                        ins = T(bank(6, P * c, P * c + P), gl[:, P * c:P * c + P], ident[:, :])
                    ins.then_inc(*ZG_pe.next("gluT"))

                def conv_turn(t, u, i):
                    pe.wait_ge(*C_vec.after(TILES * l + t, "c_silu"))
                    pe.wait_ge(*ZC_act.after(upto(t, 3)))
                    pe.wait_ge(*CY_vec.after(TILES * l + t - 1))
                    for c in range(2):
                        ins = T(bank(6, 256 + P * c, 256 + P * c + P), c_y[:, P * c:P * c + P], ident[:, :])
                    ins.then_inc(*CY_pe.next("ybT"))

                def pointwise(t, u, i):
                    q = TILES * l + t
                    pe.wait_ge(*C_act.after(q, "ybT_evac"))
                    pe.wait_ge(*ZC_act.after(upto(t, 4)))
                    for c in range(2):
                        ins = mm(bank(6, 0, 256), c_yT[:, c, :], pw[:, c, :], start=(c == 0), stop=(c == 1))
                    ins.then_inc(*CW_pe.next("pw"))

                mix = [(-1, glu_turn), (-4, conv_back, 0), (1, turn(0)), (-5, pointwise), (0, z_first), (-1, mix_tokens),
                       (0, z_second), (-4, conv_turn)]
                lag_loop(pe, mix, after=False)

                end = TILES * l + TILES

                def banks_free():
                    pe.wait_ge(mla_loaded, 32 * l + 32)
                    for s in (Z_vec, ZS_vec, V_vec, Z_act):
                        pe.wait_ge(*s.before(end))
                    for s in (FX.lo, FX.hi):
                        pe.wait_ge(*s.before(24 * l + TILES))
                    settle(pe, passed)

                def q_main(t, u, i):
                    g = TILES * l + t
                    pe.wait_ge(*QC_vec.after(g, "cn"))
                    for k in range(3):
                        ins = T(bank(1, P * k, P * k + P), cn[u][:, P * k:P * k + P], ident[:, :])
                    ins.then_inc(*QM_pe.next("cT"))
                    pe.wait_ge(*QT_act.after(g))
                    pe.wait_ge(*QM_raw.before(g))
                    for half in range(2):
                        w = HC * QK
                        for k in range(2):
                            ins = mm(bank(2 + half, 0, w), cnT[:, k, :], w_uq[:, k, w * half:w * half + w], start=(k == 0), stop=(k == 1))
                    ins.then_inc(*QM_pe.next("q_mm"))
                    for half in range(2):
                        ins = mm(bank(4 + half), cnT[:, 2, :], w_ukv[:, 512 * half:512 * half + 512], start=True, stop=True)
                    ins.then_inc(*QM_pe.next("kv_mm"))

                def q_turn(t, u, i):
                    g = TILES * l + t
                    pe.wait_ge(*R_act.before(g))
                    pe.wait_ge(*R_vec.before(g))
                    pe.wait_ge(*Q_vec.after(g, "heads"))
                    pe.wait_ge(*C_vec.before(end))
                    for name, b, src in (("q_lo", 0, qs[u][:, 0:HC]), ("q_hi", 7, qs[u][:, HC:]), ("k_lo", 0, ks[u][:, 0:HC]),
                                         ("k_hi", 7, ks[u][:, HC:])):
                        if name == "k_lo":
                            pe.wait_ge(*R_act.after(g, "q_lo"))
                        if name == "k_hi":
                            pe.wait_ge(*R_vec.after(g, "q_hi"))
                        for k in range(HC):
                            ins = T(ps[0:QK, b, P * k:P * k + P], src[:, k, :], ident[:, :])
                        ins.then_inc(*R_pe.next(name))

                mla = [(1, q_main), (-1, q_turn)]
                handover(mix, [], [q_main], [], [], [q_turn], banks_free)
                lag_loop(pe, mla, before=False, start=1)

                for s in (Q_vec, QM_raw, R_act, R_vec, CY_vec, C_act):
                    pe.wait_ge(*s.before(end))
                settle(pe, passed)

                def before(hh, j, back):
                    return (hh, j - back) if j >= back else (hh - 1, j - back + TILES)

                def scores(hh, u, j, i):
                    if j in (0, EARLY):
                        pe.wait_ge(qk_loaded[j == EARLY][u], 32 * (HEADS // 2 * l + i) + 32)
                    h2, j2 = before(hh, j, 2)
                    pe.wait_ge(*X_act.after(h2, f"exp{j2}"))
                    settle(pe, passed)
                    q = q_ring[u][0:QK, P * j:P * j + P]
                    b = 2 * (j % 2)
                    cols = (j + 1) * P
                    for c in range(0, cols, 512):
                        w = min(512, cols - c)
                        last = c + 512 >= cols
                        mm(bank(b + c // 512, 0, w), q, k_ring[u][0:QK, c:c + w], start=True, stop=not last, skip_group_check=True)
                    d = (j * P) % 512
                    mm(bank(b + j // 4, d, d + P), ident_b[:, :], mask_b[:, :], start=False, stop=True,
                       skip_group_check=True).then_inc(*S_pe.next(f"s{j}"))

                def transposed(hh, j):
                    h1, j1 = before(hh, j, 1)
                    pe.wait_ge(*X_lo.after(h1, f"lo{j1}"))
                    if j1 >= 4:
                        pe.wait_ge(*X_hi.after(h1, f"hi{j1}"))
                    pe.wait_ge(*X_act.after(hh, f"exp{j}"))
                    for k in range(j + 1):
                        ins = T(bank(4 + k // 4, P * (k % 4), P * (k % 4) + P), prob[j % 2][:, P * k:P * k + P], ident[:, :])
                        if k == min(j, 3):
                            ins.then_inc(*T_pe.next(f"lo{j}"))
                    if j >= 4:
                        ins.then_inc(*T_pe.next(f"hi{j}"))

                def outputs(hh, head, j):
                    pe.wait_ge(*X_lo.after(hh, f"lo{j}"))
                    if j >= 4:
                        pe.wait_ge(*X_hi.after(hh, f"hi{j}"))
                    h2, j2 = before(hh, j, 2)
                    pe.wait_ge(*X_fin.after(h2, f"fin{j2}"))
                    for k in range(j + 1):
                        ins = mm(bank(6 + j % 2, 0, HEAD), prob_t[j % 2][:, k, :], vals[:, k, head, :], start=(k == 0), stop=(k == j))
                    ins.then_inc(*O_pe.next(f"o{j}"))

                scores(HEADS * l, 0, 0, 0)
                with pe.Fori(0, HEADS // 2) as i:
                    hh = HEADS * l + 2 * i
                    for n in range(2 * TILES):
                        if n + 1 < 2 * TILES:
                            scores(hh + (n + 1) // TILES, (n + 1) // TILES, (n + 1) % TILES, i)
                        else:
                            guarded(pe, i < HEADS // 2 - 1, lambda: scores(hh + 2, 0, 0, i + 1))
                        transposed(hh + n // TILES, n % TILES)
                        if n:
                            outputs(hh + (n - 1) // TILES, 2 * i + (n - 1) // TILES, (n - 1) % TILES)
                    outputs(hh + 1, 2 * i + 1, TILES - 1)

                pe.wait_ge(*X_fin.before(HEADS * l + HEADS))
                pe.wait_ge(wo_loaded, 16 * l + 16)
                pe.wait_ge(late_loaded, N_LATE * l + N_LATE)
                settle(pe, passed)

                def w_half(k):
                    def go(t, u, i):
                        g = TILES * l + t
                        if k == 0:
                            turned(1, t)
                        pe.wait_ge(*W_vec.after(g - 1, ("lo", "hi")[k]))
                        product(bank(2 + k), aT[u], w_o, 512 * k, 512 * k + 512).then_inc(*W_pe.next(("lo", "hi")[k]))
                    return go

                def g_main(t, u, i):
                    g = TILES * l + t
                    pe.wait_ge(*FM.lo.after(g))
                    pe.wait_ge(*FM.hi.after(g))
                    pe.wait_ge(*G_vec.after(g - 2))
                    product(bank(4 + u, 0, NG + NE), mT, w_r, 0, NG + NE).then_inc(*G_pe.next("logits"))

                lag_loop(pe, [(1, turn(1)), (0, w_half(0)), (-1, turn_m), (0, w_half(1)), (-1, g_main)])

                pe.wait_ge(p_loaded, 16 * l + 16)
                pe.wait_ge(proj_loaded, 16 * l + 16)
                for s in (W_vec, G_vec, FM.lo, FM.hi):
                    pe.wait_ge(*s.before(end))
                for s in (FX.lo, FX.hi):
                    pe.wait_ge(*s.before(24 * l + 2 * TILES))
                settle(pe, passed)

                for k in range(PAIRS):
                    if k >= 2:
                        pe.wait_ge(*PT_act.after(l, f"pair{k - 2}"))
                    for u in range(2):
                        for c in range(2):
                            a = P * (2 * u + c)
                            ins = T(bank(k % 2, a, a + P), p_all[:, 2 * k + u, P * c:P * c + P], ident[:, :])
                    ins.then_inc(*PT_pe.next(f"pair{k}"))

                def project(i):
                    pe.wait_ge(*PT_act.after(l, f"pair{i}"))
                    for u in range(2):
                        pe.wait_ge(*P_act.after(TILES * l + (2 * i + u - 2), "copied"))
                        for half in range(2):
                            for k in range(2):
                                ins = mm(bank(2 + 2 * u + half), pT[:, i, u, k, :], ple_p[:, k, 512 * half:512 * half + 512],
                                         start=(k == 0), stop=(k == 1))
                        ins.then_inc(*P_pe.next("e"))

                project(0)

                pe.wait_ge(*K_vec.after(l, "picked"))
                settle(pe, passed)
                for t in range(TILES):
                    mm(ps[0:NE, 6, 0:1], picked_b[:, t, :], ones_b[:, 0:1], start=(t == 0), stop=(t == TILES - 1))
                for t in range(TILES):
                    for s in range(t + 1):
                        lhs = tri_b if s == t else ones_b
                        ins = mm(bank(7, NE * t, NE * t + NE), lhs[:, :], picked_b[:, s, :], start=(s == 0), stop=(s == t))
                ins.then_inc(*K_pe.next("ranks"))
                pe.wait_ge(*K_vec.after(l, "nb_col"))
                settle(pe, passed)
                mm(bank(6, 64, 64 + NE), nb_col[0:NE, :], tri_b[0:NE, 0:NE], start=True, stop=True)
                mm(bank(6, 64 + NE, 64 + 2 * NE), nb_col[0:NE, :], tri_b[0:NE, 0:NE], start=True, stop=False)
                mm(bank(6, 64 + NE, 64 + 2 * NE), nb_col[0:NE, :], ident_b[0:NE, 0:NE], start=False,
                   stop=True).then_inc(*K_pe.next("starts"))
                project(1)
                project(2)
                pe.wait_ge(*K_vec.after(l, "hots"))
                settle(pe, passed)
                for c in range(2 * TILES):
                    ins = mm(bank(6, 128, 128 + MAXB1), hot_s[:, c, :], hot_b[:, c, :], start=(c == 0), stop=(c == 2 * TILES - 1))
                ins.then_inc(*K_pe.next("lists"))

                project(3)
                pe.wait_ge(*P_act.before(end))
                pe.wait_ge(*PT_act.after(l))
                settle(pe, passed)

                prev, n, used = counters(pe, l, passed)

                def turn_x(m, s, use):
                    pe.wait_ge(x_gathered[s], (used[s] + use) * 16 + 16)
                    pe.wait_ge(*M_xlo.before(m))
                    pe.wait_ge(*M_xhi.before(m))
                    for k in range(KD):
                        ins = T(bank(k // 4, P * (k % 4), P * (k % 4) + P), x_blk[s][:, P * k:P * k + P], ident[:, :])
                        if k % 4 == 3:
                            ins.then_inc(*M_xT.next(("lo", "hi")[k // 4]))

                def gate_up(m, s, use):
                    pe.wait_ge(gu_loaded[s], (used[s] + use) * 32 + 32)
                    pe.wait_ge(*M_xlo.after(m))
                    pe.wait_ge(*M_xhi.after(m))
                    for k in range(KD):
                        ins = mm(bank(2), xT[:, k, :], w_gu[s][:, k, :], start=(k == 0), stop=(k == KD - 1))
                    ins.then_inc(*M_gu.next("gu"))

                def down(m, s, use):
                    pe.wait_ge(dn_loaded[s], (used[s] + use) * 16 + 16)
                    pe.wait_ge(*M_h.after(m))
                    pe.wait_ge(*M_ylo.before(m))
                    pe.wait_ge(*M_yhi.before(m))
                    for half in range(2):
                        for k in range(2):
                            ins = mm(bank(4 + half), hid_t[:, k, :], w_dn[s][:, k, 512 * half:512 * half + 512], start=(k == 0),
                                     stop=(k == 1))
                        ins.then_inc(*M_dn.next(("lo", "hi")[half]))

                def turn_h(m):
                    pe.wait_ge(*M_prod.after(m))
                    for k in range(2):
                        ins = T(bank(3, P * k, P * k + P), hid[:, P * k:P * k + P], ident[:, :])
                    ins.then_inc(*M_hT.next("hT"))

                turn_x(prev, 0, 0)
                gate_up(prev, 0, 0)
                turn_x(prev + 1, 1, 0)
                turn_h(prev)

                def expert(b, here, nxt, last):
                    m = prev + b
                    guarded(pe, b < n, lambda: gate_up(m, *here))
                    guarded(pe, b + 1 < n, lambda: turn_x(m + 1, *nxt))
                    guarded(pe, b <= n, lambda: down(m - 1, *last))
                    guarded(pe, b < n, lambda: turn_h(m))

                block_loop(pe, n, expert)

                pe.wait_ge(ple_loaded, 48 * l + 48)
                settle(pe, passed)

                def ple_main(t, u, i):
                    g = TILES * l + t
                    turned(2, t)
                    for k, half in enumerate(("g_lo", "g_hi")):
                        pe.wait_ge(*E_act.after(g - 1, ("t_lo", "t_hi")[k]))
                        product(bank(2 + k), aT[u], ple_g, 512 * k, 512 * k + 512).then_inc(*E_pe.next(half))

                lag_loop(pe, [(1, turn(2)), (0, ple_main)])


_INS = ["x", "p", "positions", "mix_norm_g", "w_in", "sgu_ln_g", "sgu_ln_b", "sgu_w", "sgu_b", "conv_w", "conv_b",
        "conv_ln_g", "conv_ln_b", "conv_pw_w", "conv_pw_b", "q_a_norm_g", "w_uq", "kv_a_norm_g", "w_ukv", "q_norm_g",
        "k_norm_g", "branch_norm_g", "w_o", "ffn_norm_g", "router_group_w", "router_group_b", "router_expert_w",
        "router_expert_b", "moe_w_gate", "moe_w_up", "moe_w_down", "ple_norm_g", "ple_gate_w", "ple_proj_w",
        "ple_post_norm_g"]


def kernel(**inputs):
    import numpy as _np
    import concourse.bacc as _bacc
    from concourse import mybir as _mybir
    from concourse.bass_utils import run_bass_kernel_spmd as _run

    nc = _bacc.Bacc("TRN2", target_bir_lowering=False, num_devices=1)
    arrays, args = {}, {}
    for name in _INS:
        a = _np.ascontiguousarray(inputs[name])
        arrays[f"in_{name}_dram"] = a
        args[name] = nc.dram_tensor(f"in_{name}_dram", a.shape, _mybir.dt.from_np(a.dtype), kind="ExternalInput").ap()
    out = nc.dram_tensor("out_0_dram", inputs["x"].shape, _mybir.dt.from_np(_np.dtype("float32")), kind="ExternalOutput").ap()
    build(nc, args, out)
    r = _run(nc, [arrays], core_ids=[0])
    return r.results[0]["out_0_dram"]
```
